# Optimizing a Trainium2 kernel written in Bass

```python
import math
import jax, jax.numpy as jnp
from jax import lax
import numpy as np

D_MODEL = 1024
BATCH = 1
SEQ = 512
DEPTH = 2
DEC_BATCH = 1
DEC_SEQ = 32
PAST_LEN = 512

CHUNK = 64
N_RET_HEADS = 4
RET_DK = 128
RET_DV = 256
RET_ROPE_THETA = 10000.0
N_DIFF_HEADS = 8
DIFF_HD = 64
DIFF_ROT = DIFF_HD // 4
ROPE_THETA = 500000.0
Q_BLOCK = 128
D_FF = 2816
CONV_W = 3
EPS = 1e-6

RET_QK = N_RET_HEADS * RET_DK
RET_V = N_RET_HEADS * RET_DV
DIFF_W = N_DIFF_HEADS * 2 * DIFF_HD
SPLITS = (RET_QK, RET_QK, RET_V, RET_V, DIFF_W, DIFF_W, DIFF_W, D_MODEL, D_MODEL)
IN_W = sum(SPLITS)

kernel_name = 'hybrid_retention_diffattn_streaming_step'

def rmsnorm(x, g):
    xf = x.astype(jnp.float32)
    y = xf * lax.rsqrt(jnp.mean(xf * xf, axis=-1, keepdims=True) + EPS)
    return (y * g.astype(jnp.float32)).astype(x.dtype)

def rope(x, pos, rot_dim, theta):
    half = rot_dim // 2
    inv = theta ** (-jnp.arange(half, dtype=jnp.float32) / half)
    ang = pos.astype(jnp.float32)[:, None] * inv[None, :]
    shape = (ang.shape[0],) + (1,) * (x.ndim - 3) + (half,)
    cos = jnp.cos(ang).reshape(shape).astype(x.dtype)
    sin = jnp.sin(ang).reshape(shape).astype(x.dtype)
    xr, xp = x[..., :rot_dim], x[..., rot_dim:]
    x1, x2 = xr[..., :half], xr[..., half:]
    return jnp.concatenate([x1 * cos - x2 * sin, x2 * cos + x1 * sin, xp], axis=-1)

def ret_log_decay():
    return jnp.log1p(-jnp.exp2(-5.0 - jnp.arange(N_RET_HEADS, dtype=jnp.float32)))

def retention_chunk(S, q, k, v):
    L = q.shape[1]
    log_g = ret_log_decay()
    idx = jnp.arange(L, dtype=jnp.float32)
    rel = idx[:, None] - idx[None, :]
    decay = jnp.where(rel >= 0, jnp.exp(log_g[:, None, None] * jnp.maximum(rel, 0.0)), 0.0)
    xi = jnp.exp(log_g[None, :] * (idx[:, None] + 1.0))
    zeta = jnp.exp(log_g[None, :] * (L - 1.0 - idx[:, None]))
    g_len = jnp.exp(log_g * L)
    scores = jnp.einsum('bihd,bjhd->bhij', q, k) * decay.astype(q.dtype)
    o = (jnp.einsum('bhij,bjhe->bihe', scores, v)
         + jnp.einsum('bihd,bhde->bihe', q, S) * xi[None, :, :, None].astype(q.dtype))
    S_new = (S * g_len[None, :, None, None].astype(S.dtype)
             + jnp.einsum('bjhd,bjhe->bhde', k * zeta[None, :, :, None].astype(k.dtype), v))
    return o, S_new.astype(S.dtype)

def retention_prompt(q, k, v):
    B, T = q.shape[:2]
    nc = T // CHUNK
    qc = jnp.moveaxis(q.reshape(B, nc, CHUNK, N_RET_HEADS, RET_DK), 1, 0)
    kc = jnp.moveaxis(k.reshape(B, nc, CHUNK, N_RET_HEADS, RET_DK), 1, 0)
    vc = jnp.moveaxis(v.reshape(B, nc, CHUNK, N_RET_HEADS, RET_DV), 1, 0)
    S0 = jnp.zeros((B, N_RET_HEADS, RET_DK, RET_DV), v.dtype)

    def step(S, xs):
        o, S = retention_chunk(S, xs[0], xs[1], xs[2])
        return S, o

    S_fin, o = lax.scan(step, S0, (qc, kc, vc))
    return jnp.moveaxis(o, 0, 1).reshape(B, T, N_RET_HEADS, RET_DV), S_fin

def diff_attn_block(q, qpos, k, v, kpos, lam):
    s = jnp.einsum('bqhcd,bkhcd->bhcqk', q, k).astype(jnp.float32) * (DIFF_HD ** -0.5)
    visible = (kpos // CHUNK)[None, :] <= (qpos // CHUNK)[:, None]
    s = jnp.where(visible, s, -jnp.inf)
    p = jax.nn.softmax(s, axis=-1)
    a = p[:, :, 0] - lam * p[:, :, 1]
    return jnp.einsum('bhqk,bkhe->bqhe', a.astype(v.dtype), v)

def diff_lambda(p, lam_init):
    f32 = jnp.float32
    return (jnp.exp(jnp.sum(p['lambda_q1'].astype(f32) * p['lambda_k1'].astype(f32)))
            - jnp.exp(jnp.sum(p['lambda_q2'].astype(f32) * p['lambda_k2'].astype(f32))) + lam_init)

def mixer_inputs(h, pos, p):
    B, L = h.shape[:2]
    points = [int(c) for c in np.cumsum(SPLITS)[:-1]]
    q_r, k_r, v_r, g_r, q_d, k_d, v_d, ga, gb = jnp.split(h @ p['w_in'], points, axis=-1)
    q_r = rope(q_r.reshape(B, L, N_RET_HEADS, RET_DK), pos, RET_DK, RET_ROPE_THETA)
    k_r = rope(k_r.reshape(B, L, N_RET_HEADS, RET_DK), pos, RET_DK, RET_ROPE_THETA) * (RET_DK ** -0.5)
    v_r = v_r.reshape(B, L, N_RET_HEADS, RET_DV)
    q_d = rope(rmsnorm(q_d.reshape(B, L, N_DIFF_HEADS, 2, DIFF_HD), p['q_norm_g']), pos, DIFF_ROT, ROPE_THETA)
    k_d = rope(rmsnorm(k_d.reshape(B, L, N_DIFF_HEADS, 2, DIFF_HD), p['k_norm_g']), pos, DIFF_ROT, ROPE_THETA)
    v_d = v_d.reshape(B, L, N_DIFF_HEADS, 2 * DIFF_HD)
    return (q_r, k_r, v_r, g_r), (q_d, k_d, v_d), (ga, gb)

def mixer_output(o_r, g_r, o_d, ga, gb, p, lam_init):
    B, L = o_r.shape[:2]
    ret = rmsnorm(o_r, p['ret_norm_g']).reshape(B, L, RET_V) * jax.nn.silu(g_r)
    dif = (rmsnorm(o_d, p['diff_norm_g']) * (1.0 - lam_init)).reshape(B, L, DIFF_W)
    y = jax.nn.sigmoid(ga) * (ret @ p['w_branch_a']) + jax.nn.sigmoid(gb) * (dif @ p['w_branch_b'])
    return y @ p['w_out']

def conv_glu(h, prev, p):
    u = h @ p['w_up']
    L = u.shape[1]
    pad = jnp.concatenate([prev, u], axis=1)
    c = p['conv_b'] + p['conv_w'][0] * pad[:, 0:L]
    for j in range(1, CONV_W):
        c = c + p['conv_w'][j] * pad[:, j:j + L]
    a, g = jnp.split(c, 2, axis=-1)
    return (jax.nn.silu(g) * a) @ p['w_down'], pad[:, -(CONV_W - 1):]

def layer_prompt(x, pos, p, lam_init):
    B, T = x.shape[:2]
    h = rmsnorm(x, p['norm1_g'])
    (q_r, k_r, v_r, g_r), (q_d, k_d, v_d), (ga, gb) = mixer_inputs(h, pos, p)
    o_r, S = retention_prompt(q_r, k_r, v_r)
    lam = diff_lambda(p, lam_init)
    nb = T // Q_BLOCK
    qb = jnp.moveaxis(q_d.reshape(B, nb, Q_BLOCK, N_DIFF_HEADS, 2, DIFF_HD), 1, 0)
    pb = pos.reshape(nb, Q_BLOCK)
    o_d = lax.map(lambda a: diff_attn_block(a[0], a[1], k_d, v_d, pos, lam), (qb, pb))
    o_d = jnp.moveaxis(o_d, 0, 1).reshape(B, T, N_DIFF_HEADS, 2 * DIFF_HD)
    x = x + mixer_output(o_r, g_r, o_d, ga, gb, p, lam_init)
    f, conv_state = conv_glu(rmsnorm(x, p['norm2_g']), jnp.zeros((B, CONV_W - 1, 2 * D_FF), x.dtype), p)
    return x + f, (k_d.reshape(B, T, N_DIFF_HEADS, 2 * DIFF_HD), v_d, S, conv_state)

def layer_sample(x, pos, ck, cv, s_ret, s_conv, p, lam_init):
    B, L = x.shape[:2]
    past = ck.shape[1]
    h = rmsnorm(x, p['norm1_g'])
    (q_r, k_r, v_r, g_r), (q_d, k_d, v_d), (ga, gb) = mixer_inputs(h, pos, p)
    o_r, S = retention_chunk(s_ret, q_r, k_r, v_r)
    lam = diff_lambda(p, lam_init)
    k_all = jnp.concatenate([ck.reshape(B, past, N_DIFF_HEADS, 2, DIFF_HD), k_d], axis=1)
    v_all = jnp.concatenate([cv, v_d], axis=1)
    kpos = jnp.arange(past + L, dtype=jnp.int32)
    o_d = diff_attn_block(q_d, pos, k_all, v_all, kpos, lam)
    x = x + mixer_output(o_r, g_r, o_d, ga, gb, p, lam_init)
    f, conv_state = conv_glu(rmsnorm(x, p['norm2_g']), s_conv, p)
    return x + f, (k_d.reshape(B, L, N_DIFF_HEADS, 2 * DIFF_HD), v_d, S, conv_state)

def setup_inputs(seed: int = 0) -> dict:
    key = jax.random.key(seed)
    ks = jax.random.split(key, 24)

    def nrm(k, shape, scale):
        return jax.random.normal(k, shape, jnp.float32) * scale

    return {
        'x_prompt': nrm(ks[0], (BATCH, SEQ, D_MODEL), 1.0),
        'x_sample': nrm(ks[1], (DEC_BATCH, DEC_SEQ, D_MODEL), 1.0),
        'cache_k': nrm(ks[2], (DEPTH, DEC_BATCH, PAST_LEN, N_DIFF_HEADS, 2 * DIFF_HD), 1.0),
        'cache_v': nrm(ks[3], (DEPTH, DEC_BATCH, PAST_LEN, N_DIFF_HEADS, 2 * DIFF_HD), 1.0),
        'state_ret': nrm(ks[4], (DEPTH, DEC_BATCH, N_RET_HEADS, RET_DK, RET_DV), 0.5),
        'state_conv': nrm(ks[5], (DEPTH, DEC_BATCH, CONV_W - 1, 2 * D_FF), 1.0),
        'norm1_g': 1.0 + nrm(ks[6], (DEPTH, D_MODEL), 0.05),
        'w_in': nrm(ks[7], (DEPTH, D_MODEL, IN_W), D_MODEL ** -0.5),
        'ret_norm_g': 1.0 + nrm(ks[8], (DEPTH, RET_DV), 0.05),
        'q_norm_g': 1.0 + nrm(ks[9], (DEPTH, DIFF_HD), 0.05),
        'k_norm_g': 1.0 + nrm(ks[10], (DEPTH, DIFF_HD), 0.05),
        'lambda_q1': nrm(ks[11], (DEPTH, DIFF_HD), 0.1),
        'lambda_k1': nrm(ks[12], (DEPTH, DIFF_HD), 0.1),
        'lambda_q2': nrm(ks[13], (DEPTH, DIFF_HD), 0.1),
        'lambda_k2': nrm(ks[14], (DEPTH, DIFF_HD), 0.1),
        'diff_norm_g': 1.0 + nrm(ks[15], (DEPTH, 2 * DIFF_HD), 0.05),
        'w_branch_a': nrm(ks[16], (DEPTH, RET_V, D_MODEL), RET_V ** -0.5),
        'w_branch_b': nrm(ks[17], (DEPTH, DIFF_W, D_MODEL), DIFF_W ** -0.5),
        'w_out': nrm(ks[18], (DEPTH, D_MODEL, D_MODEL), D_MODEL ** -0.5),
        'norm2_g': 1.0 + nrm(ks[19], (DEPTH, D_MODEL), 0.05),
        'w_up': nrm(ks[20], (DEPTH, D_MODEL, 2 * D_FF), D_MODEL ** -0.5),
        'conv_w': nrm(ks[21], (DEPTH, CONV_W, 2 * D_FF), CONV_W ** -0.5),
        'conv_b': nrm(ks[22], (DEPTH, 2 * D_FF), 0.02),
        'w_down': nrm(ks[23], (DEPTH, D_FF, D_MODEL), D_FF ** -0.5),
    }

def reference(x_prompt, x_sample, cache_k, cache_v, state_ret, state_conv, norm1_g, w_in, ret_norm_g,
              q_norm_g, k_norm_g, lambda_q1, lambda_k1, lambda_q2, lambda_k2, diff_norm_g, w_branch_a,
              w_branch_b, w_out, norm2_g, w_up, conv_w, conv_b, w_down):
    past = cache_k.shape[2]
    pos_p = jnp.arange(x_prompt.shape[1], dtype=jnp.int32)
    pos_s = past + jnp.arange(x_sample.shape[1], dtype=jnp.int32)
    yp, ys = x_prompt, x_sample
    kp_l, vp_l, sp_l, cp_l = [], [], [], []
    ks_l, vs_l, ss_l, cs_l = [], [], [], []
    for l in range(DEPTH):
        p = {
            'norm1_g': norm1_g[l], 'w_in': w_in[l], 'ret_norm_g': ret_norm_g[l],
            'q_norm_g': q_norm_g[l], 'k_norm_g': k_norm_g[l],
            'lambda_q1': lambda_q1[l], 'lambda_k1': lambda_k1[l],
            'lambda_q2': lambda_q2[l], 'lambda_k2': lambda_k2[l],
            'diff_norm_g': diff_norm_g[l], 'w_branch_a': w_branch_a[l], 'w_branch_b': w_branch_b[l],
            'w_out': w_out[l], 'norm2_g': norm2_g[l], 'w_up': w_up[l], 'conv_w': conv_w[l],
            'conv_b': conv_b[l], 'w_down': w_down[l],
        }
        lam_init = 0.8 - 0.6 * math.exp(-0.3 * l)
        yp, (kp, vp, sp, cp) = layer_prompt(yp, pos_p, p, lam_init)
        ys, (kn, vn, sn, cn) = layer_sample(ys, pos_s, cache_k[l], cache_v[l], state_ret[l], state_conv[l], p, lam_init)
        kp_l.append(kp); vp_l.append(vp); sp_l.append(sp); cp_l.append(cp)
        ks_l.append(kn); vs_l.append(vn); ss_l.append(sn); cs_l.append(cn)
    return (yp, ys, jnp.stack(kp_l), jnp.stack(vp_l), jnp.stack(sp_l), jnp.stack(cp_l),
            jnp.stack(ks_l), jnp.stack(vs_l), jnp.stack(ss_l), jnp.stack(cs_l))


_drawn_inputs = setup_inputs


def setup_inputs(seed=0):
    import zlib

    import numpy as np

    out = dict(_drawn_inputs(seed))
    spreads = {}
    factors = {'conv_b': 2.787}
    for name, (base, spread) in spreads.items():
        noise = np.random.default_rng([zlib.crc32(name.encode()), seed]).standard_normal(out[name].shape)
        drawn = base * np.exp(spread * noise) if base else spread * noise
        out[name] = __import__('jax').numpy.asarray(drawn.astype(out[name].dtype))
    for name, factor in factors.items():
        out[name] = (out[name] * factor).astype(out[name].dtype)
    return out
```

```python
from contextlib import ExitStack, contextmanager

import numpy as np

import concourse.bass as bass
from concourse import mybir

F32 = mybir.dt.float32
F32R = mybir.dt.float32r
ALU = mybir.AluOpType
ACT = mybir.ActivationFunctionType
AX = mybir.AxisListType.X
ds = bass.ds

P = 128
DEPTH = 2
D_MODEL = 1024
SEQ = 512
DEC = 32
PAST = 512
TOK = SEQ + DEC
HALF = TOK // 2
NT = SEQ // P
TILES = NT + 1
ROWS = [P] * NT + [DEC]
RET_HEADS, RET_DK, RET_DV = 4, 128, 256
DIFF_HEADS, DIFF_HD, DIFF_ROT = 8, 64, 16
HW = 2 * DIFF_HD
CHUNK = 64
D_FF = 2816
EPS = 1e-6
KC = D_MODEL // P
UC = 256
UNIT = KC * UC
IN_W = 8192
COL = dict(qr=0, kr=512, vr=1024, gr=2048, qd=3072, kd=4096, vd=5120, ga=6144, gb=7168)
FT = D_FF // P
FB = FT // 2
DOWN = [[4, 4, 3], [3, 3, 3, 2]]
GP = TOK + 2
NEG = -1.0e30
NVEC = 19

ORDER = [("N", 1), ("D", 4), ("R", 2), ("M", 1), ("F", 2)]


def shape_tables():
    f = np.float32
    pos = np.zeros((P, TILES), f)
    for m in range(NT):
        pos[:, m] = m * P + np.arange(P)
    pos[:DEC, NT] = PAST + np.arange(DEC)

    def rope(half, theta):
        inv = (f(theta) ** (-np.arange(half, dtype=f) / f(half))).astype(f)
        ang = (pos[:, :, None] * inv).astype(f)
        return np.cos(ang).astype(f), np.sin(ang).astype(f)

    rc, rs = rope(RET_DK // 2, 10000.0)
    dc, dsn = rope(DIFF_ROT // 2, 500000.0)
    log_g = np.log1p(-np.exp2(-5.0 - np.arange(RET_HEADS, dtype=f))).astype(f)
    ks = f(RET_DK ** -0.5)
    rel = np.arange(SEQ, dtype=f)[None, :] - np.arange(P, dtype=f)[:, None]
    decay = np.where(rel[:, None, :] >= 0, np.exp(log_g[None, :, None] * np.maximum(rel, 0)[:, None, :]), 0) * ks
    zeta = np.zeros((P, TILES, RET_HEADS), f)
    for m in range(NT):
        zeta[:, m] = np.exp(log_g * (SEQ - 1.0 - pos[:, m:m + 1])) * ks
    zeta[:DEC, NT] = np.exp(log_g * (DEC - 1.0 - np.arange(DEC, dtype=f)[:, None])) * ks
    xi = np.exp(log_g[:, None] * (np.arange(DEC, dtype=f) + 1.0))
    lam = [0.8 - 0.6 * np.exp(-0.3 * l) for l in range(DEPTH)]
    small = np.concatenate([
        np.eye(P, dtype=f), rc.reshape(P, -1), rs.reshape(P, -1), dc.reshape(P, -1), dsn.reshape(P, -1),
        zeta.reshape(P, -1), np.broadcast_to(xi.reshape(1, -1), (P, RET_HEADS * DEC)),
        np.broadcast_to(np.exp(log_g * f(DEC))[None], (P, RET_HEADS)),
        np.broadcast_to(np.array([[lam[0], lam[1], 1 - lam[0], 1 - lam[1]]]), (P, 4))], axis=1)
    return small.astype(f), np.ascontiguousarray(decay.astype(f).reshape(P, RET_HEADS * SEQ))


class Counts:

    def __init__(self):
        self.per = {}
        self.keys = {}

    def start(self, phase):
        out = {}
        for name, times in ORDER:
            if name == phase:
                break
            for s, n in self.per.get(name, {}).items():
                out[s] = out.get(s, 0) + n * times
        return out

    def layer(self, sem):
        return sum(self.per.get(name, {}).get(sem, 0) * times for name, times in ORDER)


class Stream:

    def __init__(self, eng, name, known, seen, handles):
        self.e, self.known, self.seen, self.handles = eng, known, seen, handles
        self.step = name + "_step"
        self.layer = self.index = None
        self.phase = "P"
        self.here, self.waited, self.pending = {}, {}, set()
        self.last = None

    @contextmanager
    def layers(self):
        self.leave()
        with self.e.Fori(0, DEPTH) as l:
            self.layer = l
            yield l
        self.layer, self.phase, self.index, self.here, self.waited = None, "end", None, {}, {}

    @contextmanager
    def body(self, phase):
        times = dict(ORDER)[phase]
        self.phase, self.here, self.last, self.waited = phase, {}, None, {}
        if times == 1:
            self.index = None
            yield 0
            self.leave()
        else:
            with self.e.Fori(0, times) as i:
                self.index = i
                yield i
                self.leave()

    def leave(self):
        if self.last and self.waited.get(self.last[0], self.last[1] - 1) < self.last[1]:
            self.e.wait_ge(*self.own())
        self.settle()
        self.last = None
        per = self.seen.per.setdefault(self.phase, {})
        for s, n in self.here.items():
            per[s] = per.get(s, 0) + n

    def at(self, sem, key=None, k=None):
        if k is None:
            k = self.known.keys[(self.phase, sem, key)] if self.known else 1
        k = max(k, self.waited.get(sem, k))
        if sem in self.pending and k > self.waited[sem]:
            self.settle()
        self.waited[sem] = k
        self.pending.add(sem)
        if self.known is None:
            return self.handles(sem), 1
        c = self.known
        if self.phase == "P":
            return self.handles(sem), k
        value = c.per.get("P", {}).get(sem, 0) + k
        if self.phase == "end":
            return self.handles(sem), value + DEPTH * c.layer(sem)
        value += c.start(self.phase).get(sem, 0)
        if c.layer(sem):
            value = self.layer * c.layer(sem) + value
        each = c.per.get(self.phase, {}).get(sem, 0)
        if self.index is not None and each:
            value = self.index * each + value
        return self.handles(sem), value

    def own(self):
        sem, k = self.last or (self.step, self.here.get(self.step, 0))
        return self.at(sem, k=k)

    def up(self, sem, key=None, n=1):
        self.pending.clear()
        self.here[sem] = self.here.get(sem, 0) + n
        if key is not None:
            assert (self.phase, sem, key) not in self.seen.keys, (self.phase, sem, key)
            self.seen.keys[(self.phase, sem, key)] = self.here[sem]
        if n == 1:
            self.last = (sem, self.here[sem])
        return self.handles(sem), n

    def note(self, sem, key):
        self.seen.keys[(self.phase, sem, key)] = self.here[sem]

    def settle(self):
        self.e.sem_inc(self.handles("settled"), 1)
        self.pending.clear()

    def prime(self, sem, n):
        self.e.sem_inc(self.handles(sem), n)
        self.here[sem] = self.here.get(sem, 0) + n


def program(nc, A, known):
    seen = Counts()
    handles = {}
    ctx = ExitStack()
    with ctx:
        def sem(name):
            if name not in handles:
                handles[name] = ctx.enter_context(nc.semaphore(name))
            return handles[name]

        def sb(name, shape, dt=F32, stack=ctx):
            return stack.enter_context(nc.sbuf_tensor(name, shape, dt))

        x = sb("x", [P, TILES, D_MODEL])
        hl1 = sb("hl1", [P, KC, 2, TOK], F32R)
        xs = sb("xs", [P, KC, 2, DEC], F32R)
        whi = sb("whi", [P, 2, UNIT], F32R)
        wlo = sb("wlo", [P, 2, UNIT], F32R)
        raw = sb("raw", [P, 2, UNIT])
        nsmall = P + 2 * TILES * 64 + 2 * TILES * 8 + TILES * 4 + 4 * DEC + 4 + 4
        small = sb("small", [P, nsmall])
        at = 0

        def take(n):
            nonlocal at
            at += n
            return small[:, at - n:at]

        ident = take(P)
        rcos = take(TILES * 64).rearrange("p (m d) -> p m d", m=TILES)
        rsin = take(TILES * 64).rearrange("p (m d) -> p m d", m=TILES)
        dcos = take(TILES * 8).rearrange("p (m d) -> p m d", m=TILES)
        dsin = take(TILES * 8).rearrange("p (m d) -> p m d", m=TILES)
        zeta = take(TILES * 4).rearrange("p (m h) -> p m h", m=TILES)
        xi = take(4 * DEC).rearrange("p (h i) -> p h i", h=4)
        g32 = take(4)
        lamc = take(4)
        vecs = sb("vecs", [P, DEPTH, NVEC])
        conv = sb("conv", [P, DEPTH, 6, 2 * FT])
        qkg = sb("qkg", [P, DEPTH, 2, DIFF_HD])
        lam = sb("lam", [P, DEPTH])
        sgn = sb("sgn", [2 * DEC, DEPTH])
        gd = sb("gd", [P, DEPTH])
        mhalf = sb("mhalf", [P, 40])
        ss = sb("ss", [P, 40])
        ms = sb("ms", [P, 40])
        rstd = sb("rstd", [P, 40])
        ssr = sb("ssr", [P, TILES, RET_HEADS])
        rest = sb("rest", [DEC, 512])
        odif = sb("odif", [P, TILES, D_MODEL])
        sTs_x = sb("sTs", [DEC, DEC])
        qx = sb("qx", [P, DEC])

        mix = ExitStack()
        mer = sb("mer", [P, KC, TOK], F32, mix)
        with ExitStack() as s:
            qz = sb("qz", [P, 2, 2 * TOK], F32, s)
            kdT = sb("kdT", [P, 2, TOK], F32, s)
            vd = sb("vd", [P, TILES, UC], F32, s)
            rawq = sb("rawq", [P, TILES, UC], F32, s)
            rawk = sb("rawk", [P, TILES, UC], F32, s)
            prob = sb("prob", [P, 2, 1024], F32, s)
            aT = sb("aT", [P, 2, SEQ], F32, s)
            rt = sb("rt", [P, 2, TILES * 4 * 8], F32, s)
            kc_n = sb("kc_n", [P, NT, HW], F32, s)
            vc_n = sb("vc_n", [P, NT, HW], F32, s)
            kcT = sb("kcT", [P, SEQ], F32, s)
            aTs = sb("aTs", [P, TILES, DEC], F32, s)
            aTt = sb("aTt", [P, TILES, DEC], F32, s)
            nmax = sb("nmax", [P, 2, 2], F32, s)
            sums = sb("sums", [P, 2, 2], F32, s)
            rinv = sb("rinv", [P, 2, 3], F32, s)
        with ExitStack() as s:
            tb = sb("tb", [P, KC, TOK], F32, s)
            with ExitStack() as s2:
                oret = sb("oret", [P, TILES, D_MODEL], F32, s2)
                decay = sb("decay", [P, 2, SEQ], F32, s2)
                rk = sb("rk", [P, TILES, UC], F32, s2)
                gs = sb("gs", [P, TILES, UC], F32, s2)
                sin = sb("sin", [P, RET_DV], F32, s2)
                sout = sb("sout", [P, 2, RET_DV], F32, s2)
                s2.close()
            with ExitStack() as s2:
                sb("oret_again", [P, TILES, D_MODEL], F32, s2)
                oret_sq = sb("sq", [P, TILES, 512], F32, s2)
            hl2 = sb("hl2", [P, KC, 2, TOK], F32R, s)
            xs2 = sb("xs2", [P, KC, 2, DEC], F32R, s)
        with ExitStack() as s:
            sT = sb("sT", [P, 1280], F32, s)
            vr = sb("vr", [P, TILES, UC], F32, s)
            qrT = sb("qrT", [P, TOK], F32, s)
            krT = sb("krT", [P, TOK], F32, s)
            kz = sb("kz", [P, TILES, RET_DK], F32, s)
        mix.close()
        with ExitStack() as s:
            xn = sb("xn", [P, TILES, D_MODEL], F32, s)
        with ExitStack() as s:
            act = sb("act", [P, FB, 2, GP], F32R, s)
            acts = sb("acts", [P, FB, 2, DEC], F32R, s)
            up = sb("up", [P, 2, 2, GP + 2], F32, s)
            ca = sb("ca", [P, 2, GP], F32, s)
            th = sb("th", [P, GP], F32, s)
            af = sb("af", [P, GP], F32, s)
            cs = sb("cs", [P, 4, 2 * FB], F32, s)
            csT = sb("csT", [2 * FB, 4, P], F32, s)

        ps = ctx.enter_context(nc.psum_tensor("ps", [P, 4096], F32))
        BANK = dict(mm0=0, mm1=512, s0=1024, s1=2048, t=3072, o=3584)

        def pv(bank, rows, n, off=0):
            return ps[0:rows, BANK[bank] + off:BANK[bank] + off + n]

        W = dict(A)

        def cols(name, l, col):
            return [(0, UC, W[name][ds(l, 1), :, ds(col, UC)])]

        def units(phase, l, i):
            if phase == "D":
                return [cols("w_in", l, i * UC + COL[n]) for n in ("qd", "kd", "vd", "ga")]
            if phase == "R":
                out = []
                for hh in range(2):
                    q = [(0, P, W["w_in"][ds(l, 1), :, ds(i * 2 * P + hh * P + COL["qr"], P)]),
                         (P, P, W["w_in"][ds(l, 1), :, ds(i * 2 * P + hh * P + COL["kr"], P)])]
                    out += [q, cols("w_in", l, i * 2 * UC + hh * UC + COL["vr"]),
                            cols("w_in", l, i * 2 * UC + hh * UC + COL["gr"])]
                return out
            if phase == "M":
                return ([cols("w_in", l, COL["gb"] + u * UC) for u in range(4)]
                        + [cols(n, l, u * UC) for n in ("w_branch_a", "w_branch_b", "w_out") for u in range(4)])
            if phase == "F":
                out = []
                for j in range(FB):
                    out.append([(0, P, W["w_up"][ds(l, 1), :, ds(i * FB * P + j * P, P)]),
                                (P, P, W["w_up"][ds(l, 1), :, ds(i * FB * P + j * P + D_FF, P)])])
                for hf in range(2):
                    k0 = 0
                    for nk in DOWN[hf]:
                        out.append((nk, W["w_down"][ds(l, 1), ds(i * FB * P + k0 * P, nk * P), hf * 512:hf * 512 + 512]))
                        k0 += nk
                return out
            return []

        UNITS = dict(N=0, D=4, R=6, M=16, F=FB + 7)
        LEN = dict(D=[UNIT] * 4, R=[UNIT] * 6, M=[UNIT] * 16,
                   F=[UNIT] * FB + [nk * 512 for half in DOWN for nk in half])

        def prep_len(phase, j):
            return LEN[phase][j] if j < UNITS.get(phase, 0) else UNIT

        def cache_load(S, e, l, i, hh):
            for buf, name in ((kc_n, "cache_k"), (vc_n, "cache_v")):
                src = A[name][ds(l, 1), 0, :, ds(i * 2 + hh, 1), :]
                e.dma_start(buf[:, :, :], src.rearrange("a (c p) h d -> p (a c h) d", p=P)).then_inc(*S.up(f"cache{hh}", "kv" if name == "cache_v" else None, n=16))

        def sync_program(S):
            e = S.e

            def load_unit(j, what):
                e.wait_ge(*S.at("w_ready", k=j - 2))
                slot = f"raw{j % 2}"
                if isinstance(what, tuple):
                    nk, src = what
                    v = src.rearrange("a (c p) n -> p (a c) n", p=P)
                    r = raw[:, j % 2, 0:nk * 512].rearrange("p (c n) -> p c n", c=nk)
                    cut = [(0, nk - 1), (nk - 1, nk)]
                    for a, b in cut:
                        e.dma_start(r[:, a:b, :], v[:, a:b, :]).then_inc(*S.up(slot, n=16))
                    return
                r = raw[:, j % 2, :].rearrange("p (c n) -> p c n", c=KC)
                if len(what) == 2:
                    for c0, n, src in what:
                        e.dma_start(r[:, :, c0:c0 + n], src.rearrange("a (c p) n -> p (a c) n", p=P)).then_inc(*S.up(slot, n=16))
                else:
                    v = what[0][2].rearrange("a (c p) n -> p (a c) n", p=P)
                    for a in (0, KC // 2):
                        e.dma_start(r[:, a:a + KC // 2, :], v[:, a:a + KC // 2, :]).then_inc(*S.up(slot, n=16))

            S.prime("kv_out", 16)
            e.dma_start(small[:, :], A["tab_small"]).then_inc(*S.up("tables", "small", n=16))
            for m in range(NT):
                e.dma_start(x[:, m, :], A["x_prompt"][0, m * P:(m + 1) * P, :]).then_inc(*S.up("x_in", n=16))
            e.dma_start(x[0:DEC, NT, :], A["x_sample"][0]).then_inc(*S.up("x_in", "x", n=16))
            pr = th
            for l in range(DEPTH):
                o = l * NVEC
                for r0, n, name in ((0, KC, "norm1_g"), (KC, KC, "norm2_g"), (2 * KC, 2, "ret_norm_g"), (18, 1, "diff_norm_g")):
                    e.dma_start(pr[o + r0:o + r0 + n, 0:P], A[name][l].rearrange("(c p) -> c p", p=P)).then_inc(*S.up("params", n=16))
                for v, src in enumerate([A["state_conv"][l, 0, 0], A["state_conv"][l, 0, 1], A["conv_w"][l, 0],
                                         A["conv_w"][l, 1], A["conv_w"][l, 2], A["conv_b"][l]]):
                    e.dma_start(xn[0:2 * FT, l, v * P:(v + 1) * P], src.rearrange("(c p) -> c p", p=P)).then_inc(*S.up("params", n=16))
                for v, name in enumerate(("q_norm_g", "k_norm_g")):
                    e.dma_start(qkg[:, l, v, :], A[name][l].partition_broadcast(P)).then_inc(*S.up("params", n=16))
                for v, name in enumerate(("lambda_q1", "lambda_q2", "lambda_k1", "lambda_k2")):
                    e.dma_start(prob[:, l, v * DIFF_HD:(v + 1) * DIFF_HD], A[name][l].partition_broadcast(P)).then_inc(*S.up("params", n=16))
            S.note("params", "all")
            with S.layers() as l:
                for phase, _ in ORDER:
                    with S.body(phase) as i:
                        us = units(phase, l, i)
                        assert len(us) == UNITS[phase]
                        if phase == "D":
                            for j, what in enumerate(us):
                                load_unit(j, what)
                                if j == 1:
                                    e.wait_ge(*S.at("o_ready", k=0))
                                    e.wait_ge(*S.at("t_ready", k=0))
                                    e.wait_ge(*S.at("pool_step", k=0))
                                    cache_load(S, e, l, i, 0)
                            e.wait_ge(*S.at("dve_step", ("rope", "k")))
                            for m in (0, 4):
                                dst = A["new_k_prompt"][ds(l, 1), 0, :, ds(i * 2, 2), :].rearrange("a (c p) h d -> p (a c) h d", p=P) \
                                    if m == 0 else A["new_k_sample"][ds(l, 1), 0, :, ds(i * 2, 2), :].rearrange("a s h d -> s a h d")
                                src = rawk[:, 0:NT, :] if m == 0 else rawk[0:DEC, NT:TILES, :]
                                e.dma_start(dst, src.rearrange("p c (h d) -> p c h d", h=2)).then_inc(*S.up("kv_out", ("k", m), n=16))
                            e.wait_ge(*S.at("act_free_mm1", ("v", 3)))
                            e.wait_ge(*S.at("act_free_mm0", ("v", 2)))
                            e.wait_ge(*S.at("dve_step", ("rest", "v")))
                            for m in (0, 4):
                                dst = A["new_v_prompt"][ds(l, 1), 0, :, ds(i * 2, 2), :].rearrange("a (c p) h d -> p (a c) h d", p=P) \
                                    if m == 0 else A["new_v_sample"][ds(l, 1), 0, :, ds(i * 2, 2), :].rearrange("a s h d -> s a h d")
                                src = vd[:, 0:NT, :] if m == 0 else vd[0:DEC, NT:TILES, :]
                                e.dma_start(dst, src.rearrange("p c (h d) -> p c h d", h=2)).then_inc(*S.up("kv_out", ("v", m), n=16))
                        elif phase == "R":
                            for j, what in enumerate(us):
                                load_unit(j, what)
                                if j == 0:
                                    e.wait_ge(*S.at("pe_step", k=0))
                                    e.wait_ge(*S.at("dve_step", k=0))
                                    e.wait_ge(*S.at("act_step", k=0))
                                    e.wait_ge(*S.at("act_free_t", k=0))
                                    e.wait_ge(*S.at("dve_free_t", k=0))
                                    e.wait_ge(*S.at("dve_free_o", k=0))
                                    e.dma_start(decay[:, :, :].rearrange("p h n -> p (h n)"),
                                                         A["tab_decay"][:, ds(i * 2 * SEQ, 2 * SEQ)]).then_inc(*S.up("decay_in", "d", n=16))
                                if j in (0, 3):
                                    hh = j // 3
                                    if hh:
                                        e.wait_ge(*S.at("dve_free_t", ("snew", 0)))
                                    e.dma_start(sin[:, :], A["state_ret"][ds(l, 1), 0, ds(i * 2 + hh, 1)]
                                             .rearrange("a h d e -> d (a h e)")).then_inc(*S.up("sin_in", ("s", hh), n=16))
                        else:
                            for j, what in enumerate(us):
                                load_unit(j, what)
            e.wait_ge(*S.at("w_ready", k=-2))
            for a in (0, KC // 2):
                e.dma_start(raw[:, 0, a * UC:(a + KC // 2) * UC].rearrange("p (c n) -> p c n", c=KC // 2),
                                     A["w_in"][0, a * P:(a + KC // 2) * P, 0:UC].rearrange("(c p) n -> p c n", p=P)).then_inc(*S.up("raw0", n=16))
            e.wait_ge(*S.at("dve_step", k=0))
            for m in range(TILES):
                dst = A["y_prompt"][0, m * P:(m + 1) * P, :] if m < NT else A["y_sample"][0]
                e.dma_start(dst, x[0:ROWS[m], m, :]).then_inc(*S.up("y_out", "y%d" % m, n=16))
            e.wait_ge(*S.at("y_out", k=TILES * 16))
            e.wait_ge(*S.at("kv_out", k=0))
            e.wait_ge(*S.at("st_out0", k=0))
            e.wait_ge(*S.at("st_out1", k=0))
            e.wait_ge(*S.at("cs_out", k=0))
            e.wait_ge(*S.at("w_ready", k=0))

        def pool_program(S):
            e = S.e

            def lo(phase, j):
                n = prep_len(phase, j)
                s = j % 2
                e.wait_ge(*S.at("hi_ready", k=j)) if phase != "P" else e.wait_ge(*S.at("hi_ready", ("hi", 0)))
                e.tensor_tensor(wlo[:, s, 0:n], raw[:, s, 0:n], whi[:, s, 0:n].bitcast(F32), ALU.subtract).then_inc(*S.up("w_ready", ("lo", j)))

            def power(n, key):
                e.wait_ge(*S.at("dve_step", ("ms", key)))
                e.tensor_tensor(rstd[:, 0:n], ms[:, 0:n], mhalf[:, 0:n], ALU.pow).then_inc(*S.up("pool_step", ("rstd", key)))

            S.prime("w_ready", 2)
            S.prime("pool_step", 1)
            e.memset(mhalf[:, :], -0.5).then_inc(*S.up("pool_step"))
            lo("P", 0)
            with S.layers() as l:
                with S.body("N"):
                    power(5, "n")
                with S.body("D") as p:
                    lo("D", 1)
                    power(20, "q")
                    lo("D", 2)
                    power(20, "k")
                    lo("D", 3)
                    lo("D", 4)
                with S.body("R") as i:
                    for hh in range(2):
                        for j in range(3 * hh + 1, 3 * hh + 4):
                            lo("R", j)
                with S.body("M"):
                    lo("M", 1)
                    power(40, "dif")
                    lo("M", 2)
                    power(20, "ret")
                    for j in range(3, 17):
                        lo("M", j)
                        if j == 16:
                            power(5, "n")
                with S.body("F") as f:
                    for j in range(FB):
                        lo("F", j + 1)
                    for j in range(FB, UNITS["F"]):
                        lo("F", j + 1)

        def pe_program(S):
            e = S.e
            free = {}

            def acquire(bank, act=0, dve=0):
                if bank not in free:
                    free[bank] = {"act": 0, "dve": 0, "last": ("act", "dve")}
                b = free[bank]
                for who in b["last"]:
                    e.wait_ge(*S.at(f"{who}_free_{bank}", k=b[who]))
                b["last"] = tuple(w for w, n in (("act", act), ("dve", dve)) if n)
                b["act"] += act
                b["dve"] += dve

            def start():
                free.clear()

            tile = [0]

            def mm_bank():
                tile[0] += 1
                return f"mm{(tile[0] - 1) % 2}"

            def ready(ins, *keys):
                ins.then_inc(*S.up("mm_ready", keys[0]))
                for k in keys[1:]:
                    S.note("mm_ready", k)

            def t_tile(j, col, half, X, act=0, dve=0):
                bank = mm_bank()
                acquire(bank, act, dve)
                out = pv(bank, P, HALF)
                for c in range(KC):
                    w0 = c * UC + col * P
                    hi, lo = (X[:, c, v, half * HALF:(half + 1) * HALF] for v in (0, 1))
                    wh, wl = whi[:, j % 2, w0:w0 + P], wlo[:, j % 2, w0:w0 + P]
                    e.matmul(out, wh, hi, start=(c == 0), stop=False)
                    e.matmul(out, wh, lo, start=False, stop=False)
                    ins = e.matmul(out, wl, hi, start=False, stop=(c == KC - 1))
                keys = [("T", j, col, half)] + ([("end", j)] if col and half else [])
                ready(ins, *keys)

            def n_tile(j, m, X, XS, act=0, dve=0):
                bank = mm_bank()
                acquire(bank, act, dve)
                if m < NT:
                    out = pv(bank, P, UC)
                    for c in range(KC):
                        hi, lo = (X[:, c, v, m * P:(m + 1) * P] for v in (0, 1))
                        wh, wl = (w[:, j % 2, c * UC:(c + 1) * UC] for w in (whi, wlo))
                        e.matmul(out, hi, wh, start=(c == 0), stop=False)
                        e.matmul(out, hi, wl, start=False, stop=False)
                        ins = e.matmul(out, lo, wh, start=False, stop=(c == KC - 1))
                    ready(ins, ("N", j, m))
                else:
                    out = pv(bank, 2 * DEC, UC)
                    for c in range(KC):
                        st = XS[:, c, :, :].rearrange("p v s -> p (v s)")
                        e.matmul(out, st, whi[:, j % 2, c * UC:(c + 1) * UC], start=(c == 0), stop=False)
                        ins = e.matmul(out, st, wlo[:, j % 2, c * UC:(c + 1) * UC], start=False, stop=(c == KC - 1))
                    ready(ins, ("N", j, m), ("end", j))

            def n_unit(j, X, XS, dve=False, after=None):
                e.wait_ge(*S.at("w_ready", k=j))
                for m in range(TILES):
                    if m == NT:
                        n_tile(j, m, X, XS, act=1, dve=1)
                    else:
                        n_tile(j, m, X, XS, act=int(not dve), dve=int(dve))
                    if after:
                        after(m)

            def feature_transposes(src, bank, key, act, dve):
                acquire(bank, act, dve)
                for m in range(TILES):
                    ins = e.transpose(pv(bank, P, ROWS[m], m * P), src(m), ident[0:ROWS[m], 0:ROWS[m]])
                ins.then_inc(*S.up("s_ready", key))

            def norm(key):
                for c in range(KC):
                    if c == 0:
                        e.wait_ge(*S.at("dve_step", ("xn", key)))
                    feature_transposes(lambda m: xn[0:ROWS[m], m, c * P:(c + 1) * P], f"s{c % 2}", ("norm", c), 1, 1)

            S.prime("mm_ready", 1)
            S.prime("pe_step", 1)
            S.prime("o_ready", 1)
            S.prime("t_ready", 1)
            S.prime("s_ready", 1)
            e.wait_ge(*S.at("tables", "small"))
            e.wait_ge(*S.at("params", "all"))
            n = DEPTH * NVEC
            e.transpose(pv("t", P, n), th[0:n, 0:P], ident[0:n, 0:n])
            for l in range(DEPTH):
                for v in range(6):
                    o = (l * 6 + v) * 2 * FT
                    ins = e.transpose(ps[:, BANK[f"s{l}"] + v * 2 * FT:BANK[f"s{l}"] + (v + 1) * 2 * FT],
                                      xn[0:2 * FT, l, v * P:(v + 1) * P], ident[0:2 * FT, 0:2 * FT])
            ins.then_inc(*S.up("pe_step", "params"))
            with S.layers():
                with S.body("N"):
                    start()
                    norm("n")
                with S.body("D"):
                    start()
                    tile[0] = 0
                    e.wait_ge(*S.at("act_step", k=0))
                    n_unit(0, hl1, xs)

                    def cached_keys(hh):
                        e.wait_ge(*S.at(f"cache{hh}", "kv"))
                        acquire("t", act=1)
                        for c in range(NT):
                            ins = e.transpose(pv("t", P, P, c * P), kc_n[:, c, :], ident)
                        ins.then_inc(*S.up("t_ready", ("kc", hh)))

                    n_unit(1, hl1, xs)
                    for hh in range(2):
                        if hh == 0:
                            e.wait_ge(*S.at("dve_step", ("rope", "q")))
                        feature_transposes(lambda m: rawq[0:ROWS[m], m, hh * P:(hh + 1) * P], f"s{hh}", ("q", hh), 1, 2)
                    n_unit(2, hl1, xs)
                    cached_keys(0)
                    for hh in range(2):
                        if hh == 0:
                            e.wait_ge(*S.at("dve_step", ("rope", "k")))
                        feature_transposes(lambda m: rawk[0:ROWS[m], m, hh * P:(hh + 1) * P], f"s{hh}", ("k", hh), 1, 0)
                    e.wait_ge(*S.at("w_ready", k=3))

                    steps = [(hh, ib) for hh in range(2) for ib in range(TILES)]

                    def scores(n):
                        hh, ib = steps[n]
                        bank = f"s{n % 2}"
                        if ib < NT:
                            acquire(bank, act=1)
                            if n == 0:
                                e.wait_ge(*S.at("act_free_s0", ("q", 0)))
                                e.wait_ge(*S.at("dve_free_s0", ("q1", 0)))
                                e.wait_ge(*S.at("act_free_s0", ("k", 0)))
                            if n == 5:
                                e.wait_ge(*S.at("dve_free_s1", ("q1", 1)))
                                e.wait_ge(*S.at("act_free_s1", ("k", 1)))
                            keys = (ib + 1) * P
                            for c in range(2):
                                o = c * (TOK + DEC) + ib * P
                                ins = e.matmul(pv(bank, P, keys, c * 512), qz[:, hh, o:o + P], kdT[:, hh, 0:keys],
                                               start=True, stop=True)
                        else:
                            acquire(bank, act=1)
                            e.wait_ge(*S.at("act_free_t", ("kc", hh)))
                            st = qz[:, hh, SEQ:SEQ + 2 * DEC]
                            e.matmul(pv(bank, 2 * DEC, PAST), st, kcT[:, :], start=True, stop=True)
                            ins = e.matmul(pv(bank, 2 * DEC, DEC, PAST), st, kdT[:, hh, SEQ:TOK], start=True, stop=True)
                        ins.then_inc(*S.up("s_ready", ("s", n)))

                    def weighted(n):
                        hh, ib = steps[n]
                        e.wait_ge(*S.at("dve_step", ("a", n)))
                        if ib < NT:
                            acquire("t", act=1)
                            for jb in range(ib + 1):
                                ins = e.transpose(pv("t", P, P, jb * P), prob[:, n % 2, jb * P:(jb + 1) * P], ident)
                            ins.then_inc(*S.up("t_ready", ("a", n)))
                        else:
                            acquire("t", act=2, dve=2)
                            S.settle()
                            for c in range(TILES):
                                ins = e.transpose(pv("t", ROWS[c], 2 * DEC, c * 2 * DEC),
                                                  prob[0:2 * DEC, n % 2, c * P:c * P + ROWS[c]], ident[0:2 * DEC, 0:2 * DEC])
                            ins.then_inc(*S.up("t_ready", ("a", n)))

                    def values(n):
                        hh, ib = steps[n]
                        acquire("o", dve=1)
                        if ib < NT:
                            e.wait_ge(*S.at("act_free_t", ("aT", n)))
                            if n == 0:
                                e.wait_ge(*S.at("act_free_mm1", ("v", 3)))
                                e.wait_ge(*S.at("act_free_mm0", ("v", 2)))
                            for jb in range(ib + 1):
                                ins = e.matmul(pv("o", P, HW), aT[:, n % 2, jb * P:(jb + 1) * P],
                                               vd[:, jb, hh * HW:(hh + 1) * HW], start=(jb == 0), stop=(jb == ib))
                        else:
                            e.wait_ge(*S.at("dve_free_t", ("aT", n)))
                            e.wait_ge(*S.at("dve_step", ("rest", "v")))
                            for c in range(TILES):
                                r = ROWS[c]
                                v = vc_n[:, c, :] if c < NT else vd[0:DEC, NT, hh * HW:(hh + 1) * HW]
                                ins = e.matmul(pv("o", DEC, HW), aTs[0:r, c, :], v, start=(c == 0), stop=(c == NT))
                        ins.then_inc(*S.up("o_ready", (hh, ib)))

                    def gate_tile(t):
                        t_tile(3, t // 2, t % 2, hl1, act=1)

                    gate_tile(0)
                    scores(0)
                    scores(1)
                    for n in range(10):
                        if n in (1, 4, 7):
                            gate_tile({1: 1, 4: 2, 7: 3}[n])
                        weighted(n)
                        if n + 2 < 10:
                            scores(n + 2)
                        values(n)
                        if n == 6:
                            cached_keys(1)
                with S.body("R"):
                    start()
                    tile[0] = 0
                    for hh in range(2):
                        u = 3 * hh
                        n_unit(u, hl1, xs)
                        n_unit(u + 1, hl1, xs)
                        e.wait_ge(*S.at("dve_step", ("rope", hh)))
                        for v in range(2):
                            feature_transposes(lambda m: rk[0:ROWS[m], m, v * P:(v + 1) * P], f"s{v}", ("qk", hh, v), 1, 0)
                        e.wait_ge(*S.at("w_ready", k=u + 2))

                        def rscores(jb):
                            n = SEQ - jb * P
                            if jb == 0:
                                e.wait_ge(*S.at("act_free_s0", ("qk", hh, 0)))
                                e.wait_ge(*S.at("act_free_s1", ("qk", hh, 1)))
                                acquire("s0", dve=2)
                            if jb == 2:
                                acquire("s1", dve=2)
                            bank = "s0" if jb < 2 else "s1"
                            e.matmul(pv(bank, P, n, (jb % 2) * 512), krT[:, jb * P:(jb + 1) * P], qrT[:, jb * P:SEQ],
                                              start=True, stop=True).then_inc(*S.up("s_ready", ("ret", hh, jb)))

                        def outs(ib):
                            bank = "to"[ib % 2]
                            acquire(bank, act=1, dve=1)
                            e.wait_ge(*S.at(("dve_free_s0", "dve_free_s1")[ib // 2], ("sT", hh, ib)))
                            for jb in range(ib + 1):
                                o = SOFF[jb] + (ib - jb) * P
                                ins = e.matmul(pv(bank, P, RET_DV), sT[:, o:o + P], vr[:, jb, :], start=(jb == 0), stop=(jb == ib))
                            ins.then_inc(*S.up(("t_ready", "o_ready")[ib % 2], ("o", hh, ib)))

                        j = u + 2
                        n_tile(j, 0, hl1, xs, dve=1, act=1)
                        rscores(0)
                        rscores(1)
                        n_tile(j, 1, hl1, xs, dve=1, act=1)
                        rscores(2)
                        rscores(3)
                        n_tile(j, 2, hl1, xs, dve=1, act=1)
                        outs(0)
                        outs(1)
                        acquire("s0", dve=1)
                        S.settle()
                        e.matmul(pv("s0", DEC, DEC), krT[:, SEQ:TOK], qrT[:, SEQ:TOK], start=True, stop=True).then_inc(*S.up("s_ready", ("rets", hh)))
                        n_tile(j, 3, hl1, xs, dve=1, act=1)
                        outs(2)
                        outs(3)
                        n_tile(j, 4, hl1, xs, act=1, dve=2)
                        acquire("t", act=1, dve=1)
                        e.wait_ge(*S.at("dve_step", ("qx", hh)))
                        e.wait_ge(*S.at("sin_in", ("s", hh)))
                        S.settle()
                        e.matmul(pv("t", DEC, RET_DV), sTs_x[:, :], vr[0:DEC, NT, :], start=True, stop=False)
                        e.matmul(pv("t", DEC, RET_DV), qx[:, :], sin[:, :], start=False, stop=True).then_inc(*S.up("t_ready", ("os", hh)))
                        acquire("o", act=1)
                        e.wait_ge(*S.at("dve_step", ("kz", hh)))
                        for m in range(NT):
                            ins = e.matmul(pv("o", P, RET_DV), kz[:, m, :], vr[:, m, :], start=(m == 0), stop=(m == NT - 1))
                        ins.then_inc(*S.up("o_ready", ("sfin", hh)))
                        acquire("t", dve=1)
                        e.matmul(pv("t", P, RET_DV), kz[0:DEC, NT, :], vr[0:DEC, NT, :], start=True, stop=True).then_inc(*S.up("t_ready", ("snew", hh)))
                with S.body("M"):
                    start()
                    tile[0] = 0

                    def t_unit(j, X, act=0, dve=0, after=None):
                        e.wait_ge(*S.at("w_ready", k=j))
                        for t in range(4):
                            t_tile(j, t // 2, t % 2, X, act, dve)
                            if after:
                                after(t)

                    for j in range(4):
                        t_unit(j, hl1, act=1)
                    e.wait_ge(*S.at("dve_step", ("oret", "done")))
                    for c in range(KC):
                        feature_transposes(lambda m: oret[0:ROWS[m], m, c * P:(c + 1) * P], f"s{c % 2}", ("ret", c), 1, 2)
                    e.wait_ge(*S.at("act_step", ("hl", "ret")))
                    e.wait_ge(*S.at("dve_step", ("lo", "ret", KC - 1)))

                    def dif_chunk(c):
                        if c == 0:
                            e.wait_ge(*S.at("dve_step", ("odif", "done")))
                        feature_transposes(lambda m: odif[0:ROWS[m], m, c * P:(c + 1) * P], f"s{c % 2}", ("dif", c), 1, 1)

                    for u in range(4):
                        t_unit(4 + u, hl1, dve=1, after=lambda t, u=u: dif_chunk(2 * u + t // 2) if t % 2 else None)
                    e.wait_ge(*S.at("dve_free_s1", ("lo", "dif", KC - 1)))
                    e.wait_ge(*S.at("dve_free_s0", ("lo", "dif", KC - 2)))
                    for u in range(4):
                        t_unit(8 + u, hl2, dve=1)
                    e.wait_ge(*S.at("act_step", ("xs", "mer")))
                    e.wait_ge(*S.at("dve_step", ("lo", "mer")))
                    for u in range(4):
                        n_unit(12 + u, hl1, xs, dve=True)
                    norm("n")
                with S.body("F"):
                    start()
                    tile[0] = 0
                    e.wait_ge(*S.at("act_step", k=0))
                    for j in range(FB):
                        e.wait_ge(*S.at("w_ready", k=j))
                        for t in range(4):
                            t_tile(j, t // 2, t % 2, hl1, act=(2 if t % 2 else 1) * (t < 2), dve=(2 if t % 2 else 1) * (t >= 2))

                    def conv_rows():
                        acquire("t", dve=1)
                        e.wait_ge(*S.at("dve_step", ("cs", FB - 1)))
                        for q in range(4):
                            ins = e.transpose(pv("t", 2 * FB, P, q * P), cs[:, q, :], ident)
                        ins.then_inc(*S.up("t_ready", "cs"))

                    e.wait_ge(*S.at("act_step", ("acts", 0)))
                    e.wait_ge(*S.at("dve_step", ("alo", FB - 1)))
                    j = FB
                    for hf in range(2):
                        acquire("mm0", dve=1)
                        acquire("mm1", dve=1)
                        acquire("s0", dve=2)
                        acquire("s1", act=1, dve=1)
                        kc = 0
                        for nk in DOWN[hf]:
                            e.wait_ge(*S.at("w_ready", k=j))
                            for q in range(nk):
                                last = kc == FB - 1
                                wh, wl = (w[:, j % 2, q * 512:(q + 1) * 512] for w in (whi, wlo))
                                for m in range(NT):
                                    out = ps[:, m * 512:(m + 1) * 512]
                                    hi, lo = (act[:, kc, v, m * P:(m + 1) * P] for v in (0, 1))
                                    e.matmul(out, hi, wh, start=(kc == 0), stop=False)
                                    e.matmul(out, hi, wl, start=False, stop=False)
                                    ins = e.matmul(out, lo, wh, start=False, stop=last)
                                    if last:
                                        ready(ins, ("down", hf, m))
                                st = acts[:, kc, :, :].rearrange("p v s -> p (v s)")
                                out = ps[0:2 * DEC, 2048:2560]
                                e.matmul(out, st, wh, start=(kc == 0), stop=False)
                                ins = e.matmul(out, st, wl, start=False, stop=last)
                                if last:
                                    ready(ins, ("down", hf, NT), ("end", j))
                                elif q == nk - 1:
                                    ready(ins, ("end", j))
                                kc += 1
                            j += 1
                        if hf == 0:
                            conv_rows()

        SOFF = [0, 512, 896, 1152]

        def act_program(S):
            e = S.e


            def hi(phase, j, part):
                n = prep_len(phase, j)
                s = j % 2
                if part == 0:
                    if phase != "P":
                        if j >= 2:
                            e.wait_ge(*S.at("mm_ready", ("end", j - 2)))
                        else:
                            e.wait_ge(*S.at("mm_ready", k=0))
                    e.wait_ge(*S.at(f"raw{s}", k=32 * (j // 2 + 1) if phase != "P" else 32))
                a, b = (0, n // 2) if part == 0 else (n // 2, n)
                if part == 0:
                    e.activation(whi[:, s, a:b], raw[:, s, a:b], ACT.Copy)
                else:
                    e.activation(whi[:, s, a:b], raw[:, s, a:b], ACT.Copy).then_inc(*S.up("hi_ready", ("hi", j)))

            def prep(phase, j):
                hi(phase, j, 0)
                hi(phase, j, 1)

            def wait_rest(prev):
                if prev is None:
                    e.wait_ge(*S.at("dve_step", k=0))
                else:
                    e.wait_ge(*S.at("dve_step", prev))

            def rest_copy(bank, key, prev, n=UC):
                e.wait_ge(*S.at("mm_ready", key))
                wait_rest(prev)
                e.wait_ge(*S.own())
                e.activation(rest[:, 0:n], ps[DEC:2 * DEC, BANK[bank]:BANK[bank] + n], ACT.Copy).then_inc(*S.up(f"act_free_{bank}", ("rest",) + key))

            def norm(key):
                for m in range(TILES):
                    r = ROWS[m]
                    if m == 0:
                        if key == "n" and S.phase == "N":
                            e.wait_ge(*S.at("dve_step", k=0))
                            e.wait_ge(*S.at("pe_step", k=0))
                        else:
                            e.wait_ge(*S.at("dve_step", ("xdone", 3)))
                    if m == 4 and S.phase == "M":
                        e.wait_ge(*S.at("dve_step", ("xdone", 4)))
                    e.activation(xn[0:r, m, :], x[0:r, m, :], ACT.Square, accum_out=ss[0:r, m:m + 1]).then_inc(*S.up("act_step", key=("ssq", key, m)))
                for c in range(KC):
                    g = vecs[:, ds(S.layer, 1), (c if S.phase == "N" else KC + c):(c if S.phase == "N" else KC + c) + 1].rearrange(
                        "p a b -> p (a b)")
                    e.wait_ge(*S.at("s_ready", ("norm", c)))
                    if c == 0:
                        e.wait_ge(*S.at("mm_ready", k=0)) if S.phase == "N" else e.wait_ge(*S.at("mm_ready", ("end", 15)))
                    e.wait_ge(*S.own())
                    S.settle()
                    e.activation(hl1[:, c, 0, :], pv(f"s{c % 2}", P, TOK), ACT.Copy, scale=g).then_inc(*S.up(f"act_free_s{c % 2}", ("norm", c)))
                e.wait_ge(*S.at("dve_free_s1", ("norm", KC - 1)))
                e.wait_ge(*S.at("dve_free_s0", ("norm", KC - 2)))
                e.wait_ge(*S.own())
                e.activation(xs[:, :, :, :].rearrange("p c v s -> p (c v) s"),
                                hl1[:, :, :, SEQ:TOK].rearrange("p c v s -> p (c v) s"), ACT.Copy).then_inc(*S.up("act_step", key=("xs", key)))

            for b in BANK:
                S.prime(f"act_free_{b}", 1)
            S.prime("act_step", 1)
            for s in ("st_out0", "st_out1", "cs_out"):
                S.prime(s, 16)
            S.prime("hi_ready", 1)
            e.wait_ge(*S.at("raw0", k=32))
            hi("P", 0, 0)
            hi("P", 0, 1)
            e.wait_ge(*S.at("dve_step", "lamp"))
            e.activation(aT[:, 0, 0:2 * DEPTH], aT[:, 0, 8:8 + 2 * DEPTH], ACT.Exp).then_inc(*S.up("act_step", key="lexp"))
            with S.layers() as l:
                with S.body("N"):
                    norm("n")
                with S.body("D") as p:
                    prev = None
                    t = 0
                    for u, (name, buf) in enumerate((("q", rawq), ("k", rawk), ("v", vd))):
                        for m in range(TILES):
                            bank = f"mm{t % 2}"
                            t += 1
                            if m == 0:
                                e.wait_ge(*S.at("dve_step", k=0))
                                e.wait_ge(*S.at("dve_free_o", k=0))
                                e.wait_ge(*S.at("kv_out", k=0))
                                e.wait_ge(*S.at("o_ready", k=0))
                            if m < NT:
                                e.wait_ge(*S.at("mm_ready", ("N", u, m)))
                                e.activation(buf[:, m, :], pv(bank, P, UC), ACT.Copy).then_inc(*S.up(f"act_free_{bank}", (name, m)))
                            else:
                                rest_copy(bank, ("N", u, m), prev)
                                prev = ("rest", name)
                            if m in (0, 1):
                                hi("D", u + 1, m)
                            if u == 1 and m == 0:
                                e.wait_ge(*S.at("dve_step", ("rest", "q")))
                                e.wait_ge(*S.own())
                                e.activation(prob[:, :, :].rearrange("p a b -> p (a b)")[:, 0:TILES * UC],
                                                rawq[:, :, :].rearrange("p a b -> p (a b)"), ACT.Square).then_inc(*S.up("act_step", key=("sq", "q")))
                            if u == 2 and m == 0:
                                e.wait_ge(*S.at("dve_step", ("rest", "k")))
                                e.wait_ge(*S.at("dve_step", ("ss", "q")))
                                e.wait_ge(*S.own())
                                e.activation(prob[:, :, :].rearrange("p a b -> p (a b)")[:, 0:TILES * UC],
                                                rawk[:, :, :].rearrange("p a b -> p (a b)"), ACT.Square).then_inc(*S.up("act_step", key=("sq", "k")))
                            if u == 2 and m in (1, 2):
                                hh = m - 1
                                e.wait_ge(*S.at("s_ready", ("q", hh)))
                                e.wait_ge(*S.at("s_ready", k=0))
                                e.activation(qz[0:DIFF_HD, hh, 0:TOK], pv(f"s{hh}", DIFF_HD, TOK), ACT.Copy,
                                                scale=DIFF_HD ** -0.5).then_inc(*S.up(f"act_free_s{hh}", ("q", hh)))
                    e.wait_ge(*S.at("t_ready", ("kc", 0)))
                    e.activation(kcT[:, :], pv("t", P, PAST), ACT.Copy).then_inc(*S.up("act_free_t", ("kc", 0)))
                    for hh in range(2):
                        e.wait_ge(*S.at("s_ready", ("k", hh)))
                        e.activation(kdT[:, hh, :], pv(f"s{hh}", P, TOK), ACT.Copy).then_inc(*S.up(f"act_free_s{hh}", ("k", hh)))

                    def gate(tt):
                        bank = f"mm{(15 + tt) % 2}"
                        e.wait_ge(*S.at("mm_ready", ("T", 3, tt // 2, tt % 2)))
                        e.wait_ge(*S.own())
                        S.settle()
                        e.activation(mer[:, ds(p * 2 + tt // 2, 1), (tt % 2) * HALF:(tt % 2 + 1) * HALF].rearrange("p a b -> p (a b)"),
                                        pv(bank, P, HALF), ACT.Tanh, scale=0.5).then_inc(*S.up(f"act_free_{bank}", ("ga", tt)))

                    steps = [(hh, ib) for hh in range(2) for ib in range(TILES)]

                    def exps(n):
                        hh, ib = steps[n]
                        b = n % 2
                        e.wait_ge(*S.at("dve_step", ("max", n)))
                        if n >= 2:
                            e.wait_ge(*S.at("t_ready", ("a", n - 2)))
                        e.wait_ge(*S.own())
                        if ib < NT:
                            k = (ib + 1) * P
                            for c in range(2):
                                src = pv(f"s{b}", P, k, c * 512)
                                dst = prob[:, b, c * 512:c * 512 + k]
                                i = e.activation(dst, src, ACT.Exp, bias=nmax[:, b, c:c + 1], accum_out=sums[:, b, c:c + 1])
                                if c == 0:
                                    i.then_inc(*S.up("act_step"))
                                else:
                                    i.then_inc(*S.up(f"act_free_s{b}", ("exp", n)))
                        else:
                            e.activation(prob[0:2 * DEC, b, 0:TOK], pv(f"s{b}", 2 * DEC, TOK), ACT.Exp,
                                            bias=nmax[0:2 * DEC, b, 0:1], accum_out=sums[0:2 * DEC, b, 0:1]).then_inc(*S.up(f"act_free_s{b}", ("exp", n)))

                    def turn(n):
                        hh, ib = steps[n]
                        e.wait_ge(*S.at("t_ready", ("a", n)))
                        if n >= 2:
                            e.wait_ge(*S.at("o_ready", steps[n - 2]))
                        e.wait_ge(*S.own())
                        if ib < NT:
                            e.activation(aT[:, n % 2, 0:(ib + 1) * P], pv("t", P, (ib + 1) * P), ACT.Copy).then_inc(*S.up("act_free_t", ("aT", n)))
                        else:
                            v = pv("t", P, TILES * 2 * DEC).rearrange("p (c n) -> p c n", c=TILES)
                            e.activation(aTt[:, 0:NT, :], v[:, 0:NT, DEC:2 * DEC], ACT.Copy).then_inc(*S.up("act_free_t"))
                            e.activation(aTt[0:DEC, NT, :], v[0:DEC, NT, DEC:2 * DEC], ACT.Copy).then_inc(*S.up("act_free_t", ("aTt", n)))

                    hi("D", 4, 0)
                    gate(0)
                    hi("D", 4, 1)
                    exps(0)
                    exps(1)
                    for n in range(10):
                        if n in (1, 4, 7):
                            gate({1: 1, 4: 2, 7: 3}[n])
                        turn(n)
                        if n + 2 < 10:
                            exps(n + 2)
                        if n == 5:
                            e.wait_ge(*S.at("o_ready", (0, NT)))
                            cache_load(S, e, l, p, 1)
                        if n == 6:
                            e.wait_ge(*S.at("t_ready", ("kc", 1)))
                            e.wait_ge(*S.own())
                            e.activation(kcT[:, :], pv("t", P, PAST), ACT.Copy).then_inc(*S.up("act_free_t", ("kc", 1)))
                with S.body("R") as i:
                    prev = None
                    t = 0
                    for hh in range(2):
                        for u, buf in ((0, rk), (1, vr), (2, gs)):
                            for m in range(TILES):
                                bank = f"mm{t % 2}"
                                t += 1
                                j = 3 * hh + u
                                if m == 0 and hh == 0 and u == 0:
                                    for s in ("dve_step", "s_ready", "o_ready", "t_ready", "dve_free_t", "dve_free_o", "dve_free_s0", "dve_free_s1", "kv_out"):
                                        e.wait_ge(*S.at(s, k=0))
                                if m == 0 and hh == 1 and u == 0:
                                    e.wait_ge(*S.at("dve_step", ("kz", 0)))
                                    e.wait_ge(*S.at("s_ready", ("qk", 0, 1)))
                                if m == 0 and hh == 1 and u == 1:
                                    e.wait_ge(*S.at("t_ready", ("snew", 0)))
                                if m == 0 and hh == 1 and u == 2:
                                    e.wait_ge(*S.at("dve_free_t", ("os", 0)))
                                    e.wait_ge(*S.at("dve_free_o", ("o", 0, 3)))
                                key = (("rk", "vr", "gr")[u], hh, m)
                                if m < NT:
                                    e.wait_ge(*S.at("mm_ready", ("N", j, m)))
                                    if u == 2:
                                        e.wait_ge(*S.own())
                                        e.activation(gs[:, m, :], pv(bank, P, UC), ACT.Tanh, scale=0.5).then_inc(*S.up(f"act_free_{bank}", key))
                                    else:
                                        e.activation(buf[:, m, :], pv(bank, P, UC), ACT.Copy).then_inc(*S.up(f"act_free_{bank}", key))
                                else:
                                    rest_copy(bank, ("N", j, m), prev)
                                    prev = ("rest", hh, u)
                                    if u == 2:
                                        e.wait_ge(*S.at("dve_step", ("gsum", hh)))
                                        e.wait_ge(*S.own())
                                        e.activation(gs[0:DEC, NT, :], rest[:, 0:UC], ACT.Tanh, scale=0.5).then_inc(*S.up("act_step", key=("gs", hh)))
                                if m in (0, 1):
                                    hi("R", j + 1, m)
                                if u == 2 and m in (2, 3):
                                    for ib in ((0, 1) if m == 2 else (2, 3)):
                                        squares(S, e, hh, ib, i)
                            if u == 1:
                                for v, dst in ((0, qrT), (1, krT)):
                                    e.wait_ge(*S.at("s_ready", ("qk", hh, v)))
                                    e.wait_ge(*S.own())
                                    e.activation(dst[:, :], pv(f"s{v}", P, TOK), ACT.Copy).then_inc(*S.up(f"act_free_s{v}", ("qk", hh, v)))
                        squares(S, e, hh, NT, i)
                        e.wait_ge(*S.at("o_ready", ("sfin", hh)))
                        if hh:
                            e.wait_ge(*S.at("st_out0", ("st", 0)))
                        else:
                            e.wait_ge(*S.at("st_out0", k=0))
                        e.wait_ge(*S.own())
                        e.activation(sout[:, 0, :], pv("o", P, RET_DV), ACT.Copy).then_inc(*S.up("act_free_o", ("sfin", hh)))
                        for b, (name, w, key) in enumerate((("state_ret_prompt", "act_free_o", ("sfin", hh)),
                                                            ("state_ret_sample", "dve_free_t", ("snew", hh)))):
                            e.wait_ge(*S.at(w, key))
                            e.dma_start(A[name][ds(l, 1), 0, ds(i * 2 + hh, 1)].rearrange("a h d e -> d (a h e)"),
                                                 sout[:, b, :]).then_inc(*S.up(f"st_out{b}", ("st", hh), n=16))
                with S.body("M"):
                    for j in range(16):
                        kind = j // 4
                        if kind == 0:
                            for tt in range(4):
                                bank = f"mm{(4 * j + tt) % 2}"
                                e.wait_ge(*S.at("mm_ready", ("T", j, tt // 2, tt % 2)))
                                if j == 0 and tt == 0:
                                    for s in ("t_ready", "o_ready", "s_ready", "dve_step", "dve_free_t"):
                                        e.wait_ge(*S.at(s, k=0))
                                e.activation(tb[:, 2 * j + tt // 2, (tt % 2) * HALF:(tt % 2 + 1) * HALF], pv(bank, P, HALF),
                                                ACT.Tanh, scale=0.5).then_inc(*S.up(f"act_free_{bank}", ("gb", j, tt)))
                                if tt < 2:
                                    hi("M", j + 1, tt)
                            if j == 0:
                                sqv = oret_sq[:, :, :]
                                e.wait_ge(*S.at("dve_free_o", k=0))
                                for q in range(2):
                                    if q:
                                        e.wait_ge(*S.at("dve_step", ("ssd", 0)))
                                    e.wait_ge(*S.own())
                                    e.activation(sqv, odif[:, :, q * 512:(q + 1) * 512], ACT.Square).then_inc(*S.up("act_step", key=("sqd", q)))
                            if j == 3:
                                for c in range(KC):
                                    g = vecs[:, ds(l, 1), 2 * KC + c % 2:2 * KC + c % 2 + 1].rearrange("p a b -> p (a b)")
                                    e.wait_ge(*S.at("s_ready", ("ret", c)))
                                    if c == 0:
                                        e.wait_ge(*S.at("mm_ready", ("end", 3)))
                                    e.wait_ge(*S.own())
                                    S.settle()
                                    e.activation(hl1[:, c, 0, :], pv(f"s{c % 2}", P, TOK), ACT.Copy, scale=g).then_inc(*S.up(f"act_free_s{c % 2}", ("ret", c)))
                                e.wait_ge(*S.own())
                                e.activation(rest[0:DEC, 0:2], ident[0:DEC, 0:2], ACT.Copy).then_inc(*S.up("act_step", key=("hl", "ret")))
                        elif kind == 1:
                            u = j - 4
                            for tt in range(4):
                                if tt < 2:
                                    hi("M", j + 1, tt)
                                if tt % 2:
                                    c = 2 * u + tt // 2
                                    e.wait_ge(*S.at("s_ready", ("dif", c)))
                                    e.wait_ge(*S.own())
                                    S.settle()
                                    e.activation(hl2[:, c, 0, :], pv(f"s{c % 2}", P, TOK), ACT.Copy, scale=gd[:, ds(l, 1)]).then_inc(*S.up(f"act_free_s{c % 2}", ("dif", c)))
                        elif kind == 2:
                            u = j - 8
                            for tt in range(4):
                                if tt < 2:
                                    hi("M", j + 1, tt)
                                c, h0 = 2 * u + tt // 2, (tt % 2) * HALF
                                e.wait_ge(*S.at("dve_step", ("mer", j, tt)))
                                if j == 8 and tt == 0:
                                    e.wait_ge(*S.at("mm_ready", ("end", 7)))
                                e.wait_ge(*S.own())
                                e.activation(hl1[:, c, 0, h0:h0 + HALF], mer[:, c, h0:h0 + HALF], ACT.Copy, scale=0.5).then_inc(*S.up("act_step", key=("mhi", j, tt)))
                            if u == 3:
                                e.wait_ge(*S.at("dve_step", ("lo", "mer")))
                                e.wait_ge(*S.own())
                                e.activation(xs[:, :, :, :].rearrange("p c v s -> p (c v) s"),
                                                hl1[:, :, :, SEQ:TOK].rearrange("p c v s -> p (c v) s"), ACT.Copy).then_inc(*S.up("act_step", key=("xs", "mer")))
                        else:
                            for m in range(2):
                                hi("M", j + 1, m)
                            rest_copy(f"mm{(48 + (j - 12) * 5 + 4) % 2}", ("N", j, 4), ("rest", j - 1) if j > 12 else None)
                    norm("n")
                with S.body("F") as f:
                    for s in ("dve_step", "s_ready", "dve_free_s0", "dve_free_s1", "dve_free_t", "cs_out", "st_out0", "st_out1", "mm_ready"):
                        e.wait_ge(*S.at(s, k=0))
                    for j in range(FB):
                        b = j % 2
                        w = lambda v, s: conv[:, ds(l, 1), v, ds(f * FB + (j + s * FT), 1)]
                        for tt in range(2):
                            bank = f"mm{tt % 2}"
                            e.wait_ge(*S.at("mm_ready", ("T", j, 0, tt)))
                            if tt == 0 and j >= 2:
                                e.wait_ge(*S.at("dve_step", ("cs", j - 2)))
                                e.wait_ge(*S.at("dve_step", ("conv2", j - 2, 1)))
                            if tt == 0:
                                e.activation(up[:, b, 0, 2:2 + HALF], pv(bank, P, HALF), ACT.Copy).then_inc(*S.up(f"act_free_{bank}", ("ua", j, 0)))
                            else:
                                e.activation(up[:, b, 0, 2 + HALF:2 + SEQ], pv(bank, P, SEQ - HALF), ACT.Copy).then_inc(*S.up(f"act_free_{bank}"))
                                e.activation(up[:, b, 0, 4 + SEQ:4 + TOK], pv(bank, P, DEC, SEQ - HALF), ACT.Copy).then_inc(*S.up(f"act_free_{bank}", ("ua", j, 1)))
                            hi("F", j + 1, tt)
                        for s in range(2):
                            if s == 0:
                                e.wait_ge(*S.at("dve_step", ("pads", j)))
                                if j:
                                    e.wait_ge(*S.at("dve_step", ("af", j - 1)))
                            else:
                                e.wait_ge(*S.at("dve_free_mm1", ("ug", j, 1)))
                            e.wait_ge(*S.own())
                            S.settle()
                            e.activation(ca[:, s, :], up[:, b, s, 0:GP], ACT.Identity, bias=w(5, s), scale=w(2, s)).then_inc(*S.up("act_step", key=("tap0", j, s)))
                        e.wait_ge(*S.at("dve_step", ("conv2", j, 1)))
                        e.wait_ge(*S.own())
                        e.activation(th[:, :], ca[:, 1, :], ACT.Tanh, scale=0.5).then_inc(*S.up("act_step", key=("th", j)))
                        e.wait_ge(*S.at("dve_step", ("af", j)))
                        e.wait_ge(*S.own())
                        e.activation(act[:, j, 0, :], af[:, :], ACT.Copy).then_inc(*S.up("act_step", key=("ahi", j)))
                    e.wait_ge(*S.at("dve_step", ("alo", FB - 1)))
                    e.wait_ge(*S.own())
                    e.activation(acts[:, :, :, :].rearrange("p c v s -> p (c v) s"),
                                    act[:, :, :, GP - DEC:GP].rearrange("p c v s -> p (c v) s"), ACT.Copy).then_inc(*S.up("act_step", key=("acts", 0)))
                    j = FB
                    for hf in range(2):
                        for n, nk in enumerate(DOWN[hf]):
                            prep("F", j + 1)
                            j += 1
                        rest_copy("s1", ("down", hf, NT), ("drest", 0) if hf else None, 512)
                    e.wait_ge(*S.at("dve_free_t", "cs"))
                    for q in range(2):
                        name = ("state_conv_prompt", "state_conv_sample")[q]
                        for s in range(2):
                            dst = A[name][ds(l, 1), 0, :, ds(f * FB * P + s * D_FF, FB * P)].rearrange(
                                "a t (c p) -> c (a t) p", p=P)
                            e.dma_start(dst, csT[s * FB:(s + 1) * FB, 2 * q:2 * q + 2, :]).then_inc(*S.up("cs_out", ("cs", q, s), n=16))

        def squares(S, e, hh, ib, i):
            r = ROWS[ib]
            bank = "to"[ib % 2]
            key = ("o", hh, ib) if ib < NT else ("os", hh)
            e.wait_ge(*S.at(f"dve_free_{bank}", key))
            e.wait_ge(*S.own())
            junk = rk[0:r, 0, :]
            S.settle()
            e.activation(junk, pv(bank, r, RET_DV), ACT.Square,
                                  accum_out=ssr[0:r, ib, ds(i * 2 + hh, 1)]).then_inc(*S.up(f"act_free_{bank}", key))

        def dve_program(S):
            e = S.e





            def mean(n, width, key):
                e.wait_ge(*S.own())
                e.tensor_scalar(ms[:, 0:n], ss[:, 0:n], 1.0 / width, EPS, ALU.mult, ALU.add).then_inc(*S.up("dve_step", key=("ms", key)))

            def norm(key):
                for m in range(TILES):
                    e.wait_ge(*S.at("act_step", ("ssq", key, m)))
                e.wait_ge(*S.at("pool_step", k=0)) if S.phase == "N" else e.wait_ge(*S.at("pool_step", ("rstd", "ret")))
                mean(5, D_MODEL, key)
                e.wait_ge(*S.at("pool_step", ("rstd", key)))
                for m in range(TILES):
                    r = ROWS[m]
                    e.wait_ge(*S.own())
                    e.tensor_scalar(xn[0:r, m, :], x[0:r, m, :], rstd[0:r, m:m + 1], None, ALU.mult).then_inc(*S.up("dve_step", key=("xn", key) if m == NT else None))
                for c in range(KC):
                    o = c if S.phase == "N" else KC + c
                    g = vecs[:, ds(S.layer, 1), o:o + 1].rearrange("p a b -> p (a b)")
                    e.wait_ge(*S.at(f"act_free_s{c % 2}", ("norm", c)))
                    e.wait_ge(*S.own())
                    e.scalar_tensor_tensor(out=hl1[:, c, 1, :], in0=pv(f"s{c % 2}", P, TOK), scalar=g, in1=hl1[:, c, 0, :].bitcast(F32), op0=ALU.mult, op1=ALU.subtract).then_inc(*S.up(f"dve_free_s{c % 2}", ("norm", c)))

            for b in BANK:
                S.prime(f"dve_free_{b}", 1)
            S.prime("dve_step", 1)
            e.wait_ge(*S.at("params", "all"))
            e.wait_ge(*S.at("tables", "small"))
            e.wait_ge(*S.at("x_in", "x"))
            e.memset(ss[:, :], 1.0).then_inc(*S.up("dve_step"))
            e.memset(ssr[:, :, :], 1.0).then_inc(*S.up("dve_step"))
            for l in range(DEPTH):
                v = prob[:, l, 0:4 * DIFF_HD].rearrange("p (a b) -> p a b", a=4)
                e.wait_ge(*S.own())
                e.tensor_tensor(v[:, 0:2, :], v[:, 0:2, :], v[:, 2:4, :], ALU.mult).then_inc(*S.up("dve_step"))
                e.wait_ge(*S.own())
                e.tensor_reduce(aT[:, 0, 8 + 2 * l:10 + 2 * l], v[:, 0:2, :], AX, ALU.add).then_inc(*S.up("dve_step", key="lamp" if l == DEPTH - 1 else None))
            e.wait_ge(*S.at("act_step", "lexp"))
            for l in range(DEPTH):
                e.wait_ge(*S.own())
                e.tensor_tensor(lam[:, l:l + 1], aT[:, 0, 2 * l + 1:2 * l + 2], aT[:, 0, 2 * l:2 * l + 1], ALU.subtract).then_inc(*S.up("dve_step"))
                e.wait_ge(*S.own())
                e.tensor_tensor(lam[:, l:l + 1], lam[:, l:l + 1], lamc[:, l:l + 1], ALU.subtract).then_inc(*S.up("dve_step"))
                e.wait_ge(*S.own())
                e.memset(sgn[0:DEC, l:l + 1], 1.0).then_inc(*S.up("dve_step"))
                e.wait_ge(*S.own())
                e.tensor_copy(sgn[DEC:2 * DEC, l:l + 1], lam[0:DEC, l:l + 1]).then_inc(*S.up("dve_step"))
            e.wait_ge(*S.at("pe_step", "params"))
            for l in range(DEPTH):
                e.wait_ge(*S.own())
                e.tensor_copy(vecs[:, l, :], pv("t", P, NVEC, l * NVEC)).then_inc(*S.up("dve_step"))
                e.wait_ge(*S.own())
                e.tensor_copy(conv[:, l, :, :].rearrange("p a b -> p (a b)"), pv(f"s{l}", P, 12 * FT)).then_inc(*S.up("dve_step"))
                e.wait_ge(*S.own())
                e.tensor_tensor(gd[:, l:l + 1], vecs[:, l, 18:19], lamc[:, 2 + l:3 + l], ALU.mult).then_inc(*S.up("dve_step"))
            with S.layers() as l:
                with S.body("N"):
                    norm("n")
                    for s in ("mm_ready", "s_ready", "act_step"):
                        e.wait_ge(*S.at(s, k=0))
                    e.wait_ge(*S.at("s_ready", ("norm", KC - 1)))
                    e.wait_ge(*S.at("act_step", ("xs", "n")))
                    e.wait_ge(*S.own())
                    e.memset(qz[DIFF_HD:P, :, 0:TOK], 0.0).then_inc(*S.up("dve_step"))
                    e.memset(qz[0:DIFF_HD, :, TOK:2 * TOK], 0.0).then_inc(*S.up("dve_step"))
                    e.memset(rawq[:, NT, :], 0.0).then_inc(*S.up("dve_step"))
                    e.memset(rawk[:, NT, :], 0.0).then_inc(*S.up("dve_step"))
                    e.memset(odif[:, NT, :], 0.0).then_inc(*S.up("dve_step"))
                    e.memset(nmax[:, :, :], 0.0).then_inc(*S.up("dve_step"))
                with S.body("D") as p:
                    lreg = l

                    def sample_sum(buf, bank, key, name):
                        e.wait_ge(*S.at(f"act_free_{bank}", ("rest",) + key))
                        e.wait_ge(*S.own())
                        e.tensor_tensor(buf, pv(bank, DEC, UC), rest[:, 0:UC], ALU.add).then_inc(*S.up(f"dve_free_{bank}"))
                        e.wait_ge(*S.own())
                        e.memset(rinv[:, 0, 2:3], 0.0).then_inc(*S.up("dve_step", key=("rest", name)))

                    def qk_norm(buf, name, v):
                        e.wait_ge(*S.at("act_step", ("sq", name)))
                        e.wait_ge(*S.own())
                        e.tensor_reduce(ss[:, 0:20], prob[:, :, :].rearrange("p a b -> p (a b)")[:, 0:TILES * UC].rearrange(
                            "p (g d) -> p g d", d=DIFF_HD), AX, ALU.add).then_inc(*S.up("dve_step", key=("ss", name)))
                        mean(20, DIFF_HD, name)
                        e.wait_ge(*S.at("pool_step", ("rstd", name)))
                        b3 = buf[:, :, :].rearrange("p m (h d) -> p (m h) d", d=DIFF_HD)
                        e.wait_ge(*S.own())
                        e.tensor_tensor(b3, b3, rstd[:, 0:20].unsqueeze(2).broadcast_to([P, 20, DIFF_HD]), ALU.mult).then_inc(*S.up("dve_step"))
                        e.wait_ge(*S.own())
                        e.tensor_tensor(b3, b3, qkg[:, ds(lreg, 1), v, :].broadcast_to([P, 20, DIFF_HD]), ALU.mult).then_inc(*S.up("dve_step"))
                        b4 = buf[:, :, :].rearrange("p m (h d) -> p m h d", d=DIFF_HD)
                        x1, x2 = b4[:, :, :, 0:8], b4[:, :, :, 8:16]
                        c, s = (t.unsqueeze(2).broadcast_to([P, TILES, 4, 8]) for t in (dcos, dsin))
                        t1, t2 = (rt[:, k, :].rearrange("p (m h d) -> p m h d", m=TILES, h=4) for k in (0, 1))
                        e.wait_ge(*S.own())
                        e.tensor_tensor(t1, x2, s, ALU.mult).then_inc(*S.up("dve_step"))
                        e.wait_ge(*S.own())
                        e.tensor_tensor(t2, x1, s, ALU.mult).then_inc(*S.up("dve_step"))
                        e.wait_ge(*S.own())
                        e.tensor_tensor(x1, x1, c, ALU.mult).then_inc(*S.up("dve_step"))
                        e.wait_ge(*S.own())
                        e.tensor_tensor(x2, x2, c, ALU.mult).then_inc(*S.up("dve_step"))
                        e.wait_ge(*S.own())
                        e.tensor_tensor(x1, x1, t1, ALU.subtract).then_inc(*S.up("dve_step"))
                        e.wait_ge(*S.own())
                        e.tensor_tensor(x2, x2, t2, ALU.add).then_inc(*S.up("dve_step", key=("rope", name)))

                    sample_sum(rawq[0:DEC, NT, :], "mm0", ("N", 0, 4), "q")
                    qk_norm(rawq, "q", 0)
                    sample_sum(rawk[0:DEC, NT, :], "mm1", ("N", 1, 4), "k")
                    for hh in range(2):
                        e.wait_ge(*S.at("s_ready", ("q", hh)))
                        e.wait_ge(*S.own())
                        e.tensor_scalar(qz[DIFF_HD:P, hh, TOK + DEC:TOK + DEC + SEQ], ps[DIFF_HD:P, BANK[f"s{hh}"]:BANK[f"s{hh}"] + SEQ], DIFF_HD ** -0.5, None, ALU.mult).then_inc(*S.up(f"dve_free_s{hh}", key=("q0", hh)))
                        e.wait_ge(*S.own())
                        e.tensor_scalar(qz[DIFF_HD:P, hh, TOK:TOK + DEC], ps[DIFF_HD:P, BANK[f"s{hh}"] + SEQ:BANK[f"s{hh}"] + TOK], DIFF_HD ** -0.5, None, ALU.mult).then_inc(*S.up(f"dve_free_s{hh}", key=("q1", hh)))
                    qk_norm(rawk, "k", 1)
                    sample_sum(vd[0:DEC, NT, :], "mm0", ("N", 2, 4), "v")

                    steps = [(hh, ib) for hh in range(2) for ib in range(TILES)]

                    def maxes(n):
                        hh, ib = steps[n]
                        b = n % 2
                        e.wait_ge(*S.at("s_ready", ("s", n)))
                        if n >= 2:
                            e.wait_ge(*S.at("act_free_s%d" % b, ("exp", n - 2)))
                        if ib < NT:
                            k = (ib + 1) * P
                            v = pv(f"s{b}", P, 1024).rearrange("p (c n) -> p c n", c=2)
                            e.wait_ge(*S.own())
                            e.memset(v[0:CHUNK, :, k - CHUNK:k], NEG).then_inc(*S.up("dve_step"))
                            e.wait_ge(*S.own())
                            e.tensor_reduce(nmax[:, b, :], v[:, :, 0:k], AX, ALU.max, negate=True).then_inc(*S.up("dve_step", key=("max", n)))
                        else:
                            e.wait_ge(*S.own())
                            e.tensor_reduce(nmax[0:2 * DEC, b, 0:1], pv(f"s{b}", 2 * DEC, TOK), AX, ALU.max, negate=True).then_inc(*S.up("dve_step", key=("max", n)))

                    def combine(n):
                        hh, ib = steps[n]
                        b = n % 2
                        e.wait_ge(*S.at(f"act_free_s{b}", ("exp", n)))
                        e.wait_ge(*S.own())
                        if ib < NT:
                            k = (ib + 1) * P
                            e.reciprocal(rinv[:, b, 0:2], sums[:, b, :]).then_inc(*S.up("dve_step"))
                            e.wait_ge(*S.own())
                            e.scalar_tensor_tensor(out=rinv[:, b, 2:3], in0=sums[:, b, 0:1], scalar=lam[:, ds(lreg, 1)], in1=rinv[:, b, 1:2], op0=ALU.mult, op1=ALU.mult).then_inc(*S.up("dve_step"))
                            e.wait_ge(*S.own())
                            e.scalar_tensor_tensor(out=prob[:, b, 0:k], in0=prob[:, b, 512:512 + k], scalar=rinv[:, b, 2:3], in1=prob[:, b, 0:k], op0=ALU.mult, op1=ALU.add).then_inc(*S.up("dve_step", key=("a", n)))
                        else:
                            r = 2 * DEC
                            e.reciprocal(rinv[0:r, b, 0:1], sums[0:r, b, 0:1]).then_inc(*S.up("dve_step"))
                            e.wait_ge(*S.own())
                            e.tensor_tensor(rinv[0:r, b, 2:3], rinv[0:r, b, 0:1], sgn[:, ds(lreg, 1)], ALU.mult).then_inc(*S.up("dve_step"))
                            e.wait_ge(*S.own())
                            e.tensor_scalar(prob[0:r, b, 0:TOK], prob[0:r, b, 0:TOK], rinv[0:r, b, 2:3], None, ALU.mult).then_inc(*S.up("dve_step", key=("a", n)))

                    def weights_of_sample(n):
                        if steps[n][1] < NT:
                            return
                        v = pv("t", P, TILES * 2 * DEC).rearrange("p (c n) -> p c n", c=TILES)
                        e.wait_ge(*S.at("act_free_t", ("aTt", n)))
                        if n > 5:
                            e.wait_ge(*S.at("o_ready", (0, NT)))
                        e.wait_ge(*S.own())
                        e.tensor_tensor(aTs[:, 0:NT, :], v[:, 0:NT, 0:DEC], aTt[:, 0:NT, :], ALU.add).then_inc(*S.up("dve_free_t"))
                        e.wait_ge(*S.own())
                        e.tensor_tensor(aTs[0:DEC, NT, :], v[0:DEC, NT, 0:DEC], aTt[0:DEC, NT, :], ALU.add).then_inc(*S.up("dve_free_t", ("aT", n)))

                    def out(n):
                        hh, ib = steps[n]
                        r = ROWS[ib]
                        e.wait_ge(*S.at("o_ready", (hh, ib)))
                        dst = odif[0:r, ib, ds(p * 2 * HW + hh * HW, HW)]
                        if ib < NT:
                            e.wait_ge(*S.own())
                            e.tensor_scalar(dst, pv("o", P, HW), rinv[:, n % 2, 0:1], None, ALU.mult).then_inc(*S.up("dve_free_o", key=("o", n)))
                        else:
                            e.wait_ge(*S.own())
                            e.tensor_copy(dst, pv("o", r, HW)).then_inc(*S.up("dve_free_o", ("o", n)))

                    maxes(0)
                    maxes(1)
                    combine(0)
                    combine(1)
                    for n in range(10):
                        if n + 2 < 10:
                            maxes(n + 2)
                        weights_of_sample(n)
                        out(n)
                        if n + 2 < 10:
                            combine(n + 2)
                with S.body("R") as i:
                    for hh in range(2):
                        head = i * 2 + hh
                        t0 = 15 * hh

                        def sample_sum(buf, bank, key, u):
                            e.wait_ge(*S.at(f"act_free_{bank}", ("rest",) + key))
                            e.wait_ge(*S.own())
                            e.tensor_tensor(buf, pv(bank, DEC, UC), rest[:, 0:UC], ALU.add).then_inc(*S.up(f"dve_free_{bank}"))
                            e.wait_ge(*S.own())
                            e.memset(qx[:, 0:1], 0.0).then_inc(*S.up("dve_step", key=("rest", hh, u)))

                        if hh == 0:
                            for s in ("s_ready", "o_ready", "t_ready", "kv_out", "act_step", "act_free_t"):
                                e.wait_ge(*S.at(s, k=0))
                            e.wait_ge(*S.own())
                            e.memset(rk[:, NT, :], 0.0).then_inc(*S.up("dve_step"))
                            e.memset(oret[:, NT, :], 0.0).then_inc(*S.up("dve_step")) if False else None
                        sample_sum(rk[0:DEC, NT, :], f"mm{(t0 + 4) % 2}", ("N", 3 * hh, 4), 0)
                        e.wait_ge(*S.at("act_free_mm0", ("rk", hh, 2 if not hh else 3)))
                        e.wait_ge(*S.at("act_free_mm1", ("rk", hh, 3 if not hh else 2)))
                        if hh:
                            e.wait_ge(*S.at("t_ready", ("os", 0)))
                        rv = rk[:, :, :].rearrange("p m (v d) -> p m v d", v=2)
                        x1, x2 = rv[:, :, :, 0:64], rv[:, :, :, 64:128]
                        c, s = (t.unsqueeze(2).broadcast_to([P, TILES, 2, 64]) for t in (rcos, rsin))
                        t1, t2 = (b[:, 0:TILES * 128].rearrange("p (m v d) -> p m v d", m=TILES, v=2) for b in (sT, kzf))
                        if hh:
                            e.wait_ge(*S.at("t_ready", ("snew", 0)))
                        e.wait_ge(*S.own())
                        e.tensor_tensor(t1, x2, s, ALU.mult).then_inc(*S.up("dve_step"))
                        e.wait_ge(*S.own())
                        e.tensor_tensor(t2, x1, s, ALU.mult).then_inc(*S.up("dve_step"))
                        e.wait_ge(*S.own())
                        e.tensor_tensor(x1, x1, c, ALU.mult).then_inc(*S.up("dve_step"))
                        e.wait_ge(*S.own())
                        e.tensor_tensor(x2, x2, c, ALU.mult).then_inc(*S.up("dve_step"))
                        e.wait_ge(*S.own())
                        e.tensor_tensor(x1, x1, t1, ALU.subtract).then_inc(*S.up("dve_step"))
                        e.wait_ge(*S.own())
                        e.tensor_tensor(x2, x2, t2, ALU.add).then_inc(*S.up("dve_step", key=("rope", hh)))
                        e.wait_ge(*S.own())
                        e.tensor_tensor(kz[:, :, :], rk[:, :, P:2 * P], zeta[:, :, ds(head, 1)].broadcast_to([P, TILES, P]), ALU.mult).then_inc(*S.up("dve_step", key=("kz", hh)))
                        sample_sum(vr[0:DEC, NT, :], f"mm{(t0 + 9) % 2}", ("N", 3 * hh + 1, 4), 1)
                        e.wait_ge(*S.at("act_free_s0", ("qk", hh, 0)))
                        e.wait_ge(*S.own())
                        e.tensor_tensor(qx[:, :], qrT[:, SEQ:TOK], xi[:, ds(head, 1), :].rearrange("p a b -> p (a b)"), ALU.mult).then_inc(*S.up("dve_step", key=("qx0", hh)))

                        def gate(m):
                            bank = f"mm{(t0 + 10 + m) % 2}"
                            e.wait_ge(*S.at(f"act_free_{bank}", ("gr", hh, m)))
                            e.wait_ge(*S.own())
                            e.scalar_tensor_tensor(out=gs[:, m, :], in0=gs[:, m, :], scalar=1.0, in1=pv(bank, P, UC), op0=ALU.add, op1=ALU.mult).then_inc(*S.up(f"dve_free_{bank}", ("gr", hh, m)))

                        def decayed(jb):
                            n = SEQ - jb * P
                            bank = ("s0", "s1")[jb // 2]
                            e.wait_ge(*S.at("s_ready", ("ret", hh, jb)))
                            if jb == 0:
                                e.wait_ge(*S.at("decay_in", "d"))
                            e.wait_ge(*S.own())
                            e.tensor_tensor(sT[:, SOFF[jb]:SOFF[jb] + n], pv(bank, P, n, (jb % 2) * 512), decay[:, hh, 0:n], ALU.mult).then_inc(*S.up(f"dve_free_{bank}", ("sT", hh, jb)))

                        def gated(ib):
                            bank = "to"[ib % 2]
                            r = ROWS[ib]
                            key = ("o", hh, ib) if ib < NT else ("os", hh)
                            e.wait_ge(*S.at(f"{'to'[ib % 2]}_ready", key))
                            e.wait_ge(*S.own())
                            e.tensor_tensor(oret[0:r, ib, ds(head * RET_DV, RET_DV)], pv(bank, r, RET_DV), gs[0:r, ib, :], ALU.mult).then_inc(*S.up(f"dve_free_{bank}", key))

                        gate(0)
                        decayed(0)
                        decayed(1)
                        gate(1)
                        decayed(2)
                        decayed(3)
                        gate(2)
                        gated(0)
                        gated(1)
                        e.wait_ge(*S.at("s_ready", ("rets", hh)))
                        e.wait_ge(*S.own())
                        e.tensor_tensor(sTs_x[:, :], pv("s0", DEC, DEC), decay[0:DEC, hh, 0:DEC], ALU.mult).then_inc(*S.up("dve_free_s0", ("sTs", hh)))
                        e.wait_ge(*S.own())
                        e.memset(rstd[:, 39:40], 0.0).then_inc(*S.up("dve_step", key=("qx", hh)))
                        gate(3)
                        gated(2)
                        gated(3)
                        bank = f"mm{(t0 + 14) % 2}"
                        e.wait_ge(*S.at(f"act_free_{bank}", ("rest", "N", 3 * hh + 2, 4)))
                        e.wait_ge(*S.own())
                        e.tensor_tensor(rest[:, 0:UC], pv(bank, DEC, UC), rest[:, 0:UC], ALU.add).then_inc(*S.up(f"dve_free_{bank}"))
                        e.wait_ge(*S.own())
                        e.memset(rstd[:, 39:40], 0.0).then_inc(*S.up("dve_step", key=("gsum", hh)))
                        e.wait_ge(*S.at("act_step", ("gs", hh)))
                        e.wait_ge(*S.own())
                        e.scalar_tensor_tensor(out=gs[0:DEC, NT, :], in0=gs[0:DEC, NT, :], scalar=1.0, in1=rest[:, 0:UC], op0=ALU.add, op1=ALU.mult).then_inc(*S.up(f"dve_free_{bank}"))
                        e.wait_ge(*S.own())
                        e.memset(rstd[:, 39:40], 0.0).then_inc(*S.up("dve_step", key=("rest", hh, 2)))
                        gated(NT)
                        e.wait_ge(*S.at("t_ready", ("snew", hh)))
                        e.wait_ge(*S.at("sin_in", ("s", hh)))
                        e.wait_ge(*S.at("st_out1", ("st", 0))) if hh else e.wait_ge(*S.at("st_out1", k=0))
                        e.wait_ge(*S.own())
                        e.scalar_tensor_tensor(out=sout[:, 1, :], in0=sin[:, :], scalar=g32[:, ds(head, 1)], in1=pv("t", P, RET_DV), op0=ALU.mult, op1=ALU.add).then_inc(*S.up("dve_free_t", ("snew", hh)))
                with S.body("M"):
                    for q in range(2):
                        e.wait_ge(*S.at("act_step", ("sqd", q)))
                        e.wait_ge(*S.own())
                        e.tensor_reduce(ss[:, 0:40].rearrange("p (m q h) -> p m q h", m=TILES, q=2)[:, :, q, :],
                                           oret_sq[:, :, :].rearrange("p m (h d) -> p m h d", h=4), AX, ALU.add).then_inc(*S.up("dve_step", key=("ssd", q)))
                    mean(40, HW, "dif")
                    e.wait_ge(*S.at("pool_step", ("rstd", "dif")))
                    for m in range(TILES):
                        r = ROWS[m]
                        v = odif[0:r, m, :].rearrange("p (h d) -> p h d", h=DIFF_HEADS)
                        e.wait_ge(*S.own())
                        e.tensor_tensor(v, v, rstd[0:r, m * 8:m * 8 + 8].unsqueeze(2).broadcast_to([r, DIFF_HEADS, HW]), ALU.mult).then_inc(*S.up("dve_step", key=("odif", "done") if m == NT else None))
                    e.wait_ge(*S.at("act_free_o", k=0))
                    e.wait_ge(*S.at("act_free_t", k=0))
                    e.wait_ge(*S.own())
                    e.tensor_scalar(ms[:, 0:20], ssr[:, :, :].rearrange("p m h -> p (m h)"), 1.0 / RET_DV, EPS, ALU.mult, ALU.add).then_inc(*S.up("dve_step", key=("ms", "ret")))
                    e.wait_ge(*S.at("pool_step", ("rstd", "ret")))
                    for m in range(TILES):
                        r = ROWS[m]
                        v = oret[0:r, m, :].rearrange("p (h d) -> p h d", h=RET_HEADS)
                        e.wait_ge(*S.own())
                        e.tensor_tensor(v, v, rstd[0:r, m * 4:m * 4 + 4].unsqueeze(2).broadcast_to([r, RET_HEADS, RET_DV]), ALU.mult).then_inc(*S.up("dve_step", key=("oret", "done") if m == NT else None))
                    for c in range(KC):
                        g = vecs[:, ds(l, 1), 2 * KC + c % 2:2 * KC + c % 2 + 1].rearrange("p a b -> p (a b)")
                        e.wait_ge(*S.at(f"act_free_s{c % 2}", ("ret", c)))
                        e.wait_ge(*S.own())
                        e.scalar_tensor_tensor(out=hl1[:, c, 1, :], in0=pv(f"s{c % 2}", P, TOK), scalar=g, in1=hl1[:, c, 0, :].bitcast(F32), op0=ALU.mult, op1=ALU.subtract).then_inc(*S.up(f"dve_free_s{c % 2}"))
                        e.wait_ge(*S.own())
                        e.memset(rstd[:, 39:40], 0.0).then_inc(*S.up(f"dve_free_s{c % 2}"))
                        e.wait_ge(*S.own())
                        e.memset(rstd[:, 39:40], 0.0).then_inc(*S.up("dve_step", key=("lo", "ret", c)))
                    for u in range(4):
                        j = 4 + u
                        for t in range(4):
                            bank = f"mm{t % 2}"
                            c, h0 = 2 * u + t // 2, (t % 2) * HALF
                            e.wait_ge(*S.at("mm_ready", ("T", j, t // 2, t % 2)))
                            if u == 0 and t == 0:
                                e.wait_ge(*S.at("act_free_mm0", k=0))
                                e.wait_ge(*S.at("act_free_mm1", k=0))
                            e.wait_ge(*S.own())
                            e.scalar_tensor_tensor(out=mer[:, c, h0:h0 + HALF], in0=mer[:, c, h0:h0 + HALF], scalar=1.0, in1=pv(bank, P, HALF), op0=ALU.add, op1=ALU.mult).then_inc(*S.up(f"dve_free_{bank}", ("wa", u, t)))
                            if t % 2:
                                e.wait_ge(*S.at(f"act_free_s{c % 2}", ("dif", c)))
                                e.wait_ge(*S.own())
                                e.scalar_tensor_tensor(out=hl2[:, c, 1, :], in0=pv(f"s{c % 2}", P, TOK), scalar=gd[:, ds(l, 1)], in1=hl2[:, c, 0, :].bitcast(F32), op0=ALU.mult, op1=ALU.subtract).then_inc(*S.up(f"dve_free_s{c % 2}", ("lo", "dif", c)))
                    for u in range(4):
                        j = 8 + u
                        for t in range(4):
                            bank = f"mm{t % 2}"
                            c, h0 = 2 * u + t // 2, (t % 2) * HALF
                            e.wait_ge(*S.at("mm_ready", ("T", j, t // 2, t % 2)))
                            e.wait_ge(*S.at(f"act_free_{bank}", ("gb", u, t)))
                            e.wait_ge(*S.own())
                            e.scalar_tensor_tensor(out=tb[:, c, h0:h0 + HALF], in0=tb[:, c, h0:h0 + HALF], scalar=1.0, in1=pv(bank, P, HALF), op0=ALU.add, op1=ALU.mult).then_inc(*S.up(f"dve_free_{bank}"))
                            e.wait_ge(*S.own())
                            e.scalar_tensor_tensor(out=mer[:, c, h0:h0 + HALF], in0=mer[:, c, h0:h0 + HALF], scalar=0.5, in1=tb[:, c, h0:h0 + HALF], op0=ALU.mult, op1=ALU.add).then_inc(*S.up("dve_step", key=("mer", j, t)))
                            e.wait_ge(*S.at("act_step", ("mhi", j, t)))
                            e.wait_ge(*S.own())
                            e.scalar_tensor_tensor(out=hl1[:, c, 1, h0:h0 + HALF], in0=mer[:, c, h0:h0 + HALF], scalar=0.5, in1=hl1[:, c, 0, h0:h0 + HALF].bitcast(F32), op0=ALU.mult, op1=ALU.subtract).then_inc(*S.up("dve_step", key=("lo", "mer") if u == 3 and t == 3 else None))
                    for u in range(4):
                        j = 12 + u
                        for m in range(TILES):
                            bank = f"mm{(5 * u + m) % 2}"
                            r = ROWS[m]
                            v = x[0:r, m, u * UC:(u + 1) * UC]
                            e.wait_ge(*S.at("mm_ready", ("N", j, m)))
                            if m == NT:
                                e.wait_ge(*S.at(f"act_free_{bank}", ("rest", "N", j, m)))
                                e.wait_ge(*S.own())
                                e.tensor_tensor(v, v, rest[:, 0:UC], ALU.add).then_inc(*S.up("dve_step", key=("rest", j)))
                            e.wait_ge(*S.own())
                            e.tensor_tensor(v, v, pv(bank, r, UC), ALU.add).then_inc(*S.up(f"dve_free_{bank}"))
                            if u == 3 and m >= 3:
                                e.wait_ge(*S.own())
                                e.memset(rstd[:, 39:40], 0.0).then_inc(*S.up("dve_step", key=("xdone", m)))
                    norm("n")
                with S.body("F") as f:
                    for s in ("s_ready", "act_step", "t_ready", "mm_ready", "cs_out", "act_free_s1", "act_free_s0"):
                        e.wait_ge(*S.at(s, k=0))
                    e.wait_ge(*S.own())
                    e.memset(up[:, :, :, 0:2], 0.0).then_inc(*S.up("dve_step"))
                    for j in range(FB):
                        b = j % 2
                        w = lambda v, s: conv[:, ds(l, 1), v, ds(f * FB + (j + s * FT), 1)]
                        for s in range(2):
                            e.wait_ge(*S.own())
                            e.tensor_copy(up[:, b, s, SEQ + 2:SEQ + 4],
                                             conv[:, ds(l, 1), 0:2, ds(f * FB + (j + s * FT), 1)].rearrange("p a v c -> p (a v c)")).then_inc(*S.up("dve_step", key=("pads", j) if s else None))
                        for t in range(2):
                            bank = f"mm{t % 2}"
                            e.wait_ge(*S.at("mm_ready", ("T", j, 1, t)))
                            e.wait_ge(*S.own())
                            if t == 0:
                                e.tensor_copy(up[:, b, 1, 2:2 + HALF], pv(bank, P, HALF)).then_inc(*S.up(f"dve_free_{bank}", ("ug", j, 0)))
                            else:
                                e.tensor_copy(up[:, b, 1, 2 + HALF:2 + SEQ], pv(bank, P, SEQ - HALF)).then_inc(*S.up(f"dve_free_{bank}"))
                                e.tensor_copy(up[:, b, 1, 4 + SEQ:4 + TOK], pv(bank, P, DEC, SEQ - HALF)).then_inc(*S.up(f"dve_free_{bank}", ("ug", j, 1)))
                            if t == 0:
                                e.wait_ge(*S.at("act_step", ("tap0", j, 0)))
                                for v in (1, 2):
                                    e.wait_ge(*S.own())
                                    e.scalar_tensor_tensor(out=ca[:, 0, :], in0=up[:, b, 0, v:v + GP], scalar=w(2 + v, 0), in1=ca[:, 0, :], op0=ALU.mult, op1=ALU.add).then_inc(*S.up("dve_step"))
                        e.wait_ge(*S.at("act_step", ("tap0", j, 1)))
                        for v in (1, 2):
                            e.wait_ge(*S.own())
                            e.scalar_tensor_tensor(out=ca[:, 1, :], in0=up[:, b, 1, v:v + GP], scalar=w(2 + v, 1), in1=ca[:, 1, :], op0=ALU.mult, op1=ALU.add).then_inc(*S.up("dve_step", key=("conv2", j, 1) if v == 2 else None))
                        for q in range(2):
                            c0 = SEQ if q == 0 else TOK + 2
                            e.wait_ge(*S.own())
                            e.tensor_copy(cs[:, 2 * q:2 * q + 2, :].rearrange("p t (s c) -> p s t c", s=2)[:, :, :, j],
                                             up[:, b, :, c0:c0 + 2]).then_inc(*S.up("dve_step", key=("cs", j) if q else None))
                        e.wait_ge(*S.at("act_step", ("th", j)))
                        e.wait_ge(*S.own())
                        e.scalar_tensor_tensor(out=ca[:, 1, :], in0=th[:, :], scalar=1.0, in1=ca[:, 1, :], op0=ALU.add, op1=ALU.mult).then_inc(*S.up("dve_step"))
                        if j:
                            e.wait_ge(*S.at("act_step", ("ahi", j - 1)))
                        e.wait_ge(*S.own())
                        e.scalar_tensor_tensor(out=af[:, :], in0=ca[:, 1, :], scalar=0.5, in1=ca[:, 0, :], op0=ALU.mult, op1=ALU.mult).then_inc(*S.up("dve_step", key=("af", j)))
                        e.wait_ge(*S.at("act_step", ("ahi", j)))
                        e.wait_ge(*S.own())
                        e.tensor_tensor(act[:, j, 1, :], af[:, :], act[:, j, 0, :].bitcast(F32), ALU.subtract).then_inc(*S.up("dve_step", key=("alo", j)))
                    for hf in range(2):
                        for m in range(TILES):
                            bank = ("mm0", "mm1", "s0", "s0", "s1")[m]
                            r = ROWS[m]
                            v = x[0:r, m, hf * 512:(hf + 1) * 512]
                            e.wait_ge(*S.at("mm_ready", ("down", hf, m)))
                            if m == NT:
                                e.wait_ge(*S.at("act_free_s1", ("rest", "down", hf, NT)))
                                e.wait_ge(*S.own())
                                e.tensor_tensor(v, v, rest[:, 0:512], ALU.add).then_inc(*S.up("dve_step", key=("drest", hf)))
                            e.wait_ge(*S.own())
                            e.tensor_tensor(v, v, ps[0:r, m * 512:(m + 1) * 512], ALU.add).then_inc(*S.up(f"dve_free_{bank}", ("down", hf, m)))
                        if hf == 0:
                            e.wait_ge(*S.at("t_ready", "cs"))
                            e.wait_ge(*S.at("cs_out", k=0))
                            e.wait_ge(*S.own())
                            e.tensor_copy(csT[:, :, :].rearrange("p a b -> p (a b)"), pv("t", 2 * FB, 4 * P)).then_inc(*S.up("dve_free_t", "cs"))
                    e.wait_ge(*S.own())
                    e.memset(rstd[:, 39:40], 0.0).then_inc(*S.up("dve_step", key="x"))

        kzf = kz[:, :, :].rearrange("p m d -> p (m d)")

        with nc.Block() as block:
            @block.sync
            def _(e):
                sync_program(Stream(e, "sync", known, seen, sem))

            @block.gpsimd
            def _(e):
                pool_program(Stream(e, "pool", known, seen, sem))

            @block.tensor
            def _(e):
                pe_program(Stream(e, "pe", known, seen, sem))

            @block.scalar
            def _(e):
                act_program(Stream(e, "act", known, seen, sem))

            @block.vector
            def _(e):
                dve_program(Stream(e, "dve", known, seen, sem))
    return seen


_INS = ["x_prompt", "x_sample", "cache_k", "cache_v", "state_ret", "state_conv", "norm1_g", "w_in", "ret_norm_g",
        "q_norm_g", "k_norm_g", "lambda_q1", "lambda_k1", "lambda_q2", "lambda_k2", "diff_norm_g", "w_branch_a",
        "w_branch_b", "w_out", "norm2_g", "w_up", "conv_w", "conv_b", "w_down"]
_OUTS = [("y_prompt", (1, SEQ, D_MODEL)), ("y_sample", (1, DEC, D_MODEL)),
         ("new_k_prompt", (DEPTH, 1, SEQ, DIFF_HEADS, HW)), ("new_v_prompt", (DEPTH, 1, SEQ, DIFF_HEADS, HW)),
         ("state_ret_prompt", (DEPTH, 1, RET_HEADS, RET_DK, RET_DV)), ("state_conv_prompt", (DEPTH, 1, 2, 2 * D_FF)),
         ("new_k_sample", (DEPTH, 1, DEC, DIFF_HEADS, HW)), ("new_v_sample", (DEPTH, 1, DEC, DIFF_HEADS, HW)),
         ("state_ret_sample", (DEPTH, 1, RET_HEADS, RET_DK, RET_DV)), ("state_conv_sample", (DEPTH, 1, 2, 2 * D_FF))]


def kernel(**inputs):
    import concourse.bacc as _bacc
    from concourse.bass_utils import run_bass_kernel_spmd

    arrays = {n: np.ascontiguousarray(inputs[n]) for n in _INS}
    arrays["tab_small"], arrays["tab_decay"] = shape_tables()
    counts = None
    for _ in range(2):
        nc = _bacc.Bacc("TRN2", target_bir_lowering=False, num_devices=1)
        tensors = {n: nc.dram_tensor(f"in_{n}_dram", a.shape, F32, kind="ExternalInput").ap() for n, a in arrays.items()}
        for n, s in _OUTS:
            tensors[n] = nc.dram_tensor(f"out_{n}_dram", s, F32, kind="ExternalOutput").ap()
        counts = program(nc, tensors, counts)
    r = run_bass_kernel_spmd(nc, [{f"in_{n}_dram": a for n, a in arrays.items()}], core_ids=[0])
    return tuple(r.results[0][f"out_{n}_dram"] for n, _ in _OUTS)
```

```python
from contextlib import ExitStack, contextmanager

import numpy as np

import concourse.bass as bass
from concourse import mybir

F32 = mybir.dt.float32
F32R = mybir.dt.float32r
ALU = mybir.AluOpType
ACT = mybir.ActivationFunctionType
AX = mybir.AxisListType.X
ds = bass.ds

P = 128
DEPTH = 2
D_MODEL = 1024
SEQ = 512
DEC = 32
PAST = 512
TOK = SEQ + DEC
HALF = TOK // 2
NT = SEQ // P
TILES = NT + 1
ROWS = [P] * NT + [DEC]
RET_HEADS, RET_DK, RET_DV = 4, 128, 256
DIFF_HEADS, DIFF_HD, DIFF_ROT = 8, 64, 16
HW = 2 * DIFF_HD
CHUNK = 64
D_FF = 2816
EPS = 1e-6
KC = D_MODEL // P
UC = 256
UNIT = KC * UC
IN_W = 8192
COL = dict(qr=0, kr=512, vr=1024, gr=2048, qd=3072, kd=4096, vd=5120, ga=6144, gb=7168)
FT = D_FF // P
FB = FT // 2
DOWN = [[4, 4, 3], [3, 3, 3, 2]]
GP = TOK + 2
NEG = -1.0e30
NVEC = 19

ORDER = [("N", 1), ("D", 4), ("R", 2), ("M", 1), ("F", 2)]


def shape_tables():
    f = np.float32
    pos = np.zeros((P, TILES), f)
    for m in range(NT):
        pos[:, m] = m * P + np.arange(P)
    pos[:DEC, NT] = PAST + np.arange(DEC)

    def rope(half, theta):
        inv = (f(theta) ** (-np.arange(half, dtype=f) / f(half))).astype(f)
        ang = (pos[:, :, None] * inv).astype(f)
        return np.cos(ang).astype(f), np.sin(ang).astype(f)

    rc, rs = rope(RET_DK // 2, 10000.0)
    dc, dsn = rope(DIFF_ROT // 2, 500000.0)
    log_g = np.log1p(-np.exp2(-5.0 - np.arange(RET_HEADS, dtype=f))).astype(f)
    ks = f(RET_DK ** -0.5)
    rel = np.arange(SEQ, dtype=f)[None, :] - np.arange(P, dtype=f)[:, None]
    decay = np.where(rel[:, None, :] >= 0, np.exp(log_g[None, :, None] * np.maximum(rel, 0)[:, None, :]), 0) * ks
    zeta = np.zeros((P, TILES, RET_HEADS), f)
    for m in range(NT):
        zeta[:, m] = np.exp(log_g * (SEQ - 1.0 - pos[:, m:m + 1])) * ks
    zeta[:DEC, NT] = np.exp(log_g * (DEC - 1.0 - np.arange(DEC, dtype=f)[:, None])) * ks
    xi = np.exp(log_g[:, None] * (np.arange(DEC, dtype=f) + 1.0))
    lam = [0.8 - 0.6 * np.exp(-0.3 * l) for l in range(DEPTH)]
    small = np.concatenate([
        np.eye(P, dtype=f), rc.reshape(P, -1), rs.reshape(P, -1), dc.reshape(P, -1), dsn.reshape(P, -1),
        zeta.reshape(P, -1), np.broadcast_to(xi.reshape(1, -1), (P, RET_HEADS * DEC)),
        np.broadcast_to(np.exp(log_g * f(DEC))[None], (P, RET_HEADS)),
        np.broadcast_to(np.array([[lam[0], lam[1], 1 - lam[0], 1 - lam[1]]]), (P, 4))], axis=1)
    return small.astype(f), np.ascontiguousarray(decay.astype(f).reshape(P, RET_HEADS * SEQ))


class Counts:

    def __init__(self):
        self.per = {}
        self.keys = {}

    def start(self, phase):
        out = {}
        for name, times in ORDER:
            if name == phase:
                break
            for s, n in self.per.get(name, {}).items():
                out[s] = out.get(s, 0) + n * times
        return out

    def layer(self, sem):
        return sum(self.per.get(name, {}).get(sem, 0) * times for name, times in ORDER)


class Stream:

    def __init__(self, eng, name, known, seen, handles):
        self.e, self.known, self.seen, self.handles = eng, known, seen, handles
        self.step = name + "_step"
        self.layer = self.index = None
        self.phase = "P"
        self.here, self.waited, self.pending = {}, {}, set()
        self.last = None

    @contextmanager
    def layers(self):
        self.leave()
        with self.e.Fori(0, DEPTH) as l:
            self.layer = l
            yield l
        self.layer, self.phase, self.index, self.here, self.waited = None, "end", None, {}, {}

    @contextmanager
    def body(self, phase):
        times = dict(ORDER)[phase]
        self.phase, self.here, self.last, self.waited = phase, {}, None, {}
        if times == 1:
            self.index = None
            yield 0
            self.leave()
        else:
            with self.e.Fori(0, times) as i:
                self.index = i
                yield i
                self.leave()

    def leave(self):
        if self.last and self.waited.get(self.last[0], self.last[1] - 1) < self.last[1]:
            self.e.wait_ge(*self.own())
        self.settle()
        self.last = None
        per = self.seen.per.setdefault(self.phase, {})
        for s, n in self.here.items():
            per[s] = per.get(s, 0) + n

    def at(self, sem, key=None, k=None):
        if k is None:
            k = self.known.keys[(self.phase, sem, key)] if self.known else 1
        k = max(k, self.waited.get(sem, k))
        if sem in self.pending and k > self.waited[sem]:
            self.settle()
        self.waited[sem] = k
        self.pending.add(sem)
        if self.known is None:
            return self.handles(sem), 1
        c = self.known
        if self.phase == "P":
            return self.handles(sem), k
        value = c.per.get("P", {}).get(sem, 0) + k
        if self.phase == "end":
            return self.handles(sem), value + DEPTH * c.layer(sem)
        value += c.start(self.phase).get(sem, 0)
        if c.layer(sem):
            value = self.layer * c.layer(sem) + value
        each = c.per.get(self.phase, {}).get(sem, 0)
        if self.index is not None and each:
            value = self.index * each + value
        return self.handles(sem), value

    def own(self):
        sem, k = self.last or (self.step, self.here.get(self.step, 0))
        return self.at(sem, k=k)

    def up(self, sem, key=None, n=1):
        self.pending.clear()
        self.here[sem] = self.here.get(sem, 0) + n
        if key is not None:
            assert (self.phase, sem, key) not in self.seen.keys, (self.phase, sem, key)
            self.seen.keys[(self.phase, sem, key)] = self.here[sem]
        if n == 1:
            self.last = (sem, self.here[sem])
        return self.handles(sem), n

    def note(self, sem, key):
        self.seen.keys[(self.phase, sem, key)] = self.here[sem]

    def settle(self):
        self.e.sem_inc(self.handles("settled"), 1)
        self.pending.clear()

    def prime(self, sem, n):
        self.e.sem_inc(self.handles(sem), n)
        self.here[sem] = self.here.get(sem, 0) + n


def program(nc, A, known):
    seen = Counts()
    handles = {}
    ctx = ExitStack()
    with ctx:
        def sem(name):
            if name not in handles:
                handles[name] = ctx.enter_context(nc.semaphore(name))
            return handles[name]

        def sb(name, shape, dt=F32, stack=ctx):
            return stack.enter_context(nc.sbuf_tensor(name, shape, dt))

        x = sb("x", [P, TILES, D_MODEL])
        hl1 = sb("hl1", [P, KC, 2, TOK], F32R)
        xs = sb("xs", [P, KC, 2, DEC], F32R)
        whi = sb("whi", [P, 2, UNIT], F32R)
        wlo = sb("wlo", [P, 2, UNIT], F32R)
        raw = sb("raw", [P, 2, UNIT])
        nsmall = P + 2 * TILES * 64 + 2 * TILES * 8 + TILES * 4 + 4 * DEC + 4 + 4
        small = sb("small", [P, nsmall])
        at = 0

        def take(n):
            nonlocal at
            at += n
            return small[:, at - n:at]

        ident = take(P)
        rcos = take(TILES * 64).rearrange("p (m d) -> p m d", m=TILES)
        rsin = take(TILES * 64).rearrange("p (m d) -> p m d", m=TILES)
        dcos = take(TILES * 8).rearrange("p (m d) -> p m d", m=TILES)
        dsin = take(TILES * 8).rearrange("p (m d) -> p m d", m=TILES)
        zeta = take(TILES * 4).rearrange("p (m h) -> p m h", m=TILES)
        xi = take(4 * DEC).rearrange("p (h i) -> p h i", h=4)
        g32 = take(4)
        lamc = take(4)
        vecs = sb("vecs", [P, DEPTH, NVEC])
        conv = sb("conv", [P, DEPTH, 6, 2 * FT])
        qkg = sb("qkg", [P, DEPTH, 2, DIFF_HD])
        lam = sb("lam", [P, DEPTH])
        sgn = sb("sgn", [2 * DEC, DEPTH])
        gd = sb("gd", [P, DEPTH])
        mhalf = sb("mhalf", [P, 60])
        ss = sb("ss", [P, 60])
        ms = sb("ms", [P, 60])
        rstd = sb("rstd", [P, 60])
        ssr = sb("ssr", [P, TILES, RET_HEADS])
        rest = sb("rest", [DEC, 512])
        odif = sb("odif", [P, TILES, D_MODEL])
        sTs_x = sb("sTs", [DEC, DEC])
        qx = sb("qx", [P, DEC])

        mix = ExitStack()
        mer = sb("mer", [P, KC, TOK], F32, mix)
        with ExitStack() as s:
            qz = sb("qz", [P, 2, 2 * TOK], F32, s)
            kdT = sb("kdT", [P, 2, TOK], F32, s)
            vd = sb("vd", [P, TILES, UC], F32, s)
            rawq = sb("rawq", [P, TILES, UC], F32, s)
            rawk = sb("rawk", [P, TILES, UC], F32, s)
            prob = sb("prob", [P, 2, 1024], F32, s)
            aT = sb("aT", [P, 2, SEQ], F32, s)
            rt = sb("rt", [P, 2, TILES * 4 * 8], F32, s)
            kc_n = sb("kc_n", [P, NT, HW], F32, s)
            vc_n = sb("vc_n", [P, NT, HW], F32, s)
            kcT = sb("kcT", [P, SEQ], F32, s)
            aTs = sb("aTs", [P, TILES, DEC], F32, s)
            aTt = sb("aTt", [P, TILES, DEC], F32, s)
            nmax = sb("nmax", [P, 2, 2], F32, s)
            sums = sb("sums", [P, 2, 2], F32, s)
            rinv = sb("rinv", [P, 4, 3], F32, s)
        with ExitStack() as s:
            tb = sb("tb", [P, KC, TOK], F32, s)
            with ExitStack() as s2:
                decay = sb("decay", [P, 2, SEQ], F32, s2)
                rk = sb("rk", [P, TILES, UC], F32, s2)
                gs = sb("gs", [P, TILES, UC], F32, s2)
                oret = sb("oret", [P, KC, TILES, P], F32, s2)
                sin = sb("sin", [P, RET_DV], F32, s2)
                sout = sb("sout", [P, 2, RET_DV], F32, s2)
            with ExitStack() as s2:
                squares_of_dif = sb("squares_of_dif", [P, TILES, 512], F32, s2)
            hl2 = sb("hl2", [P, KC, 2, TOK], F32R, s)
            xs2 = sb("xs2", [P, KC, 2, DEC], F32R, s)
        with ExitStack() as s:
            sT = sb("sT", [P, 1280], F32, s)
            vr = sb("vr", [P, TILES, UC], F32, s)
            qrT = sb("qrT", [P, TOK], F32, s)
            krT = sb("krT", [P, TOK], F32, s)
            kz = sb("kz", [P, TILES, RET_DK], F32, s)
        mix.close()
        with ExitStack() as s:
            xn = sb("xn", [P, TILES, D_MODEL], F32, s)
        with ExitStack() as s:
            act = sb("act", [P, FB, 2, GP], F32R, s)
            acts = sb("acts", [P, FB, 2, DEC], F32R, s)
            up = sb("up", [P, 2, 2, GP + 2], F32, s)
            ca = sb("ca", [P, 2, GP], F32, s)
            th = sb("th", [P, GP], F32, s)
            af = sb("af", [P, GP], F32, s)
            cs = sb("cs", [P, 4, 2 * FB], F32, s)
            csT = sb("csT", [2 * FB, 4, P], F32, s)

        ps = ctx.enter_context(nc.psum_tensor("ps", [P, 4096], F32))
        BANK = dict(mm0=0, mm1=512, s0=1024, s0b=1536, s1=2048, s1b=2560, t=3072, o=3584)
        UP_BANKS = (("mm0", "mm1", "t", "o"), ("s0", "s1", "s0b", "s1b"))
        NORM_BANKS = ("mm0", "t", "s0", "s1")
        DOWN_BANKS = ("mm0", "mm1", "s0", "s0b", "s1")

        def pv(bank, rows, n, off=0):
            return ps[0:rows, BANK[bank] + off:BANK[bank] + off + n]

        W = dict(A)

        def cols(name, l, col):
            return [(0, UC, W[name][ds(l, 1), :, ds(col, UC)])]

        def units(phase, l, i):
            if phase == "D":
                return [cols("w_in", l, i * UC + COL[n]) for n in ("qd", "kd", "vd", "ga")]
            if phase == "R":
                out = []
                for hh in range(2):
                    q = [(0, P, W["w_in"][ds(l, 1), :, ds(i * 2 * P + hh * P + COL["qr"], P)]),
                         (P, P, W["w_in"][ds(l, 1), :, ds(i * 2 * P + hh * P + COL["kr"], P)])]
                    out += [q, cols("w_in", l, i * 2 * UC + hh * UC + COL["vr"]),
                            cols("w_in", l, i * 2 * UC + hh * UC + COL["gr"])]
                return out
            if phase == "M":
                return ([cols("w_in", l, COL["gb"] + u * UC) for u in range(4)]
                        + [cols(n, l, u * UC) for n in ("w_branch_a", "w_branch_b", "w_out") for u in range(4)])
            if phase == "F":
                out = []
                for j in range(FB):
                    out.append([(0, P, W["w_up"][ds(l, 1), :, ds(i * FB * P + j * P, P)]),
                                (P, P, W["w_up"][ds(l, 1), :, ds(i * FB * P + j * P + D_FF, P)])])
                for hf in range(2):
                    k0 = 0
                    for nk in DOWN[hf]:
                        out.append((nk, W["w_down"][ds(l, 1), ds(i * FB * P + k0 * P, nk * P), hf * 512:hf * 512 + 512]))
                        k0 += nk
                return out
            return []

        UNITS = dict(N=0, D=4, R=6, M=16, F=FB + 7)
        LEN = dict(D=[UNIT] * 4, R=[UNIT] * 6, M=[UNIT] * 16,
                   F=[UNIT] * FB + [nk * 512 for half in DOWN for nk in half])

        def prep_len(phase, j):
            return LEN[phase][j] if j < UNITS.get(phase, 0) else UNIT

        def cache_load(S, e, l, i, hh, name):
            src = A[f"cache_{name}"][ds(l, 1), 0, :, ds(i * 2 + hh, 1), :].rearrange("a (c p) h d -> p (a c h) d", p=P)
            e.dma_start({"k": kc_n, "v": vc_n}[name][:, :, :], src).then_inc(*S.up(f"cache_{name}{hh}", "in", n=16))

        def kv_store(S, e, l, i, name, buf):
            dst = A[f"new_{name}_prompt"][ds(l, 1), 0, :, ds(i * 2, 2), :].rearrange("a (c p) h d -> p (a c) h d", p=P)
            e.dma_start(dst, buf[:, 0:NT, :].rearrange("p c (h d) -> p c h d", h=2)).then_inc(*S.up("kv_out", (name, 0), n=16))
            dst = A[f"new_{name}_sample"][ds(l, 1), 0, :, ds(i * 2, 2), :].rearrange("a s h d -> s a h d")
            e.dma_start(dst, buf[0:DEC, NT:TILES, :].rearrange("p c (h d) -> p c h d", h=2)).then_inc(*S.up("kv_out", (name, 4), n=16))

        def sync_program(S):
            e = S.e

            def load_unit(j, what):
                e.wait_ge(*S.at("w_ready", k=j - 2))
                slot = f"raw{j % 2}"
                if isinstance(what, tuple):
                    nk, src = what
                    v = src.rearrange("a (c p) n -> p (a c) n", p=P)
                    r = raw[:, j % 2, 0:nk * 512].rearrange("p (c n) -> p c n", c=nk)
                    cut = [(0, nk - 1), (nk - 1, nk)]
                    for a, b in cut:
                        e.dma_start(r[:, a:b, :], v[:, a:b, :]).then_inc(*S.up(slot, n=16))
                    return
                r = raw[:, j % 2, :].rearrange("p (c n) -> p c n", c=KC)
                if len(what) == 2:
                    for c0, n, src in what:
                        e.dma_start(r[:, :, c0:c0 + n], src.rearrange("a (c p) n -> p (a c) n", p=P)).then_inc(*S.up(slot, n=16))
                else:
                    v = what[0][2].rearrange("a (c p) n -> p (a c) n", p=P)
                    for a in (0, KC // 2):
                        e.dma_start(r[:, a:a + KC // 2, :], v[:, a:a + KC // 2, :]).then_inc(*S.up(slot, n=16))

            e.dma_start(small[:, :], A["tab_small"]).then_inc(*S.up("tables", "small", n=16))
            for m in range(NT):
                e.dma_start(x[:, m, :], A["x_prompt"][0, m * P:(m + 1) * P, :]).then_inc(*S.up("x_in", n=16))
            e.dma_start(x[0:DEC, NT, :], A["x_sample"][0]).then_inc(*S.up("x_in", "x", n=16))
            pr = th
            for l in range(DEPTH):
                o = l * NVEC
                for r0, n, name in ((0, KC, "norm1_g"), (KC, KC, "norm2_g"), (2 * KC, 2, "ret_norm_g"), (18, 1, "diff_norm_g")):
                    e.dma_start(pr[o + r0:o + r0 + n, 0:P], A[name][l].rearrange("(c p) -> c p", p=P)).then_inc(*S.up("params", n=16))
                for v, src in enumerate([A["state_conv"][l, 0, 0], A["state_conv"][l, 0, 1], A["conv_w"][l, 0],
                                         A["conv_w"][l, 1], A["conv_w"][l, 2], A["conv_b"][l]]):
                    e.dma_start(xn[0:2 * FT, l, v * P:(v + 1) * P], src.rearrange("(c p) -> c p", p=P)).then_inc(*S.up("params", n=16))
                for v, name in enumerate(("q_norm_g", "k_norm_g")):
                    e.dma_start(qkg[:, l, v, :], A[name][l].partition_broadcast(P)).then_inc(*S.up("params", n=16))
                for v, name in enumerate(("lambda_q1", "lambda_q2", "lambda_k1", "lambda_k2")):
                    e.dma_start(prob[:, l, v * DIFF_HD:(v + 1) * DIFF_HD], A[name][l].partition_broadcast(P)).then_inc(*S.up("params", n=16))
            S.note("params", "all")
            with S.layers() as l:
                for phase, _ in ORDER:
                    with S.body(phase) as i:
                        us = units(phase, l, i)
                        assert len(us) == UNITS[phase]
                        if phase == "D":
                            for j, what in enumerate(us):
                                load_unit(j, what)
                                if j == 1:
                                    e.wait_ge(*S.at("o_ready", k=0))
                                    e.wait_ge(*S.at("t_ready", k=0))
                                    e.wait_ge(*S.at("pool_step", k=0))
                                    e.wait_ge(*S.at("act_free_o", k=0))
                                    cache_load(S, e, l, i, 0, "k")
                                    cache_load(S, e, l, i, 0, "v")
                        elif phase == "R":
                            for j, what in enumerate(us):
                                load_unit(j, what)
                                if j == 1:
                                    e.wait_ge(*S.at("pe_step", k=0))
                                    e.wait_ge(*S.at("dve_step", k=0))
                                    e.wait_ge(*S.at("act_step", k=0))
                                    e.wait_ge(*S.at("act_free_t", k=0))
                                    e.wait_ge(*S.at("dve_free_t", k=0))
                                    e.wait_ge(*S.at("dve_free_o", k=0))
                                    e.wait_ge(*S.at("act_free_o", k=0))
                                    e.dma_start(decay[:, :, :].rearrange("p h n -> p (h n)"),
                                                         A["tab_decay"][:, ds(i * 2 * SEQ, 2 * SEQ)]).then_inc(*S.up("decay_in", "d", n=16))
                                if j in (1, 4):
                                    hh = j // 3
                                    e.wait_ge(*(S.at("dve_free_s1", ("snew", 0)) if hh else S.at("dve_free_s1", k=0)))
                                    e.dma_start(sin[:, :], A["state_ret"][ds(l, 1), 0, ds(i * 2 + hh, 1)]
                                             .rearrange("a h d e -> d (a h e)")).then_inc(*S.up("sin_in", ("s", hh), n=16))
                        else:
                            for j, what in enumerate(us):
                                load_unit(j, what)
            e.wait_ge(*S.at("w_ready", k=-2))
            for a in (0, KC // 2):
                e.dma_start(raw[:, 0, a * UC:(a + KC // 2) * UC].rearrange("p (c n) -> p c n", c=KC // 2),
                                     A["w_in"][0, a * P:(a + KC // 2) * P, 0:UC].rearrange("(c p) n -> p c n", p=P)).then_inc(*S.up("raw0", n=16))
            e.wait_ge(*S.at("dve_step", k=0))
            for m in range(TILES):
                dst = A["y_prompt"][0, m * P:(m + 1) * P, :] if m < NT else A["y_sample"][0]
                e.dma_start(dst, x[0:ROWS[m], m, :]).then_inc(*S.up("y_out", "y%d" % m, n=16))
            e.wait_ge(*S.at("y_out", k=TILES * 16))
            e.wait_ge(*S.at("kv_out", k=0))
            e.wait_ge(*S.at("st_out0", k=0))
            e.wait_ge(*S.at("st_out1", k=0))
            e.wait_ge(*S.at("cs_out", k=0))
            e.wait_ge(*S.at("w_ready", k=0))

        def pool_program(S):
            e = S.e

            def lo(phase, j):
                n = prep_len(phase, j)
                s = j % 2
                e.wait_ge(*S.at("hi_ready", k=j)) if phase != "P" else e.wait_ge(*S.at("hi_ready", ("hi", 0)))
                e.tensor_tensor(wlo[:, s, 0:n], raw[:, s, 0:n], whi[:, s, 0:n].bitcast(F32), ALU.subtract).then_inc(*S.up("w_ready", ("lo", j)))

            def power(n, key, at=0):
                e.wait_ge(*S.at("dve_step", ("ms", key)))
                e.tensor_tensor(rstd[:, at:at + n], ms[:, at:at + n], mhalf[:, at:at + n], ALU.pow).then_inc(
                    *S.up("pool_step", ("rstd", key)))

            S.prime("w_ready", 2)
            S.prime("pool_step", 1)
            e.memset(mhalf[:, :], -0.5).then_inc(*S.up("pool_step"))
            lo("P", 0)
            with S.layers() as l:
                with S.body("N"):
                    power(5, "n")
                with S.body("D") as p:
                    lo("D", 1)
                    lo("D", 2)
                    power(20, "q")
                    lo("D", 3)
                    power(20, "k")
                    lo("D", 4)
                with S.body("R") as i:
                    for hh in range(2):
                        for j in range(3 * hh + 1, 3 * hh + 4):
                            lo("R", j)
                with S.body("M"):
                    lo("M", 1)
                    power(20, "ret", 40)
                    lo("M", 2)
                    power(20, "dif0", 0)
                    power(20, "dif1", 20)
                    for j in range(3, 17):
                        lo("M", j)
                        if j == 16:
                            power(5, "n")
                with S.body("F") as f:
                    for j in range(FB):
                        lo("F", j + 1)
                    for j in range(FB, UNITS["F"]):
                        lo("F", j + 1)

        def pe_program(S):
            e = S.e
            free = {}

            def acquire(bank, act=0, dve=0):
                if bank not in free:
                    free[bank] = {"act": 0, "dve": 0, "last": ("act", "dve")}
                b = free[bank]
                for who in b["last"]:
                    e.wait_ge(*S.at(f"{who}_free_{bank}", k=b[who]))
                b["last"] = tuple(w for w, n in (("act", act), ("dve", dve)) if n)
                b["act"] += act
                b["dve"] += dve

            def start():
                free.clear()

            tile = [0]

            def mm_bank():
                tile[0] += 1
                return f"mm{(tile[0] - 1) % 2}"

            def ready(ins, *keys):
                ins.then_inc(*S.up("mm_ready", keys[0]))
                for k in keys[1:]:
                    S.note("mm_ready", k)

            def chunk_ready(c):
                e.wait_ge(*S.at(f"dve_free_{NORM_BANKS[c % 4]}", k=0 if c >= 4 else -1))

            def t_tile(j, col, half, X, act=0, dve=0, bank=None, chunk=None):
                bank = bank or mm_bank()
                acquire(bank, act, dve)
                out = pv(bank, P, HALF)
                for c in range(KC):
                    w0 = c * UC + col * P
                    hi, lo = (X[:, c, v, half * HALF:(half + 1) * HALF] for v in (0, 1))
                    wh, wl = whi[:, j % 2, w0:w0 + P], wlo[:, j % 2, w0:w0 + P]
                    if chunk:
                        chunk(c)
                    e.matmul(out, wh, hi, start=(c == 0), stop=False)
                    e.matmul(out, wh, lo, start=False, stop=False)
                    ins = e.matmul(out, wl, hi, start=False, stop=(c == KC - 1))
                keys = [("T", j, col, half)] + ([("end", j)] if col and half else [])
                ready(ins, *keys)

            def n_tile(j, m, X, XS, act=0, dve=0, chunk=None):
                bank = mm_bank()
                acquire(bank, act, dve)
                if m < NT:
                    out = pv(bank, P, UC)
                    for c in range(KC):
                        hi, lo = (X[:, c, v, m * P:(m + 1) * P] for v in (0, 1))
                        wh, wl = (w[:, j % 2, c * UC:(c + 1) * UC] for w in (whi, wlo))
                        if chunk:
                            chunk(c)
                        e.matmul(out, hi, wh, start=(c == 0), stop=False)
                        e.matmul(out, hi, wl, start=False, stop=False)
                        ins = e.matmul(out, lo, wh, start=False, stop=(c == KC - 1))
                    ready(ins, ("N", j, m))
                else:
                    out = pv(bank, 2 * DEC, UC)
                    for c in range(KC):
                        st = XS[:, c, :, :].rearrange("p v s -> p (v s)")
                        e.matmul(out, st, whi[:, j % 2, c * UC:(c + 1) * UC], start=(c == 0), stop=False)
                        ins = e.matmul(out, st, wlo[:, j % 2, c * UC:(c + 1) * UC], start=False, stop=(c == KC - 1))
                    ready(ins, ("N", j, m), ("end", j))

            def n_unit(j, X, XS, dve=False, before=None, after=None, chunk=None):
                e.wait_ge(*S.at("w_ready", k=j))
                for m in range(TILES):
                    if before:
                        before(m)
                    if m == NT:
                        n_tile(j, m, X, XS, act=1, dve=1)
                    else:
                        n_tile(j, m, X, XS, act=int(not dve), dve=int(dve), chunk=chunk if m == 0 else None)
                    if after:
                        after(m)

            def feature_transposes(src, bank, key, act, dve):
                acquire(bank, act, dve)
                for m in range(TILES):
                    ins = e.transpose(pv(bank, P, ROWS[m], m * P), src(m), ident[0:ROWS[m], 0:ROWS[m]])
                ins.then_inc(*S.up("s_ready", key))

            def norm(key):
                acquire("mm1")
                acquire("o")
                acquire("s0b")
                acquire("s1b")
                for c in range(KC):
                    if c == 0:
                        e.wait_ge(*S.at("act_step", ("xn", key)))
                        e.wait_ge(*S.at("dve_step", ("xn", key)))
                    feature_transposes(lambda m: xn[0:ROWS[m], m, c * P:(c + 1) * P], NORM_BANKS[c % 4], ("norm", c), 1, 1)

            S.prime("mm_ready", 1)
            S.prime("pe_step", 1)
            S.prime("o_ready", 1)
            S.prime("t_ready", 1)
            S.prime("s_ready", 1)
            e.wait_ge(*S.at("tables", "small"))
            e.wait_ge(*S.at("params", "all"))
            n = DEPTH * NVEC
            e.transpose(pv("t", P, n), th[0:n, 0:P], ident[0:n, 0:n])
            for l in range(DEPTH):
                for v in range(6):
                    o = (l * 6 + v) * 2 * FT
                    ins = e.transpose(ps[:, BANK[f"s{l}"] + v * 2 * FT:BANK[f"s{l}"] + (v + 1) * 2 * FT],
                                      xn[0:2 * FT, l, v * P:(v + 1) * P], ident[0:2 * FT, 0:2 * FT])
            ins.then_inc(*S.up("pe_step", "params"))
            with S.layers():
                with S.body("N"):
                    start()
                    norm("n")
                with S.body("D"):
                    start()
                    tile[0] = 0
                    n_unit(0, hl1, xs, before=lambda m: e.wait_ge(*S.at("act_step", k=0)) if m == NT else None, chunk=chunk_ready)

                    def cached_keys(hh):
                        e.wait_ge(*S.at(f"cache_k{hh}", "in"))
                        acquire("t", act=1)
                        for c in range(NT):
                            ins = e.transpose(pv("t", P, P, c * P), kc_n[:, c, :], ident)
                        ins.then_inc(*S.up("t_ready", ("kc", hh)))

                    n_unit(1, hl1, xs)

                    def queries(m):
                        if m == 1:
                            e.wait_ge(*S.at("dve_step", ("rope", "q")))
                            for hh in range(2):
                                feature_transposes(lambda m: rawq[0:ROWS[m], m, hh * P:(hh + 1) * P], f"s{hh}", ("q", hh), 1, 2)

                    n_unit(2, hl1, xs, after=queries)
                    cached_keys(0)
                    e.wait_ge(*S.at("w_ready", k=3))
                    t_tile(3, 0, 0, hl1, act=1)
                    for hh in range(2):
                        if hh == 0:
                            e.wait_ge(*S.at("dve_step", ("rope", "k")))
                        feature_transposes(lambda m: rawk[0:ROWS[m], m, hh * P:(hh + 1) * P], f"s{hh}", ("k", hh), 1, 0)
                    steps = [(hh, ib) for hh in range(2) for ib in range(TILES)]

                    def scores(n):
                        hh, ib = steps[n]
                        bank = f"s{n % 2}"
                        if ib < NT:
                            acquire(bank, act=1)
                            if n == 0:
                                e.wait_ge(*S.at("act_free_s0", ("q", 0)))
                                e.wait_ge(*S.at("dve_free_s0", ("q1", 0)))
                                e.wait_ge(*S.at("act_free_s0", ("k", 0)))
                            if n == 5:
                                e.wait_ge(*S.at("dve_free_s1", ("q1", 1)))
                                e.wait_ge(*S.at("act_free_s1", ("k", 1)))
                            keys = (ib + 1) * P
                            for c in range(2):
                                o = c * (TOK + DEC) + ib * P
                                ins = e.matmul(pv(bank, P, keys, c * 512), qz[:, hh, o:o + P], kdT[:, hh, 0:keys],
                                               start=True, stop=True)
                        else:
                            acquire(bank, act=1)
                            e.wait_ge(*S.at("act_free_t", ("kc", hh)))
                            st = qz[:, hh, SEQ:SEQ + 2 * DEC]
                            e.matmul(pv(bank, 2 * DEC, PAST), st, kcT[:, :], start=True, stop=True)
                            ins = e.matmul(pv(bank, 2 * DEC, DEC, PAST), st, kdT[:, hh, SEQ:TOK], start=True, stop=True)
                        ins.then_inc(*S.up("s_ready", ("s", n)))

                    def weighted(n):
                        hh, ib = steps[n]
                        e.wait_ge(*S.at("dve_step", ("a", n)))
                        if ib < NT:
                            acquire("t", act=1)
                            for jb in range(ib + 1):
                                ins = e.transpose(pv("t", P, P, jb * P), prob[:, n % 2, jb * P:(jb + 1) * P], ident)
                            ins.then_inc(*S.up("t_ready", ("a", n)))
                        else:
                            acquire("t", act=2, dve=2)
                            S.settle()
                            for c in range(TILES):
                                ins = e.transpose(pv("t", ROWS[c], 2 * DEC, c * 2 * DEC),
                                                  prob[0:2 * DEC, n % 2, c * P:c * P + ROWS[c]], ident[0:2 * DEC, 0:2 * DEC])
                            ins.then_inc(*S.up("t_ready", ("a", n)))

                    def values(n):
                        hh, ib = steps[n]
                        acquire("o", act=1)
                        if ib < NT:
                            e.wait_ge(*S.at("act_free_t", ("aT", n)))
                            if n == 0:
                                e.wait_ge(*S.at("act_free_mm1", ("v", 3)))
                                e.wait_ge(*S.at("act_free_mm0", ("v", 2)))
                            for jb in range(ib + 1):
                                ins = e.matmul(pv("o", P, HW), aT[:, n % 2, jb * P:(jb + 1) * P],
                                               vd[:, jb, hh * HW:(hh + 1) * HW], start=(jb == 0), stop=(jb == ib))
                        else:
                            e.wait_ge(*S.at("dve_free_t", ("aT", n)))
                            e.wait_ge(*S.at("dve_step", ("rest", "v")))
                            e.wait_ge(*S.at(f"cache_v{hh}", "in"))
                            for c in range(TILES):
                                r = ROWS[c]
                                v = vc_n[:, c, :] if c < NT else vd[0:DEC, NT, hh * HW:(hh + 1) * HW]
                                ins = e.matmul(pv("o", DEC, HW), aTs[0:r, c, :], v, start=(c == 0), stop=(c == NT))
                        ins.then_inc(*S.up("o_ready", (hh, ib)))

                    def gate_tile(t):
                        t_tile(3, t // 2, t % 2, hl1, act=1)

                    scores(0)
                    scores(1)
                    for n in range(10):
                        if n + 2 < 10:
                            scores(n + 2)
                        if n in GATE_AT[0:2]:
                            gate_tile(GATE_AT.index(n) + 1)
                        weighted(n)
                        if n == GATE_AT[2]:
                            gate_tile(3)
                        if n:
                            values(n - 1)
                        if n == 5:
                            cached_keys(1)
                    values(9)
                with S.body("R"):
                    start()
                    tile[0] = 0
                    for hh in range(2):
                        u = 3 * hh
                        n_unit(u, hl1, xs)
                        n_unit(u + 1, hl1, xs)
                        e.wait_ge(*S.at("dve_step", ("rope", hh)))
                        for v in range(2):
                            feature_transposes(lambda m: rk[0:ROWS[m], m, v * P:(v + 1) * P], f"s{v}", ("qk", hh, v), 1, 0)
                        e.wait_ge(*S.at("w_ready", k=u + 2))

                        def rscores(jb):
                            n = SEQ - jb * P
                            if jb == 0:
                                e.wait_ge(*S.at("act_free_s0", ("qk", hh, 0)))
                                e.wait_ge(*S.at("act_free_s1", ("qk", hh, 1)))
                                acquire("s0", dve=2)
                            if jb == 2:
                                acquire("s1", dve=2)
                            bank = "s0" if jb < 2 else "s1"
                            e.matmul(pv(bank, P, n, (jb % 2) * 512), krT[:, jb * P:(jb + 1) * P], qrT[:, jb * P:SEQ],
                                              start=True, stop=True).then_inc(*S.up("s_ready", ("ret", hh, jb)))

                        def outs(ib):
                            bank = "to"[ib % 2]
                            acquire(bank, act=1, dve=1)
                            e.wait_ge(*S.at(("dve_free_s0", "dve_free_s1")[ib // 2], ("sT", hh, ib)))
                            for jb in range(ib + 1):
                                o = SOFF[jb] + (ib - jb) * P
                                ins = e.matmul(pv(bank, P, RET_DV), sT[:, o:o + P], vr[:, jb, :], start=(jb == 0), stop=(jb == ib))
                            ins.then_inc(*S.up(("t_ready", "o_ready")[ib % 2], ("o", hh, ib)))

                        j = u + 2
                        n_tile(j, 0, hl1, xs, dve=1, act=1)
                        rscores(0)
                        rscores(1)
                        n_tile(j, 1, hl1, xs, dve=1, act=1)
                        rscores(2)
                        rscores(3)
                        n_tile(j, 2, hl1, xs, dve=1, act=1)
                        outs(0)
                        outs(1)
                        acquire("s0", dve=1)
                        S.settle()
                        e.matmul(pv("s0", DEC, DEC), krT[:, SEQ:TOK], qrT[:, SEQ:TOK], start=True, stop=True).then_inc(*S.up("s_ready", ("rets", hh)))
                        n_tile(j, 3, hl1, xs, dve=1, act=1)
                        outs(2)
                        outs(3)
                        n_tile(j, 4, hl1, xs, act=1, dve=2)
                        acquire("t", act=1, dve=1)
                        e.wait_ge(*S.at("dve_step", ("qx", hh)))
                        e.wait_ge(*S.at("sin_in", ("s", hh)))
                        S.settle()
                        e.matmul(pv("t", DEC, RET_DV), sTs_x[:, :], vr[0:DEC, NT, :], start=True, stop=False)
                        e.matmul(pv("t", DEC, RET_DV), qx[:, :], sin[:, :], start=False, stop=True).then_inc(*S.up("t_ready", ("os", hh)))
                        acquire("o", act=1)
                        e.wait_ge(*S.at("dve_step", ("kz", hh)))
                        for m in range(NT):
                            ins = e.matmul(pv("o", P, RET_DV), kz[:, m, :], vr[:, m, :], start=(m == 0), stop=(m == NT - 1))
                        ins.then_inc(*S.up("o_ready", ("sfin", hh)))
                        acquire("s1", dve=1)
                        e.matmul(pv("s1", P, RET_DV), kz[0:DEC, NT, :], vr[0:DEC, NT, :], start=True, stop=True).then_inc(*S.up("s_ready", ("snew", hh)))
                with S.body("M"):
                    start()
                    tile[0] = 0

                    def t_unit(j, X, act=0, dve=0, before=None):
                        e.wait_ge(*S.at("w_ready", k=j))
                        for t in range(4):
                            if before:
                                before(t)
                            t_tile(j, t // 2, t % 2, X, act, dve)

                    def ret_chunk(c):
                        if c == 0:
                            e.wait_ge(*S.at("dve_step", ("oret", "done")))
                        feature_transposes(lambda m: oret[0:ROWS[m], c, m, :], f"s{c % 2}", ("ret", c), 1, 1)

                    for j in range(4):
                        t_unit(j, hl1, act=1, before=(lambda t, j=j: ret_chunk(4 * (j - 2) + t)) if j >= 2 else None)
                    e.wait_ge(*S.at("dve_free_s0", ("lo", "ret", KC - 2)))
                    e.wait_ge(*S.at("dve_free_s1", ("lo", "ret", KC - 1)))

                    def dif_chunk(c):
                        if c in (0, 4):
                            e.wait_ge(*S.at("dve_step", ("odif", c // 4)))
                        feature_transposes(lambda m: odif[0:ROWS[m], m, c * P:(c + 1) * P], f"s{c % 2}", ("dif", c), 1, 1)

                    for u in range(4):
                        t_unit(4 + u, hl2, dve=1, before=lambda t, u=u: None if t % 2 else dif_chunk(2 * u + t // 2))
                    e.wait_ge(*S.at("dve_free_s1", ("lo", "dif", KC - 1)))
                    e.wait_ge(*S.at("dve_free_s0", ("lo", "dif", KC - 2)))
                    for u in range(4):
                        t_unit(8 + u, hl1, dve=1)

                    def merged(m):
                        if m == 0:
                            e.wait_ge(*S.at("dve_step", ("lo", "mer", 2)))
                        if m == 2:
                            e.wait_ge(*S.at("dve_step", ("lo", "mer", 3)))
                        if m == NT:
                            e.wait_ge(*S.at("act_step", ("xs", "mer")))

                    for u in range(4):
                        n_unit(12 + u, hl2, xs2, dve=True, before=merged if u == 0 else None)
                    norm("n")
                with S.body("F"):
                    start()
                    tile[0] = 0
                    for j in range(FB):
                        e.wait_ge(*S.at("w_ready", k=j))
                        for t in range(4):
                            reads = 2 if t % 2 else 1
                            t_tile(j, t // 2, t % 2, hl1, act=reads * (t < 2), dve=reads * (t >= 2), bank=UP_BANKS[j % 2][t],
                                   chunk=chunk_ready if j == 0 and t == 0 else None)

                    def conv_rows():
                        acquire("t", dve=1)
                        e.wait_ge(*S.at("dve_step", ("cs", FB - 1)))
                        for q in range(4):
                            ins = e.transpose(pv("t", 2 * FB, P, q * P), cs[:, q, :], ident)
                        ins.then_inc(*S.up("t_ready", "cs"))

                    j = FB
                    for hf in range(2):
                        for m, bank in enumerate(DOWN_BANKS):
                            acquire(bank, act=int(m == NT), dve=1)
                        acquire("s1b")
                        kc = 0
                        for n, nk in enumerate(DOWN[hf]):
                            e.wait_ge(*S.at("w_ready", k=j))
                            if hf == 0:
                                e.wait_ge(*S.at("act_step", ("acts", n)))
                                e.wait_ge(*S.at("dve_step", ("alo", kc + nk - 1)))
                            for q in range(nk):
                                last = kc == FB - 1
                                wh, wl = (w[:, j % 2, q * 512:(q + 1) * 512] for w in (whi, wlo))
                                for m in range(NT):
                                    out = ps[:, m * 512:(m + 1) * 512]
                                    hi, lo = (act[:, kc, v, m * P:(m + 1) * P] for v in (0, 1))
                                    e.matmul(out, hi, wh, start=(kc == 0), stop=False)
                                    e.matmul(out, hi, wl, start=False, stop=False)
                                    ins = e.matmul(out, lo, wh, start=False, stop=last)
                                    if last:
                                        ready(ins, ("down", hf, m))
                                st = acts[:, kc, :, :].rearrange("p v s -> p (v s)")
                                out = ps[0:2 * DEC, 2048:2560]
                                e.matmul(out, st, wh, start=(kc == 0), stop=False)
                                ins = e.matmul(out, st, wl, start=False, stop=last)
                                if last:
                                    ready(ins, ("down", hf, NT), ("end", j))
                                elif q == nk - 1:
                                    ready(ins, ("end", j))
                                kc += 1
                            j += 1
                        if hf == 0:
                            conv_rows()

        SOFF = [0, 512, 896, 1152]
        GATE_AT = (0, 7, 9)

        def act_program(S):
            e = S.e


            def hi(phase, j, part):
                n = prep_len(phase, j)
                s = j % 2
                if part == 0:
                    if phase != "P":
                        if j >= 2:
                            e.wait_ge(*S.at("mm_ready", ("end", j - 2)))
                        else:
                            e.wait_ge(*S.at("mm_ready", k=0))
                    e.wait_ge(*S.at(f"raw{s}", k=32 * (j // 2 + 1) if phase != "P" else 32))
                a, b = (0, n // 2) if part == 0 else (n // 2, n)
                if part == 0:
                    e.activation(whi[:, s, a:b], raw[:, s, a:b], ACT.Copy)
                else:
                    e.activation(whi[:, s, a:b], raw[:, s, a:b], ACT.Copy).then_inc(*S.up("hi_ready", ("hi", j)))

            def prep(phase, j):
                hi(phase, j, 0)
                hi(phase, j, 1)

            def wait_rest(prev):
                if prev is None:
                    e.wait_ge(*S.at("dve_step", k=0))
                else:
                    e.wait_ge(*S.at("dve_step", prev))

            def rest_copy(bank, key, prev, n=UC):
                e.wait_ge(*S.at("mm_ready", key))
                wait_rest(prev)
                e.wait_ge(*S.own())
                e.activation(rest[:, 0:n], ps[DEC:2 * DEC, BANK[bank]:BANK[bank] + n], ACT.Copy).then_inc(*S.up(f"act_free_{bank}", ("rest",) + key))

            def squares_of_x(m, c0, n, junk, at, key):
                r = ROWS[m]
                e.wait_ge(*S.own())
                e.activation(junk[0:r], x[0:r, m, c0:c0 + n], ACT.Square, accum_out=ss[0:r, at:at + 1]).then_inc(
                    *S.up("act_step", key=key))

            def norm(key):
                for m in (1, 3):
                    e.wait_ge(*S.at("pool_step", ("rstd", key)))
                    e.activation(xn[:, m, :], x[:, m, :], ACT.Copy, scale=rstd[:, m:m + 1]).then_inc(
                        *S.up("act_step", key=("xn", key) if m == 3 else None))
                for c in range(KC):
                    bank = NORM_BANKS[c % 4]
                    g = vecs[:, ds(S.layer, 1), (c if S.phase == "N" else KC + c):(c if S.phase == "N" else KC + c) + 1].rearrange(
                        "p a b -> p (a b)")
                    e.wait_ge(*S.at("s_ready", ("norm", c)))
                    if c == 0:
                        e.wait_ge(*(S.at("mm_ready", k=0) if S.phase == "N" else S.at("mm_ready", ("end", 15))))
                    e.wait_ge(*S.own())
                    S.settle()
                    e.activation(hl1[:, c, 0, :], pv(bank, P, TOK), ACT.Copy, scale=g).then_inc(*S.up(f"act_free_{bank}", ("norm", c)))
                for c in range(4, KC):
                    e.wait_ge(*S.at(f"dve_free_{NORM_BANKS[c % 4]}", ("norm", c)))
                e.wait_ge(*S.own())
                e.activation(xs[:, :, :, :].rearrange("p c v s -> p (c v) s"),
                             hl1[:, :, :, SEQ:TOK].rearrange("p c v s -> p (c v) s"), ACT.Copy).then_inc(*S.up("act_step", key=("xs", key)))

            for b in BANK:
                S.prime(f"act_free_{b}", 1)
            S.prime("act_step", 1)
            for s in ("kv_out", "st_out0", "st_out1", "cs_out"):
                S.prime(s, 16)
            S.prime("hi_ready", 1)
            e.wait_ge(*S.at("raw0", k=32))
            hi("P", 0, 0)
            hi("P", 0, 1)
            e.wait_ge(*S.at("x_in", "x"))
            e.wait_ge(*S.at("dve_step", "ones"))
            for m in range(TILES):
                for hf in range(2):
                    squares_of_x(m, hf * 512, 512, qz[:, 0, 0:512], 40 + 2 * m + hf, None)
            S.note("act_step", "ssq")
            e.wait_ge(*S.at("dve_step", "lamp"))
            e.activation(aT[:, 0, 0:2 * DEPTH], aT[:, 0, 8:8 + 2 * DEPTH], ACT.Exp).then_inc(*S.up("act_step", key="lexp"))
            with S.layers() as l:
                with S.body("N"):
                    norm("n")
                with S.body("D") as p:
                    prev = None
                    t = 0
                    for u, (name, buf) in enumerate((("q", rawq), ("k", rawk), ("v", vd))):
                        for m in range(TILES):
                            bank = f"mm{t % 2}"
                            t += 1
                            if m == 0:
                                e.wait_ge(*S.at("dve_step", k=0))
                                e.wait_ge(*S.at("dve_free_o", k=0))
                                e.wait_ge(*S.at("kv_out", k=0))
                                e.wait_ge(*S.at("o_ready", k=0))
                                hi("D", u + 1, 0)
                                hi("D", u + 1, 1)
                            if m < NT:
                                e.wait_ge(*S.at("mm_ready", ("N", u, m)))
                                e.activation(buf[:, m, :], pv(bank, P, UC), ACT.Copy).then_inc(*S.up(f"act_free_{bank}", (name, m)))
                            else:
                                rest_copy(bank, ("N", u, m), prev)
                                prev = ("rest", name)
                            if u == 1 and m == 0:
                                e.wait_ge(*S.at("dve_step", ("rest", "q")))
                                e.wait_ge(*S.own())
                                e.activation(prob[:, :, :].rearrange("p a b -> p (a b)")[:, 0:TILES * UC],
                                                rawq[:, :, :].rearrange("p a b -> p (a b)"), ACT.Square).then_inc(*S.up("act_step", key=("sq", "q")))
                            if u == 2 and m == 0:
                                e.wait_ge(*S.at("dve_step", ("rest", "k")))
                                e.wait_ge(*S.at("dve_step", ("ss", "q")))
                                e.wait_ge(*S.own())
                                e.activation(prob[:, :, :].rearrange("p a b -> p (a b)")[:, 0:TILES * UC],
                                                rawk[:, :, :].rearrange("p a b -> p (a b)"), ACT.Square).then_inc(*S.up("act_step", key=("sq", "k")))
                            if u == 2 and m == 2:
                                for hh in range(2):
                                    e.wait_ge(*S.at("s_ready", ("q", hh)))
                                    e.activation(qz[0:DIFF_HD, hh, 0:TOK], pv(f"s{hh}", DIFF_HD, TOK), ACT.Copy,
                                                 scale=DIFF_HD ** -0.5).then_inc(*S.up(f"act_free_s{hh}", ("q", hh)))
                    e.wait_ge(*S.at("t_ready", ("kc", 0)))
                    e.activation(kcT[:, :], pv("t", P, PAST), ACT.Copy).then_inc(*S.up("act_free_t", ("kc", 0)))
                    cache_load(S, e, l, p, 1, "k")
                    def gate(tt):
                        bank = f"mm{(15 + tt) % 2}"
                        e.wait_ge(*S.at("mm_ready", ("T", 3, tt // 2, tt % 2)))
                        e.wait_ge(*S.own())
                        S.settle()
                        e.activation(mer[:, ds(p * 2 + tt // 2, 1), (tt % 2) * HALF:(tt % 2 + 1) * HALF].rearrange("p a b -> p (a b)"),
                                        pv(bank, P, HALF), ACT.Tanh, scale=0.5).then_inc(*S.up(f"act_free_{bank}", ("ga", tt)))

                    steps = [(hh, ib) for hh in range(2) for ib in range(TILES)]

                    def exps(n):
                        hh, ib = steps[n]
                        b = n % 2
                        e.wait_ge(*S.at("dve_step", ("max", n)))
                        if n >= 2:
                            e.wait_ge(*S.at("t_ready", ("a", n - 2)))
                        e.wait_ge(*S.own())
                        if ib < NT:
                            k = (ib + 1) * P
                            for c in range(2):
                                src = pv(f"s{b}", P, k, c * 512)
                                dst = prob[:, b, c * 512:c * 512 + k]
                                i = e.activation(dst, src, ACT.Exp, bias=nmax[:, b, c:c + 1], accum_out=sums[:, b, c:c + 1])
                                if c == 0:
                                    i.then_inc(*S.up("act_step"))
                                else:
                                    i.then_inc(*S.up(f"act_free_s{b}", ("exp", n)))
                        else:
                            e.activation(prob[0:2 * DEC, b, 0:TOK], pv(f"s{b}", 2 * DEC, TOK), ACT.Exp,
                                            bias=nmax[0:2 * DEC, b, 0:1], accum_out=sums[0:2 * DEC, b, 0:1]).then_inc(*S.up(f"act_free_s{b}", ("exp", n)))

                    def turn(n):
                        hh, ib = steps[n]
                        e.wait_ge(*S.at("t_ready", ("a", n)))
                        if n >= 2:
                            e.wait_ge(*S.at("o_ready", steps[n - 2]))
                        e.wait_ge(*S.own())
                        if ib < NT:
                            e.activation(aT[:, n % 2, 0:(ib + 1) * P], pv("t", P, (ib + 1) * P), ACT.Copy).then_inc(*S.up("act_free_t", ("aT", n)))
                        else:
                            v = pv("t", P, TILES * 2 * DEC).rearrange("p (c n) -> p c n", c=TILES)
                            e.activation(aTt[:, 0:NT, :], v[:, 0:NT, DEC:2 * DEC], ACT.Copy).then_inc(*S.up("act_free_t"))
                            e.activation(aTt[0:DEC, NT, :], v[0:DEC, NT, DEC:2 * DEC], ACT.Copy).then_inc(*S.up("act_free_t", ("aTt", n)))

                    def out(n):
                        hh, ib = steps[n]
                        r = ROWS[ib]
                        e.wait_ge(*S.at("o_ready", (hh, ib)))
                        e.wait_ge(*S.own())
                        S.settle()
                        dst = odif[0:r, ib, ds(p * 2 * HW + hh * HW, HW)]
                        e.activation(dst, pv("o", r, HW), ACT.Copy, scale=rinv[0:r, n % 4, 0:1] if ib < NT else 1.0).then_inc(
                            *S.up("act_free_o", key=("o", n)))

                    hi("D", 4, 0)
                    hi("D", 4, 1)
                    gate(0)
                    for hh in range(2):
                        e.wait_ge(*S.at("s_ready", ("k", hh)))
                        e.activation(kdT[:, hh, :], pv(f"s{hh}", P, TOK), ACT.Copy).then_inc(*S.up(f"act_free_s{hh}", ("k", hh)))
                    exps(0)
                    e.wait_ge(*S.at("dve_step", ("rope", "k")))
                    kv_store(S, e, l, p, "k", rawk)
                    exps(1)
                    e.wait_ge(*S.at("dve_step", ("rest", "v")))
                    e.wait_ge(*S.own())
                    kv_store(S, e, l, p, "v", vd)
                    for n in range(10):
                        if n == 6:
                            e.wait_ge(*S.at("t_ready", ("kc", 1)))
                            e.wait_ge(*S.own())
                            e.activation(kcT[:, :], pv("t", P, PAST), ACT.Copy).then_inc(*S.up("act_free_t", ("kc", 1)))
                        if n in GATE_AT[0:2]:
                            gate(GATE_AT.index(n) + 1)
                        turn(n)
                        if n:
                            out(n - 1)
                        if n + 2 < 10:
                            exps(n + 2)
                        if n == 5:
                            e.wait_ge(*S.at("o_ready", (0, NT)))
                            cache_load(S, e, l, p, 1, "v")
                        if n == GATE_AT[2]:
                            gate(3)
                    out(9)
                with S.body("R") as i:
                    prev = None
                    t = 0
                    for hh in range(2):
                        for u, buf in ((0, rk), (1, vr), (2, gs)):
                            for m in range(TILES):
                                bank = f"mm{t % 2}"
                                t += 1
                                j = 3 * hh + u
                                if m == 0 and hh == 0 and u == 0:
                                    for s in ("dve_step", "s_ready", "o_ready", "t_ready", "dve_free_t", "dve_free_o", "dve_free_s0", "dve_free_s1", "kv_out"):
                                        e.wait_ge(*S.at(s, k=0))
                                if m == 0 and hh == 1 and u == 0:
                                    e.wait_ge(*S.at("dve_step", ("kz", 0)))
                                    e.wait_ge(*S.at("s_ready", ("qk", 0, 1)))
                                if m == 0 and hh == 1 and u == 1:
                                    e.wait_ge(*S.at("s_ready", ("snew", 0)))
                                if m == 0 and hh == 1 and u == 2:
                                    e.wait_ge(*S.at("dve_free_t", ("os", 0)))
                                    e.wait_ge(*S.at("dve_free_o", ("o", 0, 3)))
                                key = (("rk", "vr", "gr")[u], hh, m)
                                if m == 0:
                                    hi("R", j + 1, 0)
                                    hi("R", j + 1, 1)
                                if m < NT:
                                    e.wait_ge(*S.at("mm_ready", ("N", j, m)))
                                    if u == 2:
                                        e.wait_ge(*S.own())
                                        e.activation(gs[:, m, :], pv(bank, P, UC), ACT.Tanh, scale=0.5).then_inc(*S.up(f"act_free_{bank}", key))
                                    else:
                                        e.activation(buf[:, m, :], pv(bank, P, UC), ACT.Copy).then_inc(*S.up(f"act_free_{bank}", key))
                                else:
                                    rest_copy(bank, ("N", j, m), prev)
                                    prev = ("rest", hh, u)
                                    if u == 2:
                                        e.wait_ge(*S.at("dve_step", ("gsum", hh)))
                                        e.wait_ge(*S.own())
                                        e.activation(gs[0:DEC, NT, :], rest[:, 0:UC], ACT.Tanh, scale=0.5).then_inc(*S.up("act_step", key=("gs", hh)))
                                if u == 2 and m in (2, 3):
                                    for ib in ((0, 1) if m == 2 else (2, 3)):
                                        squares(S, e, hh, ib, i)
                            if u == 1:
                                for v, dst in ((0, qrT), (1, krT)):
                                    e.wait_ge(*S.at("s_ready", ("qk", hh, v)))
                                    e.wait_ge(*S.own())
                                    e.activation(dst[:, :], pv(f"s{v}", P, TOK), ACT.Copy).then_inc(*S.up(f"act_free_s{v}", ("qk", hh, v)))
                        squares(S, e, hh, NT, i)
                        e.wait_ge(*S.at("o_ready", ("sfin", hh)))
                        if hh:
                            e.wait_ge(*S.at("st_out0", ("st", 0)))
                        else:
                            e.wait_ge(*S.at("st_out0", k=0))
                        e.wait_ge(*S.own())
                        e.activation(sout[:, 0, :], pv("o", P, RET_DV), ACT.Copy).then_inc(*S.up("act_free_o", ("sfin", hh)))
                        for b, (name, w, key) in enumerate((("state_ret_prompt", "act_free_o", ("sfin", hh)),
                                                            ("state_ret_sample", "dve_free_s1", ("snew", hh)))):
                            e.wait_ge(*S.at(w, key))
                            e.dma_start(A[name][ds(l, 1), 0, ds(i * 2 + hh, 1)].rearrange("a h d e -> d (a h e)"),
                                                 sout[:, b, :]).then_inc(*S.up(f"st_out{b}", ("st", hh), n=16))
                with S.body("M"):
                    for j in range(16):
                        kind = j // 4
                        if kind == 0:
                            for tt in range(4):
                                bank = f"mm{(4 * j + tt) % 2}"
                                if tt == 0:
                                    hi("M", j + 1, 0)
                                    hi("M", j + 1, 1)
                                e.wait_ge(*S.at("mm_ready", ("T", j, tt // 2, tt % 2)))
                                if j == 0 and tt == 0:
                                    for s in ("t_ready", "o_ready", "s_ready", "dve_step", "dve_free_t"):
                                        e.wait_ge(*S.at(s, k=0))
                                e.activation(tb[:, 2 * j + tt // 2, (tt % 2) * HALF:(tt % 2 + 1) * HALF], pv(bank, P, HALF),
                                             ACT.Tanh, scale=0.5).then_inc(*S.up(f"act_free_{bank}", ("gb", j, tt)))
                                if j < 2 and tt == 0:
                                    if j:
                                        e.wait_ge(*S.at("dve_step", ("ssd", 0)))
                                    e.wait_ge(*S.own())
                                    e.activation(squares_of_dif[:, :, :], odif[:, :, j * 512:(j + 1) * 512], ACT.Square).then_inc(
                                        *S.up("act_step", key=("sqd", j)))
                                if j >= 2:
                                    c = 4 * (j - 2) + tt
                                    g = vecs[:, ds(l, 1), 2 * KC + c % 2:2 * KC + c % 2 + 1].rearrange("p a b -> p (a b)")
                                    e.wait_ge(*S.at("s_ready", ("ret", c)))
                                    e.wait_ge(*S.at("dve_step", ("ssd", 1)))
                                    e.wait_ge(*S.own())
                                    S.settle()
                                    e.activation(hl2[:, c, 0, :], pv(f"s{c % 2}", P, TOK), ACT.Copy, scale=g).then_inc(
                                        *S.up(f"act_free_s{c % 2}", ("ret", c)))
                        elif kind == 1:
                            u = j - 4
                            hi("M", j + 1, 0)
                            hi("M", j + 1, 1)
                            for c in (2 * u, 2 * u + 1):
                                e.wait_ge(*S.at("s_ready", ("dif", c)))
                                if c == 0:
                                    e.wait_ge(*S.at("mm_ready", ("end", 3)))
                                e.wait_ge(*S.own())
                                S.settle()
                                e.activation(hl1[:, c, 0, :], pv(f"s{c % 2}", P, TOK), ACT.Copy, scale=gd[:, ds(l, 1)]).then_inc(
                                    *S.up(f"act_free_s{c % 2}", ("dif", c)))
                        elif kind == 2:
                            u = j - 8
                            for tt in range(4):
                                if tt == 0:
                                    hi("M", j + 1, 0)
                                    hi("M", j + 1, 1)
                                c, h0 = 2 * u + tt // 2, (tt % 2) * HALF
                                e.wait_ge(*S.at("dve_step", ("mer", j, tt)))
                                if j == 8 and tt == 0:
                                    e.wait_ge(*S.at("mm_ready", ("end", 7)))
                                e.wait_ge(*S.own())
                                e.activation(hl2[:, c, 0, h0:h0 + HALF], mer[:, c, h0:h0 + HALF], ACT.Copy, scale=0.5).then_inc(*S.up("act_step", key=("mhi", j, tt)))
                            if u == 3:
                                e.wait_ge(*S.at("dve_step", ("lo", "mer", 3)))
                                for st in ("st_out0", "st_out1"):
                                    e.wait_ge(*S.at(st, k=0))
                                e.wait_ge(*S.own())
                                e.activation(xs2[:, :, :, :].rearrange("p c v s -> p (c v) s"),
                                             hl2[:, :, :, SEQ:TOK].rearrange("p c v s -> p (c v) s"), ACT.Copy).then_inc(*S.up("act_step", key=("xs", "mer")))
                        else:
                            u = j - 12
                            for m in range(2):
                                hi("M", j + 1, m)
                            for m in range(TILES):
                                bank = f"mm{(48 + u * 5 + m) % 2}"
                                if m == NT:
                                    rest_copy(bank, ("N", j, 4), ("rest", j - 1) if u else None)
                                e.wait_ge(*S.at(f"dve_free_{bank}", ("x", u, m)))
                                squares_of_x(m, u * UC, UC, xn[:, m, 0:UC], 40 + 4 * m + u, ("ssq", m) if u == 3 else None)
                    norm("n")
                with S.body("F") as f:
                    for s in ("dve_step", "s_ready", "dve_free_s0", "dve_free_s1", "dve_free_t", "cs_out", "st_out0", "st_out1", "mm_ready"):
                        e.wait_ge(*S.at(s, k=0))
                    def first_tap(j, s):
                        w = lambda v: conv[:, ds(l, 1), v, ds(f * FB + (j + s * FT), 1)]
                        if s == 0:
                            e.wait_ge(*S.at("dve_step", ("pads", j)))
                            if j:
                                e.wait_ge(*S.at("dve_step", ("af", j - 1)))
                        else:
                            e.wait_ge(*S.at("dve_free_" + UP_BANKS[j % 2][3], ("ug", j, 1)))
                        e.wait_ge(*S.own())
                        S.settle()
                        e.activation(ca[:, s, :], up[:, j % 2, s, 0:GP], ACT.Identity, bias=w(5), scale=w(2)).then_inc(
                            *S.up("act_step", key=("tap0", j, s)))

                    def half_tanh(j):
                        e.wait_ge(*S.at("dve_step", ("conv2", j, 1)))
                        e.wait_ge(*S.own())
                        e.activation(th[:, :], ca[:, 1, :], ACT.Tanh, scale=0.5).then_inc(*S.up("act_step", key=("th", j)))

                    def gated_hi(j):
                        e.wait_ge(*S.at("dve_step", ("af", j)))
                        e.wait_ge(*S.own())
                        e.activation(act[:, j, 0, :], af[:, :], ACT.Copy).then_inc(*S.up("act_step", key=("ahi", j)))

                    def sample_rows(n):
                        k0, k1 = sum(DOWN[0][:n]), sum(DOWN[0][:n + 1])
                        e.wait_ge(*S.at("dve_step", ("alo", k1 - 1)))
                        e.wait_ge(*S.own())
                        e.activation(acts[:, k0:k1, :, :].rearrange("p c v s -> p (c v) s"),
                                     act[:, k0:k1, :, GP - DEC:GP].rearrange("p c v s -> p (c v) s"),
                                     ACT.Copy).then_inc(*S.up("act_step", key=("acts", n)))

                    for j in range(FB):
                        b = j % 2
                        b0, b1 = UP_BANKS[b][0:2]
                        if j:
                            first_tap(j - 1, 1)
                        hi("F", j + 1, 0)
                        hi("F", j + 1, 1)
                        if j:
                            half_tanh(j - 1)
                        e.wait_ge(*S.at("mm_ready", ("T", j, 0, 0)))
                        if j >= 2:
                            e.wait_ge(*S.at("dve_step", ("cs", j - 2)))
                            e.wait_ge(*S.at("dve_step", ("conv2", j - 2, 1)))
                        e.activation(up[:, b, 0, 2:2 + HALF], pv(b0, P, HALF), ACT.Copy).then_inc(*S.up(f"act_free_{b0}", ("ua", j, 0)))
                        if j:
                            gated_hi(j - 1)
                        for n in (0, 1):
                            if j == sum(DOWN[0][:n + 1]) + 1:
                                sample_rows(n)
                        e.wait_ge(*S.at("mm_ready", ("T", j, 0, 1)))
                        e.activation(up[:, b, 0, 2 + HALF:2 + SEQ], pv(b1, P, SEQ - HALF), ACT.Copy).then_inc(*S.up(f"act_free_{b1}"))
                        e.activation(up[:, b, 0, 4 + SEQ:4 + TOK], pv(b1, P, DEC, SEQ - HALF), ACT.Copy).then_inc(
                            *S.up(f"act_free_{b1}", ("ua", j, 1)))
                        first_tap(j, 0)
                    first_tap(FB - 1, 1)
                    hi("F", FB + 1, 0)
                    half_tanh(FB - 1)
                    hi("F", FB + 1, 1)
                    gated_hi(FB - 1)
                    sample_rows(2)
                    j = FB
                    for hf in range(2):
                        for n, nk in enumerate(DOWN[hf]):
                            if j > FB:
                                prep("F", j + 1)
                            j += 1
                        rest_copy("s1", ("down", hf, NT), ("drest", 0) if hf else None, 512)
                        for m in range(TILES):
                            e.wait_ge(*S.at(f"dve_free_{DOWN_BANKS[m]}", ("down", hf, m)))
                            squares_of_x(m, hf * 512, 512, th[:, 0:512], 40 + 2 * m + hf, None)
                    e.wait_ge(*S.at("dve_free_t", "cs"))
                    for q in range(2):
                        name = ("state_conv_prompt", "state_conv_sample")[q]
                        for s in range(2):
                            dst = A[name][ds(l, 1), 0, :, ds(f * FB * P + s * D_FF, FB * P)].rearrange(
                                "a t (c p) -> c (a t) p", p=P)
                            e.dma_start(dst, csT[s * FB:(s + 1) * FB, 2 * q:2 * q + 2, :]).then_inc(*S.up("cs_out", ("cs", q, s), n=16))

        def squares(S, e, hh, ib, i):
            r = ROWS[ib]
            bank = "to"[ib % 2]
            key = ("o", hh, ib) if ib < NT else ("os", hh)
            e.wait_ge(*S.at(f"dve_free_{bank}", key))
            e.wait_ge(*S.own())
            junk = rk[0:r, 0, :]
            S.settle()
            e.activation(junk, pv(bank, r, RET_DV), ACT.Square,
                                  accum_out=ssr[0:r, ib, ds(i * 2 + hh, 1)]).then_inc(*S.up(f"act_free_{bank}", key))

        def dve_program(S):
            e = S.e





            def mean(n, width, key, at=0, sums=None):
                e.wait_ge(*S.own())
                e.tensor_scalar(ms[:, at:at + n], ss[:, at:at + n] if sums is None else sums, 1.0 / width, EPS, ALU.mult, ALU.add).then_inc(
                    *S.up("dve_step", key=("ms", key)))

            def norm(key, parts):
                e.wait_ge(*S.own())
                e.tensor_reduce(ss[:, 0:TILES], ss[:, 40:40 + TILES * parts].rearrange("p (m q) -> p m q", m=TILES), AX, ALU.add).then_inc(
                    *S.up("dve_step"))
                mean(TILES, D_MODEL, key)
                e.wait_ge(*S.at("pool_step", ("rstd", key)))
                for m in (0, 2, 4):
                    r = ROWS[m]
                    e.wait_ge(*S.own())
                    e.tensor_scalar(xn[0:r, m, :], x[0:r, m, :], rstd[0:r, m:m + 1], None, ALU.mult).then_inc(
                        *S.up("dve_step", key=("xn", key) if m == NT else None))
                for c in range(KC):
                    o = c if S.phase == "N" else KC + c
                    bank = NORM_BANKS[c % 4]
                    g = vecs[:, ds(S.layer, 1), o:o + 1].rearrange("p a b -> p (a b)")
                    e.wait_ge(*S.at(f"act_free_{bank}", ("norm", c)))
                    e.wait_ge(*S.own())
                    e.scalar_tensor_tensor(out=hl1[:, c, 1, :], in0=pv(bank, P, TOK), scalar=g, in1=hl1[:, c, 0, :].bitcast(F32),
                                           op0=ALU.mult, op1=ALU.subtract).then_inc(*S.up(f"dve_free_{bank}", ("norm", c)))

            for b in BANK:
                S.prime(f"dve_free_{b}", 1)
            S.prime("dve_step", 1)
            e.memset(ss[:, :], 1.0).then_inc(*S.up("dve_step"))
            e.memset(ssr[:, :, :], 1.0).then_inc(*S.up("dve_step", key="ones"))
            e.wait_ge(*S.at("params", "all"))
            e.wait_ge(*S.at("tables", "small"))
            e.wait_ge(*S.at("x_in", "x"))
            for l in range(DEPTH):
                v = prob[:, l, 0:4 * DIFF_HD].rearrange("p (a b) -> p a b", a=4)
                e.wait_ge(*S.own())
                e.tensor_tensor(v[:, 0:2, :], v[:, 0:2, :], v[:, 2:4, :], ALU.mult).then_inc(*S.up("dve_step"))
                e.wait_ge(*S.own())
                e.tensor_reduce(aT[:, 0, 8 + 2 * l:10 + 2 * l], v[:, 0:2, :], AX, ALU.add).then_inc(*S.up("dve_step", key="lamp" if l == DEPTH - 1 else None))
            e.wait_ge(*S.at("act_step", "lexp"))
            for l in range(DEPTH):
                e.wait_ge(*S.own())
                e.tensor_tensor(lam[:, l:l + 1], aT[:, 0, 2 * l + 1:2 * l + 2], aT[:, 0, 2 * l:2 * l + 1], ALU.subtract).then_inc(*S.up("dve_step"))
                e.wait_ge(*S.own())
                e.tensor_tensor(lam[:, l:l + 1], lam[:, l:l + 1], lamc[:, l:l + 1], ALU.subtract).then_inc(*S.up("dve_step"))
                e.wait_ge(*S.own())
                e.memset(sgn[0:DEC, l:l + 1], 1.0).then_inc(*S.up("dve_step"))
                e.wait_ge(*S.own())
                e.tensor_copy(sgn[DEC:2 * DEC, l:l + 1], lam[0:DEC, l:l + 1]).then_inc(*S.up("dve_step"))
            e.wait_ge(*S.at("pe_step", "params"))
            for l in range(DEPTH):
                e.wait_ge(*S.own())
                e.tensor_copy(vecs[:, l, :], pv("t", P, NVEC, l * NVEC)).then_inc(*S.up("dve_step"))
                e.wait_ge(*S.own())
                e.tensor_copy(conv[:, l, :, :].rearrange("p a b -> p (a b)"), pv(f"s{l}", P, 12 * FT)).then_inc(*S.up("dve_step"))
                e.wait_ge(*S.own())
                e.tensor_tensor(gd[:, l:l + 1], vecs[:, l, 18:19], lamc[:, 2 + l:3 + l], ALU.mult).then_inc(*S.up("dve_step"))
            with S.layers() as l:
                with S.body("N"):
                    e.wait_ge(*S.at("act_step", k=0))
                    e.wait_ge(*S.at("pool_step", k=0))
                    norm("n", 2)
                    for s in ("mm_ready", "s_ready", "act_step"):
                        e.wait_ge(*S.at(s, k=0))
                    e.wait_ge(*S.at("s_ready", ("norm", KC - 1)))
                    e.wait_ge(*S.at("act_step", ("xs", "n")))
                    e.wait_ge(*S.own())
                    e.memset(qz[DIFF_HD:P, :, 0:TOK], 0.0).then_inc(*S.up("dve_step"))
                    e.memset(qz[0:DIFF_HD, :, TOK:2 * TOK], 0.0).then_inc(*S.up("dve_step"))
                    e.memset(rawq[:, NT, :], 0.0).then_inc(*S.up("dve_step"))
                    e.memset(rawk[:, NT, :], 0.0).then_inc(*S.up("dve_step"))
                    e.memset(odif[:, NT, :], 0.0).then_inc(*S.up("dve_step"))
                    e.memset(nmax[:, :, :], 0.0).then_inc(*S.up("dve_step"))
                with S.body("D") as p:
                    lreg = l

                    def sample_sum(buf, bank, key, name):
                        e.wait_ge(*S.at(f"act_free_{bank}", ("rest",) + key))
                        e.wait_ge(*S.own())
                        e.tensor_tensor(buf, pv(bank, DEC, UC), rest[:, 0:UC], ALU.add).then_inc(*S.up(f"dve_free_{bank}"))
                        e.wait_ge(*S.own())
                        e.memset(rinv[:, 0, 2:3], 0.0).then_inc(*S.up("dve_step", key=("rest", name)))

                    def qk_sums(name):
                        e.wait_ge(*S.at("act_step", ("sq", name)))
                        e.wait_ge(*S.own())
                        e.tensor_reduce(ss[:, 0:20], prob[:, :, :].rearrange("p a b -> p (a b)")[:, 0:TILES * UC].rearrange(
                            "p (g d) -> p g d", d=DIFF_HD), AX, ALU.add).then_inc(*S.up("dve_step", key=("ss", name)))
                        mean(20, DIFF_HD, name)

                    def qk_apply(buf, name, v):
                        e.wait_ge(*S.at("pool_step", ("rstd", name)))
                        b3 = buf[:, :, :].rearrange("p m (h d) -> p (m h) d", d=DIFF_HD)
                        e.wait_ge(*S.own())
                        e.tensor_tensor(b3, b3, rstd[:, 0:20].unsqueeze(2).broadcast_to([P, 20, DIFF_HD]), ALU.mult).then_inc(*S.up("dve_step"))
                        e.wait_ge(*S.own())
                        e.tensor_tensor(b3, b3, qkg[:, ds(lreg, 1), v, :].broadcast_to([P, 20, DIFF_HD]), ALU.mult).then_inc(*S.up("dve_step"))
                        b4 = buf[:, :, :].rearrange("p m (h d) -> p m h d", d=DIFF_HD)
                        x1, x2 = b4[:, :, :, 0:8], b4[:, :, :, 8:16]
                        c, s = (t.unsqueeze(2).broadcast_to([P, TILES, 4, 8]) for t in (dcos, dsin))
                        t1, t2 = (rt[:, k, :].rearrange("p (m h d) -> p m h d", m=TILES, h=4) for k in (0, 1))
                        e.wait_ge(*S.own())
                        e.tensor_tensor(t1, x2, s, ALU.mult).then_inc(*S.up("dve_step"))
                        e.wait_ge(*S.own())
                        e.tensor_tensor(t2, x1, s, ALU.mult).then_inc(*S.up("dve_step"))
                        e.wait_ge(*S.own())
                        e.tensor_tensor(x1, x1, c, ALU.mult).then_inc(*S.up("dve_step"))
                        e.wait_ge(*S.own())
                        e.tensor_tensor(x2, x2, c, ALU.mult).then_inc(*S.up("dve_step"))
                        e.wait_ge(*S.own())
                        e.tensor_tensor(x1, x1, t1, ALU.subtract).then_inc(*S.up("dve_step"))
                        e.wait_ge(*S.own())
                        e.tensor_tensor(x2, x2, t2, ALU.add).then_inc(*S.up("dve_step", key=("rope", name)))

                    sample_sum(rawq[0:DEC, NT, :], "mm0", ("N", 0, 4), "q")
                    qk_sums("q")
                    qk_apply(rawq, "q", 0)
                    sample_sum(rawk[0:DEC, NT, :], "mm1", ("N", 1, 4), "k")
                    qk_sums("k")
                    for hh in range(2):
                        e.wait_ge(*S.at("s_ready", ("q", hh)))
                        e.wait_ge(*S.own())
                        e.tensor_scalar(qz[DIFF_HD:P, hh, TOK + DEC:TOK + DEC + SEQ], ps[DIFF_HD:P, BANK[f"s{hh}"]:BANK[f"s{hh}"] + SEQ], DIFF_HD ** -0.5, None, ALU.mult).then_inc(*S.up(f"dve_free_s{hh}", key=("q0", hh)))
                        e.wait_ge(*S.own())
                        e.tensor_scalar(qz[DIFF_HD:P, hh, TOK:TOK + DEC], ps[DIFF_HD:P, BANK[f"s{hh}"] + SEQ:BANK[f"s{hh}"] + TOK], DIFF_HD ** -0.5, None, ALU.mult).then_inc(*S.up(f"dve_free_s{hh}", key=("q1", hh)))
                    qk_apply(rawk, "k", 1)
                    sample_sum(vd[0:DEC, NT, :], "mm0", ("N", 2, 4), "v")

                    steps = [(hh, ib) for hh in range(2) for ib in range(TILES)]

                    def maxes(n):
                        hh, ib = steps[n]
                        b = n % 2
                        e.wait_ge(*S.at("s_ready", ("s", n)))
                        if n >= 2:
                            e.wait_ge(*S.at("act_free_s%d" % b, ("exp", n - 2)))
                        if ib < NT:
                            k = (ib + 1) * P
                            v = pv(f"s{b}", P, 1024).rearrange("p (c n) -> p c n", c=2)
                            e.wait_ge(*S.own())
                            e.memset(v[0:CHUNK, :, k - CHUNK:k], NEG).then_inc(*S.up("dve_step"))
                            e.wait_ge(*S.own())
                            e.tensor_reduce(nmax[:, b, :], v[:, :, 0:k], AX, ALU.max, negate=True).then_inc(*S.up("dve_step", key=("max", n)))
                        else:
                            e.wait_ge(*S.own())
                            e.tensor_reduce(nmax[0:2 * DEC, b, 0:1], pv(f"s{b}", 2 * DEC, TOK), AX, ALU.max, negate=True).then_inc(*S.up("dve_step", key=("max", n)))

                    def combine(n):
                        hh, ib = steps[n]
                        b = n % 2
                        e.wait_ge(*S.at(f"act_free_s{b}", ("exp", n)))
                        if n >= 4:
                            e.wait_ge(*S.at("act_free_o", ("o", n - 4)))
                        e.wait_ge(*S.own())
                        if ib < NT:
                            k = (ib + 1) * P
                            e.reciprocal(rinv[:, n % 4, 0:2], sums[:, b, :]).then_inc(*S.up("dve_step"))
                            e.wait_ge(*S.own())
                            e.scalar_tensor_tensor(out=rinv[:, n % 4, 2:3], in0=sums[:, b, 0:1], scalar=lam[:, ds(lreg, 1)], in1=rinv[:, n % 4, 1:2], op0=ALU.mult, op1=ALU.mult).then_inc(*S.up("dve_step"))
                            e.wait_ge(*S.own())
                            e.scalar_tensor_tensor(out=prob[:, b, 0:k], in0=prob[:, b, 512:512 + k], scalar=rinv[:, n % 4, 2:3], in1=prob[:, b, 0:k], op0=ALU.mult, op1=ALU.add).then_inc(*S.up("dve_step", key=("a", n)))
                        else:
                            r = 2 * DEC
                            e.reciprocal(rinv[0:r, n % 4, 0:1], sums[0:r, b, 0:1]).then_inc(*S.up("dve_step"))
                            e.wait_ge(*S.own())
                            e.tensor_tensor(rinv[0:r, n % 4, 2:3], rinv[0:r, n % 4, 0:1], sgn[:, ds(lreg, 1)], ALU.mult).then_inc(*S.up("dve_step"))
                            e.wait_ge(*S.own())
                            e.tensor_scalar(prob[0:r, b, 0:TOK], prob[0:r, b, 0:TOK], rinv[0:r, n % 4, 2:3], None, ALU.mult).then_inc(*S.up("dve_step", key=("a", n)))

                    def weights_of_sample(n):
                        if steps[n][1] < NT:
                            return
                        v = pv("t", P, TILES * 2 * DEC).rearrange("p (c n) -> p c n", c=TILES)
                        e.wait_ge(*S.at("act_free_t", ("aTt", n)))
                        if n > 5:
                            e.wait_ge(*S.at("o_ready", (0, NT)))
                        e.wait_ge(*S.own())
                        e.tensor_tensor(aTs[:, 0:NT, :], v[:, 0:NT, 0:DEC], aTt[:, 0:NT, :], ALU.add).then_inc(*S.up("dve_free_t"))
                        e.wait_ge(*S.own())
                        e.tensor_tensor(aTs[0:DEC, NT, :], v[0:DEC, NT, 0:DEC], aTt[0:DEC, NT, :], ALU.add).then_inc(*S.up("dve_free_t", ("aT", n)))

                    maxes(0)
                    maxes(1)
                    for n in range(10):
                        combine(n)
                        if n + 2 < 10:
                            maxes(n + 2)
                        weights_of_sample(n)
                with S.body("R") as i:
                    for hh in range(2):
                        head = i * 2 + hh
                        t0 = 15 * hh

                        def sample_sum(buf, bank, key, u):
                            e.wait_ge(*S.at(f"act_free_{bank}", ("rest",) + key))
                            e.wait_ge(*S.own())
                            e.tensor_tensor(buf, pv(bank, DEC, UC), rest[:, 0:UC], ALU.add).then_inc(*S.up(f"dve_free_{bank}"))
                            e.wait_ge(*S.own())
                            e.memset(qx[:, 0:1], 0.0).then_inc(*S.up("dve_step", key=("rest", hh, u)))

                        if hh == 0:
                            for s in ("s_ready", "o_ready", "t_ready", "kv_out", "act_step", "act_free_t"):
                                e.wait_ge(*S.at(s, k=0))
                            e.wait_ge(*S.own())
                            e.memset(rk[:, NT, :], 0.0).then_inc(*S.up("dve_step"))
                        sample_sum(rk[0:DEC, NT, :], f"mm{(t0 + 4) % 2}", ("N", 3 * hh, 4), 0)
                        e.wait_ge(*S.at("act_free_mm0", ("rk", hh, 2 if not hh else 3)))
                        e.wait_ge(*S.at("act_free_mm1", ("rk", hh, 3 if not hh else 2)))
                        if hh:
                            e.wait_ge(*S.at("t_ready", ("os", 0)))
                        rv = rk[:, :, :].rearrange("p m (v d) -> p m v d", v=2)
                        x1, x2 = rv[:, :, :, 0:64], rv[:, :, :, 64:128]
                        c, s = (t.unsqueeze(2).broadcast_to([P, TILES, 2, 64]) for t in (rcos, rsin))
                        t1, t2 = (b[:, 0:TILES * 128].rearrange("p (m v d) -> p m v d", m=TILES, v=2) for b in (sT, kzf))
                        if hh:
                            e.wait_ge(*S.at("s_ready", ("snew", 0)))
                        e.wait_ge(*S.own())
                        e.tensor_tensor(t1, x2, s, ALU.mult).then_inc(*S.up("dve_step"))
                        e.wait_ge(*S.own())
                        e.tensor_tensor(t2, x1, s, ALU.mult).then_inc(*S.up("dve_step"))
                        e.wait_ge(*S.own())
                        e.tensor_tensor(x1, x1, c, ALU.mult).then_inc(*S.up("dve_step"))
                        e.wait_ge(*S.own())
                        e.tensor_tensor(x2, x2, c, ALU.mult).then_inc(*S.up("dve_step"))
                        e.wait_ge(*S.own())
                        e.tensor_tensor(x1, x1, t1, ALU.subtract).then_inc(*S.up("dve_step"))
                        e.wait_ge(*S.own())
                        e.tensor_tensor(x2, x2, t2, ALU.add).then_inc(*S.up("dve_step", key=("rope", hh)))
                        e.wait_ge(*S.own())
                        e.tensor_tensor(kz[:, :, :], rk[:, :, P:2 * P], zeta[:, :, ds(head, 1)].broadcast_to([P, TILES, P]), ALU.mult).then_inc(*S.up("dve_step", key=("kz", hh)))
                        sample_sum(vr[0:DEC, NT, :], f"mm{(t0 + 9) % 2}", ("N", 3 * hh + 1, 4), 1)
                        e.wait_ge(*S.at("act_free_s0", ("qk", hh, 0)))
                        e.wait_ge(*S.own())
                        e.tensor_tensor(qx[:, :], qrT[:, SEQ:TOK], xi[:, ds(head, 1), :].rearrange("p a b -> p (a b)"), ALU.mult).then_inc(*S.up("dve_step", key=("qx0", hh)))

                        def gate(m):
                            bank = f"mm{(t0 + 10 + m) % 2}"
                            e.wait_ge(*S.at(f"act_free_{bank}", ("gr", hh, m)))
                            e.wait_ge(*S.own())
                            e.scalar_tensor_tensor(out=gs[:, m, :], in0=gs[:, m, :], scalar=1.0, in1=pv(bank, P, UC), op0=ALU.add, op1=ALU.mult).then_inc(*S.up(f"dve_free_{bank}", ("gr", hh, m)))

                        def decayed(jb):
                            n = SEQ - jb * P
                            bank = ("s0", "s1")[jb // 2]
                            e.wait_ge(*S.at("s_ready", ("ret", hh, jb)))
                            if jb == 0:
                                e.wait_ge(*S.at("decay_in", "d"))
                            e.wait_ge(*S.own())
                            e.tensor_tensor(sT[:, SOFF[jb]:SOFF[jb] + n], pv(bank, P, n, (jb % 2) * 512), decay[:, hh, 0:n], ALU.mult).then_inc(*S.up(f"dve_free_{bank}", ("sT", hh, jb)))

                        def gated(ib):
                            bank = "to"[ib % 2]
                            r = ROWS[ib]
                            key = ("o", hh, ib) if ib < NT else ("os", hh)
                            e.wait_ge(*S.at(f"{'to'[ib % 2]}_ready", key))
                            e.wait_ge(*S.own())
                            e.tensor_tensor(oret[0:r, ds(head * 2, 2), ib, :], pv(bank, r, RET_DV).rearrange("p (t d) -> p t d", t=2),
                                            gs[0:r, ib, :].rearrange("p (t d) -> p t d", t=2), ALU.mult).then_inc(*S.up(f"dve_free_{bank}", key))

                        gate(0)
                        decayed(0)
                        decayed(1)
                        gate(1)
                        decayed(2)
                        decayed(3)
                        gate(2)
                        gated(0)
                        gated(1)
                        e.wait_ge(*S.at("s_ready", ("rets", hh)))
                        e.wait_ge(*S.own())
                        e.tensor_tensor(sTs_x[:, :], pv("s0", DEC, DEC), decay[0:DEC, hh, 0:DEC], ALU.mult).then_inc(*S.up("dve_free_s0", ("sTs", hh)))
                        e.wait_ge(*S.own())
                        e.memset(rstd[:, 39:40], 0.0).then_inc(*S.up("dve_step", key=("qx", hh)))
                        gate(3)
                        gated(2)
                        gated(3)
                        bank = f"mm{(t0 + 14) % 2}"
                        e.wait_ge(*S.at(f"act_free_{bank}", ("rest", "N", 3 * hh + 2, 4)))
                        e.wait_ge(*S.own())
                        e.tensor_tensor(rest[:, 0:UC], pv(bank, DEC, UC), rest[:, 0:UC], ALU.add).then_inc(*S.up(f"dve_free_{bank}"))
                        e.wait_ge(*S.own())
                        e.memset(rstd[:, 39:40], 0.0).then_inc(*S.up("dve_step", key=("gsum", hh)))
                        e.wait_ge(*S.at("act_step", ("gs", hh)))
                        e.wait_ge(*S.own())
                        e.scalar_tensor_tensor(out=gs[0:DEC, NT, :], in0=gs[0:DEC, NT, :], scalar=1.0, in1=rest[:, 0:UC], op0=ALU.add, op1=ALU.mult).then_inc(*S.up(f"dve_free_{bank}"))
                        e.wait_ge(*S.own())
                        e.memset(rstd[:, 39:40], 0.0).then_inc(*S.up("dve_step", key=("rest", hh, 2)))
                        gated(NT)
                        e.wait_ge(*S.at("s_ready", ("snew", hh)))
                        e.wait_ge(*S.at("sin_in", ("s", hh)))
                        e.wait_ge(*S.at("st_out1", ("st", 0))) if hh else e.wait_ge(*S.at("st_out1", k=0))
                        e.wait_ge(*S.own())
                        e.scalar_tensor_tensor(out=sout[:, 1, :], in0=sin[:, :], scalar=g32[:, ds(head, 1)], in1=pv("s1", P, RET_DV), op0=ALU.mult, op1=ALU.add).then_inc(*S.up("dve_free_s1", ("snew", hh)))
                with S.body("M"):
                    e.wait_ge(*S.at("act_free_o", k=0))
                    e.wait_ge(*S.at("act_free_t", k=0))
                    mean(20, RET_DV, "ret", 40, ssr[:, :, :].rearrange("p m h -> p (m h)"))
                    def sums_of_dif(q):
                        e.wait_ge(*S.at("act_step", ("sqd", q)))
                        e.wait_ge(*S.own())
                        e.tensor_reduce(ss[:, q * 20:q * 20 + 20], squares_of_dif[:, :, :].rearrange("p m (h d) -> p (m h) d", h=4), AX, ALU.add).then_inc(
                            *S.up("dve_step", key=("ssd", q)))
                        mean(20, HW, f"dif{q}", q * 20)

                    def scale_dif(q):
                        e.wait_ge(*S.at("pool_step", ("rstd", f"dif{q}")))
                        for m in range(TILES):
                            r = ROWS[m]
                            v = odif[0:r, m, q * 512:(q + 1) * 512].rearrange("p (h d) -> p h d", h=4)
                            rs = rstd[0:r, q * 20 + m * 4:q * 20 + m * 4 + 4].unsqueeze(2).broadcast_to([r, 4, HW])
                            e.wait_ge(*S.own())
                            e.tensor_tensor(v, v, rs, ALU.mult).then_inc(*S.up("dve_step", key=("odif", q) if m == NT else None))

                    sums_of_dif(0)
                    e.wait_ge(*S.at("pool_step", ("rstd", "ret")))
                    for m in range(TILES):
                        r = ROWS[m]
                        v = oret[0:r, :, m, :].rearrange("p (h t) d -> p h t d", t=2)
                        rs = rstd[0:r, 40 + m * 4:44 + m * 4].unsqueeze(2).unsqueeze(3).broadcast_to([r, RET_HEADS, 2, P])
                        e.wait_ge(*S.own())
                        e.tensor_tensor(v, v, rs, ALU.mult).then_inc(*S.up("dve_step", key=("oret", "done") if m == NT else None))
                    sums_of_dif(1)
                    for c in range(KC):
                        g = vecs[:, ds(l, 1), 2 * KC + c % 2:2 * KC + c % 2 + 1].rearrange("p a b -> p (a b)")
                        e.wait_ge(*S.at(f"act_free_s{c % 2}", ("ret", c)))
                        e.wait_ge(*S.own())
                        e.scalar_tensor_tensor(out=hl2[:, c, 1, :], in0=pv(f"s{c % 2}", P, TOK), scalar=g, in1=hl2[:, c, 0, :].bitcast(F32),
                                               op0=ALU.mult, op1=ALU.subtract).then_inc(*S.up(f"dve_free_s{c % 2}", ("lo", "ret", c)))
                        if c == 3:
                            scale_dif(0)
                    for u in range(4):
                        j = 4 + u
                        for t in range(4):
                            bank = f"mm{t % 2}"
                            c, h0 = 2 * u + t // 2, (t % 2) * HALF
                            if t % 2 == 0:
                                e.wait_ge(*S.at(f"act_free_s{c % 2}", ("dif", c)))
                                e.wait_ge(*S.own())
                                e.scalar_tensor_tensor(out=hl1[:, c, 1, :], in0=pv(f"s{c % 2}", P, TOK), scalar=gd[:, ds(l, 1)],
                                                       in1=hl1[:, c, 0, :].bitcast(F32), op0=ALU.mult, op1=ALU.subtract).then_inc(
                                    *S.up(f"dve_free_s{c % 2}", ("lo", "dif", c)))
                            e.wait_ge(*S.at("mm_ready", ("T", j, t // 2, t % 2)))
                            if u == 0 and t == 0:
                                e.wait_ge(*S.at("act_free_mm0", k=0))
                                e.wait_ge(*S.at("act_free_mm1", k=0))
                            e.wait_ge(*S.own())
                            e.scalar_tensor_tensor(out=mer[:, c, h0:h0 + HALF], in0=mer[:, c, h0:h0 + HALF], scalar=1.0, in1=pv(bank, P, HALF), op0=ALU.add, op1=ALU.mult).then_inc(*S.up(f"dve_free_{bank}", ("wa", u, t)))
                            if u == 0 and t == 3:
                                scale_dif(1)
                    for u in range(4):
                        j = 8 + u
                        for t in range(4):
                            bank = f"mm{t % 2}"
                            c, h0 = 2 * u + t // 2, (t % 2) * HALF
                            e.wait_ge(*S.at("mm_ready", ("T", j, t // 2, t % 2)))
                            e.wait_ge(*S.at(f"act_free_{bank}", ("gb", u, t)))
                            e.wait_ge(*S.own())
                            e.scalar_tensor_tensor(out=tb[:, c, h0:h0 + HALF], in0=tb[:, c, h0:h0 + HALF], scalar=1.0, in1=pv(bank, P, HALF), op0=ALU.add, op1=ALU.mult).then_inc(*S.up(f"dve_free_{bank}"))
                            e.wait_ge(*S.own())
                            e.scalar_tensor_tensor(out=mer[:, c, h0:h0 + HALF], in0=mer[:, c, h0:h0 + HALF], scalar=0.5, in1=tb[:, c, h0:h0 + HALF], op0=ALU.mult, op1=ALU.add).then_inc(*S.up("dve_step", key=("mer", j, t)))
                            e.wait_ge(*S.at("act_step", ("mhi", j, t)))
                            e.wait_ge(*S.own())
                            e.scalar_tensor_tensor(out=hl2[:, c, 1, h0:h0 + HALF], in0=mer[:, c, h0:h0 + HALF], scalar=0.5, in1=hl2[:, c, 0, h0:h0 + HALF].bitcast(F32), op0=ALU.mult, op1=ALU.subtract).then_inc(*S.up("dve_step", key=("lo", "mer", t) if u == 3 and t >= 2 else None))
                    for u in range(4):
                        j = 12 + u
                        for m in range(TILES):
                            bank = f"mm{(5 * u + m) % 2}"
                            r = ROWS[m]
                            v = x[0:r, m, u * UC:(u + 1) * UC]
                            e.wait_ge(*S.at("mm_ready", ("N", j, m)))
                            if m == NT:
                                e.wait_ge(*S.at(f"act_free_{bank}", ("rest", "N", j, m)))
                                e.wait_ge(*S.own())
                                e.tensor_tensor(v, v, rest[:, 0:UC], ALU.add).then_inc(*S.up("dve_step", key=("rest", j)))
                            e.wait_ge(*S.own())
                            e.tensor_tensor(v, v, pv(bank, r, UC), ALU.add).then_inc(*S.up(f"dve_free_{bank}", ("x", u, m)))
                    e.wait_ge(*S.at("act_step", ("ssq", NT)))
                    norm("n", 4)
                with S.body("F") as f:
                    for s in ("s_ready", "act_step", "t_ready", "mm_ready", "cs_out", "act_free_s1", "act_free_s0"):
                        e.wait_ge(*S.at(s, k=0))
                    e.wait_ge(*S.own())
                    e.memset(up[:, :, :, 0:2], 0.0).then_inc(*S.up("dve_step"))
                    for j in range(FB):
                        b = j % 2
                        w = lambda v, s: conv[:, ds(l, 1), v, ds(f * FB + (j + s * FT), 1)]
                        for s in range(2):
                            e.wait_ge(*S.own())
                            e.tensor_copy(up[:, b, s, SEQ + 2:SEQ + 4],
                                             conv[:, ds(l, 1), 0:2, ds(f * FB + (j + s * FT), 1)].rearrange("p a v c -> p (a v c)")).then_inc(*S.up("dve_step", key=("pads", j) if s else None))
                        for t in range(2):
                            bank = UP_BANKS[j % 2][2 + t]
                            e.wait_ge(*S.at("mm_ready", ("T", j, 1, t)))
                            e.wait_ge(*S.own())
                            if t == 0:
                                e.tensor_copy(up[:, b, 1, 2:2 + HALF], pv(bank, P, HALF)).then_inc(*S.up(f"dve_free_{bank}", ("ug", j, 0)))
                            else:
                                e.tensor_copy(up[:, b, 1, 2 + HALF:2 + SEQ], pv(bank, P, SEQ - HALF)).then_inc(*S.up(f"dve_free_{bank}"))
                                e.tensor_copy(up[:, b, 1, 4 + SEQ:4 + TOK], pv(bank, P, DEC, SEQ - HALF)).then_inc(*S.up(f"dve_free_{bank}", ("ug", j, 1)))
                            if t == 0:
                                e.wait_ge(*S.at("act_step", ("tap0", j, 0)))
                                for v in (1, 2):
                                    e.wait_ge(*S.own())
                                    e.scalar_tensor_tensor(out=ca[:, 0, :], in0=up[:, b, 0, v:v + GP], scalar=w(2 + v, 0), in1=ca[:, 0, :], op0=ALU.mult, op1=ALU.add).then_inc(*S.up("dve_step"))
                        e.wait_ge(*S.at("act_step", ("tap0", j, 1)))
                        for v in (1, 2):
                            e.wait_ge(*S.own())
                            e.scalar_tensor_tensor(out=ca[:, 1, :], in0=up[:, b, 1, v:v + GP], scalar=w(2 + v, 1), in1=ca[:, 1, :], op0=ALU.mult, op1=ALU.add).then_inc(*S.up("dve_step", key=("conv2", j, 1) if v == 2 else None))
                        for q in range(2):
                            c0 = SEQ if q == 0 else TOK + 2
                            e.wait_ge(*S.own())
                            e.tensor_copy(cs[:, 2 * q:2 * q + 2, :].rearrange("p t (s c) -> p s t c", s=2)[:, :, :, j],
                                             up[:, b, :, c0:c0 + 2]).then_inc(*S.up("dve_step", key=("cs", j) if q else None))
                        e.wait_ge(*S.at("act_step", ("th", j)))
                        e.wait_ge(*S.own())
                        e.scalar_tensor_tensor(out=ca[:, 1, :], in0=th[:, :], scalar=1.0, in1=ca[:, 1, :], op0=ALU.add, op1=ALU.mult).then_inc(*S.up("dve_step"))
                        if j:
                            e.wait_ge(*S.at("act_step", ("ahi", j - 1)))
                        e.wait_ge(*S.own())
                        e.scalar_tensor_tensor(out=af[:, :], in0=ca[:, 1, :], scalar=0.5, in1=ca[:, 0, :], op0=ALU.mult, op1=ALU.mult).then_inc(*S.up("dve_step", key=("af", j)))
                        e.wait_ge(*S.at("act_step", ("ahi", j)))
                        e.wait_ge(*S.own())
                        e.tensor_tensor(act[:, j, 1, :], af[:, :], act[:, j, 0, :].bitcast(F32), ALU.subtract).then_inc(*S.up("dve_step", key=("alo", j)))
                    for hf in range(2):
                        for m in range(TILES):
                            bank = DOWN_BANKS[m]
                            r = ROWS[m]
                            v = x[0:r, m, hf * 512:(hf + 1) * 512]
                            e.wait_ge(*S.at("mm_ready", ("down", hf, m)))
                            if m == NT:
                                e.wait_ge(*S.at("act_free_s1", ("rest", "down", hf, NT)))
                                e.wait_ge(*S.own())
                                e.tensor_tensor(v, v, rest[:, 0:512], ALU.add).then_inc(*S.up("dve_step", key=("drest", hf)))
                            e.wait_ge(*S.own())
                            e.tensor_tensor(v, v, ps[0:r, m * 512:(m + 1) * 512], ALU.add).then_inc(*S.up(f"dve_free_{bank}", ("down", hf, m)))
                        if hf == 0:
                            e.wait_ge(*S.at("t_ready", "cs"))
                            e.wait_ge(*S.at("cs_out", k=0))
                            e.wait_ge(*S.own())
                            e.tensor_copy(csT[:, :, :].rearrange("p a b -> p (a b)"), pv("t", 2 * FB, 4 * P)).then_inc(*S.up("dve_free_t", "cs"))
                    e.wait_ge(*S.own())
                    e.memset(rstd[:, 39:40], 0.0).then_inc(*S.up("dve_step", key="x"))

        kzf = kz[:, :, :].rearrange("p m d -> p (m d)")

        with nc.Block() as block:
            @block.sync
            def _(e):
                sync_program(Stream(e, "sync", known, seen, sem))

            @block.gpsimd
            def _(e):
                pool_program(Stream(e, "pool", known, seen, sem))

            @block.tensor
            def _(e):
                pe_program(Stream(e, "pe", known, seen, sem))

            @block.scalar
            def _(e):
                act_program(Stream(e, "act", known, seen, sem))

            @block.vector
            def _(e):
                dve_program(Stream(e, "dve", known, seen, sem))
    return seen


_INS = ["x_prompt", "x_sample", "cache_k", "cache_v", "state_ret", "state_conv", "norm1_g", "w_in", "ret_norm_g",
        "q_norm_g", "k_norm_g", "lambda_q1", "lambda_k1", "lambda_q2", "lambda_k2", "diff_norm_g", "w_branch_a",
        "w_branch_b", "w_out", "norm2_g", "w_up", "conv_w", "conv_b", "w_down"]
_OUTS = [("y_prompt", (1, SEQ, D_MODEL)), ("y_sample", (1, DEC, D_MODEL)),
         ("new_k_prompt", (DEPTH, 1, SEQ, DIFF_HEADS, HW)), ("new_v_prompt", (DEPTH, 1, SEQ, DIFF_HEADS, HW)),
         ("state_ret_prompt", (DEPTH, 1, RET_HEADS, RET_DK, RET_DV)), ("state_conv_prompt", (DEPTH, 1, 2, 2 * D_FF)),
         ("new_k_sample", (DEPTH, 1, DEC, DIFF_HEADS, HW)), ("new_v_sample", (DEPTH, 1, DEC, DIFF_HEADS, HW)),
         ("state_ret_sample", (DEPTH, 1, RET_HEADS, RET_DK, RET_DV)), ("state_conv_sample", (DEPTH, 1, 2, 2 * D_FF))]


def kernel(**inputs):
    import concourse.bacc as _bacc
    from concourse.bass_utils import run_bass_kernel_spmd

    arrays = {n: np.ascontiguousarray(inputs[n]) for n in _INS}
    arrays["tab_small"], arrays["tab_decay"] = shape_tables()
    counts = None
    for _ in range(2):
        nc = _bacc.Bacc("TRN2", target_bir_lowering=False, num_devices=1)
        tensors = {n: nc.dram_tensor(f"in_{n}_dram", a.shape, F32, kind="ExternalInput").ap() for n, a in arrays.items()}
        for n, s in _OUTS:
            tensors[n] = nc.dram_tensor(f"out_{n}_dram", s, F32, kind="ExternalOutput").ap()
        counts = program(nc, tensors, counts)
    r = run_bass_kernel_spmd(nc, [{f"in_{n}_dram": a for n, a in arrays.items()}], core_ids=[0])
    return tuple(r.results[0][f"out_{n}_dram"] for n, _ in _OUTS)
```

```python
from contextlib import ExitStack, contextmanager

import numpy as np

import concourse.bass as bass
from concourse import mybir

F32 = mybir.dt.float32
F32R = mybir.dt.float32r
ALU = mybir.AluOpType
ACT = mybir.ActivationFunctionType
AX = mybir.AxisListType.X
ds = bass.ds

P = 128
DEPTH = 2
D_MODEL = 1024
SEQ = 512
DEC = 32
PAST = 512
TOK = SEQ + DEC
HALF = TOK // 2
NT = SEQ // P
TILES = NT + 1
ROWS = [P] * NT + [DEC]
RET_HEADS, RET_DK, RET_DV = 4, 128, 256
DIFF_HEADS, DIFF_HD, DIFF_ROT = 8, 64, 16
HW = 2 * DIFF_HD
CHUNK = 64
D_FF = 2816
EPS = 1e-6
KC = D_MODEL // P
UC = 256
UNIT = KC * UC
COL = dict(qr=0, kr=512, vr=1024, gr=2048, qd=3072, kd=4096, vd=5120, ga=6144, gb=7168)
FT = D_FF // P
FB = FT // 2
DOWN = [[4, 4, 3], [3, 3, 3, 2]]
GP = TOK + 2
NEG = -1.0e30
NVEC = 19

ORDER = [("N", 1), ("D", 4), ("R", 2), ("M", 1), ("F", 2)]


def shape_tables():
    f = np.float32
    pos = np.zeros((P, TILES), f)
    for m in range(NT):
        pos[:, m] = m * P + np.arange(P)
    pos[:DEC, NT] = PAST + np.arange(DEC)

    def rope(half, theta):
        inv = (f(theta) ** (-np.arange(half, dtype=f) / f(half))).astype(f)
        ang = (pos[:, :, None] * inv).astype(f)
        return np.cos(ang).astype(f), np.sin(ang).astype(f)

    rc, rs = rope(RET_DK // 2, 10000.0)
    dc, dsn = rope(DIFF_ROT // 2, 500000.0)
    log_g = np.log1p(-np.exp2(-5.0 - np.arange(RET_HEADS, dtype=f))).astype(f)
    ks = f(RET_DK ** -0.5)
    rel = np.arange(SEQ, dtype=f)[None, :] - np.arange(P, dtype=f)[:, None]
    decay = np.where(rel[:, None, :] >= 0, np.exp(log_g[None, :, None] * np.maximum(rel, 0)[:, None, :]), 0) * ks
    zeta = np.zeros((P, TILES, RET_HEADS), f)
    for m in range(NT):
        zeta[:, m] = np.exp(log_g * (SEQ - 1.0 - pos[:, m:m + 1])) * ks
    zeta[:DEC, NT] = np.exp(log_g * (DEC - 1.0 - np.arange(DEC, dtype=f)[:, None])) * ks
    xi = np.exp(log_g[:, None] * (np.arange(DEC, dtype=f) + 1.0))
    lam = [0.8 - 0.6 * np.exp(-0.3 * l) for l in range(DEPTH)]
    small = np.concatenate([
        np.eye(P, dtype=f), rc.reshape(P, -1), rs.reshape(P, -1), dc.reshape(P, -1), dsn.reshape(P, -1),
        zeta.reshape(P, -1), np.broadcast_to(xi.reshape(1, -1), (P, RET_HEADS * DEC)),
        np.broadcast_to(np.exp(log_g * f(DEC))[None], (P, RET_HEADS)),
        np.broadcast_to(np.array([[lam[0], lam[1], 1 - lam[0], 1 - lam[1]]]), (P, 4))], axis=1)
    return small.astype(f), np.ascontiguousarray(decay.astype(f).reshape(P, RET_HEADS * SEQ))


class Counts:

    def __init__(self):
        self.per = {}
        self.keys = {}

    def start(self, phase):
        out = {}
        for name, times in ORDER:
            if name == phase:
                break
            for s, n in self.per.get(name, {}).items():
                out[s] = out.get(s, 0) + n * times
        return out

    def layer(self, sem):
        return sum(self.per.get(name, {}).get(sem, 0) * times for name, times in ORDER)


class Stream:

    def __init__(self, eng, name, known, seen, handles):
        self.e, self.known, self.seen, self.handles = eng, known, seen, handles
        self.step = name + "_step"
        self.layer = self.index = None
        self.phase = "P"
        self.here, self.waited, self.pending = {}, {}, set()
        self.last = None

    @contextmanager
    def layers(self):
        self.leave()
        with self.e.Fori(0, DEPTH) as l:
            self.layer = l
            yield l
        self.layer, self.phase, self.index, self.here, self.waited = None, "end", None, {}, {}

    @contextmanager
    def body(self, phase):
        times = dict(ORDER)[phase]
        self.phase, self.here, self.last, self.waited = phase, {}, None, {}
        if times == 1:
            self.index = None
            yield 0
            self.leave()
        else:
            with self.e.Fori(0, times) as i:
                self.index = i
                yield i
                self.leave()

    def leave(self):
        if self.pending:
            self.settle()
        self.last = None
        per = self.seen.per.setdefault(self.phase, {})
        for s, n in self.here.items():
            per[s] = per.get(s, 0) + n

    def at(self, sem, key=None, k=None):
        if k is None:
            k = self.known.keys[(self.phase, sem, key)] if self.known else 1
        k = max(k, self.waited.get(sem, k))
        if sem in self.pending and k > self.waited[sem]:
            self.settle()
        self.waited[sem] = k
        self.pending.add(sem)
        if self.known is None:
            return self.handles(sem), 1
        c = self.known
        if self.phase == "P":
            return self.handles(sem), k
        value = c.per.get("P", {}).get(sem, 0) + k
        if self.phase == "end":
            return self.handles(sem), value + DEPTH * c.layer(sem)
        value += c.start(self.phase).get(sem, 0)
        if c.layer(sem):
            value = self.layer * c.layer(sem) + value
        each = c.per.get(self.phase, {}).get(sem, 0)
        if self.index is not None and each:
            value = self.index * each + value
        return self.handles(sem), value

    def own(self):
        sem, k = self.last or (self.step, self.here.get(self.step, 0))
        return self.at(sem, k=k)

    def up(self, sem, key=None, n=1):
        self.pending.clear()
        self.here[sem] = self.here.get(sem, 0) + n
        if key is not None:
            assert (self.phase, sem, key) not in self.seen.keys, (self.phase, sem, key)
            self.seen.keys[(self.phase, sem, key)] = self.here[sem]
        if n == 1:
            self.last = (sem, self.here[sem])
        return self.handles(sem), n

    def note(self, sem, key):
        self.seen.keys[(self.phase, sem, key)] = self.here[sem]

    def settle(self):
        self.e.sem_inc(self.handles("settled"), 1)
        self.pending.clear()

    def prime(self, sem, n):
        self.e.sem_inc(self.handles(sem), n)
        self.here[sem] = self.here.get(sem, 0) + n


def program(nc, A, known):
    seen = Counts()
    handles = {}
    ctx = ExitStack()
    with ctx:
        def sem(name):
            if name not in handles:
                handles[name] = ctx.enter_context(nc.semaphore(name))
            return handles[name]

        def sb(name, shape, dt=F32, stack=ctx):
            return stack.enter_context(nc.sbuf_tensor(name, shape, dt))

        x = sb("x", [P, TILES, D_MODEL])
        hl1 = sb("hl1", [P, KC, 2, TOK], F32R)
        xs = sb("xs", [P, KC, 2, DEC], F32R)
        whi = sb("whi", [P, 2, UNIT], F32R)
        wlo = sb("wlo", [P, 2, UNIT], F32R)
        raw = sb("raw", [P, 2, UNIT])
        nsmall = P + 2 * TILES * 64 + 2 * TILES * 8 + TILES * 4 + 4 * DEC + 4 + 4
        small = sb("small", [P, nsmall])
        at = 0

        def take(n):
            nonlocal at
            at += n
            return small[:, at - n:at]

        ident = take(P)
        rcos = take(TILES * 64).rearrange("p (m d) -> p m d", m=TILES)
        rsin = take(TILES * 64).rearrange("p (m d) -> p m d", m=TILES)
        dcos = take(TILES * 8).rearrange("p (m d) -> p m d", m=TILES)
        dsin = take(TILES * 8).rearrange("p (m d) -> p m d", m=TILES)
        zeta = take(TILES * 4).rearrange("p (m h) -> p m h", m=TILES)
        xi = take(4 * DEC).rearrange("p (h i) -> p h i", h=4)
        g32 = take(4)
        lamc = take(4)
        par = sb("par", [P, DEPTH, NVEC + 12 * FT + 2 * DIFF_HD])
        vecs = par[:, :, 0:NVEC]
        conv = par[:, :, NVEC:NVEC + 12 * FT].rearrange("p l (v c) -> p l v c", v=6)
        qkg = par[:, :, NVEC + 12 * FT:].rearrange("p l (v d) -> p l v d", v=2)
        lam = sb("lam", [P, DEPTH])
        sgn = sb("sgn", [2 * DEC, DEPTH])
        gd = sb("gd", [P, DEPTH])
        mhalf = sb("mhalf", [P, 60])
        ss = sb("ss", [P, 60])
        ms = sb("ms", [P, 60])
        rstd = sb("rstd", [P, 60])
        ssr = sb("ssr", [P, TILES, RET_HEADS])
        rest = sb("rest", [DEC, 512])
        odif = sb("odif", [P, TILES, D_MODEL])
        sTs_x = sb("sTs", [DEC, DEC])
        qx = sb("qx", [P, DEC])

        mix = ExitStack()
        mer = sb("mer", [P, KC, TOK], F32, mix)
        with ExitStack() as s:
            qz = sb("qz", [P, 2, 2 * TOK], F32, s)
            kdT = sb("kdT", [P, 2, TOK], F32, s)
            vd = sb("vd", [P, TILES, UC], F32, s)
            rawq = sb("rawq", [P, TILES, UC], F32, s)
            rawk = sb("rawk", [P, TILES, UC], F32, s)
            prob = sb("prob", [P, 2, 1024], F32, s)
            aT = sb("aT", [P, 2, SEQ], F32, s)
            rt = sb("rt", [P, 2, TILES * 4 * 8], F32, s)
            kc_n = sb("kc_n", [P, NT, HW], F32, s)
            vc_n = sb("vc_n", [P, NT, HW], F32, s)
            kcT = sb("kcT", [P, SEQ], F32, s)
            aTs = sb("aTs", [P, TILES, DEC], F32, s)
            aTt = sb("aTt", [P, TILES, DEC], F32, s)
            nmax = sb("nmax", [P, 2, 2], F32, s)
            sums = sb("sums", [P, 2, 2], F32, s)
            rinv = sb("rinv", [P, 4, 3], F32, s)
        with ExitStack() as s:
            tb = sb("tb", [P, KC, TOK], F32, s)
            with ExitStack() as s2:
                decay = sb("decay", [P, 2, SEQ], F32, s2)
                rk = sb("rk", [P, TILES, UC], F32, s2)
                gs = sb("gs", [P, TILES, UC], F32, s2)
                oret = sb("oret", [P, KC, TILES, P], F32, s2)
                sin = sb("sin", [P, RET_DV], F32, s2)
                sout = sb("sout", [P, 2, RET_DV], F32, s2)
            with ExitStack() as s2:
                squares_of_dif = sb("squares_of_dif", [P, TILES, 512], F32, s2)
            hl2 = sb("hl2", [P, KC, 2, TOK], F32R, s)
            xs2 = sb("xs2", [P, KC, 2, DEC], F32R, s)
        with ExitStack() as s:
            sT = sb("sT", [P, 1280], F32, s)
            vr = sb("vr", [P, TILES, UC], F32, s)
            qrT = sb("qrT", [P, TOK], F32, s)
            krT = sb("krT", [P, TOK], F32, s)
            kz = sb("kz", [P, TILES, RET_DK], F32, s)
        mix.close()
        with ExitStack() as s:
            xn = sb("xn", [P, TILES, D_MODEL], F32, s)
        with ExitStack() as s:
            act = sb("act", [P, FB, 2, GP], F32R, s)
            acts = sb("acts", [P, FB, 2, DEC], F32R, s)
            up = sb("up", [P, 2, 2, GP + 2], F32, s)
            ca = sb("ca", [P, 2, GP], F32, s)
            th = sb("th", [P, GP], F32, s)
            af = sb("af", [P, GP], F32, s)
            cs = sb("cs", [P, 4, 2 * FB], F32, s)
            csT = sb("csT", [2 * FB, 4, P], F32, s)
        with ExitStack() as s:
            sb("xn_again", [P, TILES, D_MODEL], F32, s)
            junk = sb("junk", [P, 512], F32, s)

        ps = ctx.enter_context(nc.psum_tensor("ps", [P, 4096], F32))
        BANK = dict(mm0=0, mm1=512, s0=1024, s0b=1536, s1=2048, s1b=2560, t=3072, o=3584)
        UP_BANKS = (("mm0", "mm1", "t", "o"), ("s0", "s1", "s0b", "s1b"))
        NORM_BANKS = ("mm0", "t", "s0", "s1")
        DOWN_BANKS = ("mm0", "mm1", "s0", "s0b", "s1")

        def pv(bank, rows, n, off=0):
            return ps[0:rows, BANK[bank] + off:BANK[bank] + off + n]

        W = dict(A)

        def cols(name, l, col):
            return [(0, UC, W[name][ds(l, 1), :, ds(col, UC)])]

        def units(phase, l, i):
            if phase == "D":
                return [cols("w_in", l, i * UC + COL[n]) for n in ("qd", "kd", "vd", "ga")]
            if phase == "R":
                out = []
                for hh in range(2):
                    q = [(0, P, W["w_in"][ds(l, 1), :, ds(i * 2 * P + hh * P + COL["qr"], P)]),
                         (P, P, W["w_in"][ds(l, 1), :, ds(i * 2 * P + hh * P + COL["kr"], P)])]
                    out += [q, cols("w_in", l, i * 2 * UC + hh * UC + COL["vr"]),
                            cols("w_in", l, i * 2 * UC + hh * UC + COL["gr"])]
                return out
            if phase == "M":
                return ([cols("w_in", l, COL["gb"] + u * UC) for u in range(4)]
                        + [cols(n, l, u * UC) for n in ("w_branch_a", "w_branch_b", "w_out") for u in range(4)])
            if phase == "F":
                out = []
                for j in range(FB):
                    out.append([(0, P, W["w_up"][ds(l, 1), :, ds(i * FB * P + j * P, P)]),
                                (P, P, W["w_up"][ds(l, 1), :, ds(i * FB * P + j * P + D_FF, P)])])
                for hf in range(2):
                    k0 = 0
                    for nk in DOWN[hf]:
                        out.append((nk, W["w_down"][ds(l, 1), ds(i * FB * P + k0 * P, nk * P), hf * 512:hf * 512 + 512]))
                        k0 += nk
                return out
            return []

        UNITS = dict(N=0, D=4, R=6, M=16, F=FB + 7)
        LEN = dict(D=[UNIT] * 4, R=[UNIT] * 6, M=[UNIT] * 16,
                   F=[UNIT] * FB + [nk * 512 for half in DOWN for nk in half])

        def prep_len(phase, j):
            return LEN[phase][j] if j < UNITS.get(phase, 0) else UNIT

        def cache_load(S, e, l, i, hh, name):
            src = A[f"cache_{name}"][ds(l, 1), 0, :, ds(i * 2 + hh, 1), :].rearrange("a (c p) h d -> p (a c h) d", p=P)
            e.dma_start({"k": kc_n, "v": vc_n}[name][:, :, :], src).then_inc(*S.up(f"cache_{name}{hh}", "in", n=16))

        def kv_store(S, e, l, i, name, buf):
            dst = A[f"new_{name}_prompt"][ds(l, 1), 0, :, ds(i * 2, 2), :].rearrange("a (c p) h d -> p (a c) h d", p=P)
            e.dma_start(dst, buf[:, 0:NT, :].rearrange("p c (h d) -> p c h d", h=2)).then_inc(*S.up("kv_out", (name, 0), n=16))
            dst = A[f"new_{name}_sample"][ds(l, 1), 0, :, ds(i * 2, 2), :].rearrange("a s h d -> s a h d")
            e.dma_start(dst, buf[0:DEC, NT:TILES, :].rearrange("p c (h d) -> p c h d", h=2)).then_inc(
                *S.up("kv_out", (name, 4), n=16))

        def sync_program(S):
            e = S.e

            def load_unit(j, what):
                e.wait_ge(*S.at("w_ready", k=j - 2))
                slot = f"raw{j % 2}"
                if isinstance(what, tuple):
                    nk, src = what
                    v = src.rearrange("a (c p) n -> p (a c) n", p=P)
                    r = raw[:, j % 2, 0:nk * 512].rearrange("p (c n) -> p c n", c=nk)
                    cut = [(0, nk - 1), (nk - 1, nk)]
                    for a, b in cut:
                        e.dma_start(r[:, a:b, :], v[:, a:b, :]).then_inc(*S.up(slot, n=16))
                    return
                r = raw[:, j % 2, :].rearrange("p (c n) -> p c n", c=KC)
                if len(what) == 2:
                    for c0, n, src in what:
                        e.dma_start(r[:, :, c0:c0 + n], src.rearrange("a (c p) n -> p (a c) n", p=P)).then_inc(
                            *S.up(slot, n=16))
                else:
                    v = what[0][2].rearrange("a (c p) n -> p (a c) n", p=P)
                    for a in (0, KC // 2):
                        e.dma_start(r[:, a:a + KC // 2, :], v[:, a:a + KC // 2, :]).then_inc(*S.up(slot, n=16))

            e.dma_start(prob[:, :, 0:4 * DIFF_HD], A["lambdas"]).then_inc(*S.up("lambdas", "in", n=16))
            with S.layers() as l:
                for phase, _ in ORDER:
                    with S.body(phase) as i:
                        us = units(phase, l, i)
                        assert len(us) == UNITS[phase]
                        if phase == "D":
                            for j, what in enumerate(us):
                                load_unit(j, what)
                                if j == 1:
                                    e.wait_ge(*S.at("o_ready", k=0))
                                    e.wait_ge(*S.at("t_ready", k=0))
                                    e.wait_ge(*S.at("pool_step", k=0))
                                    e.wait_ge(*S.at("act_free_o", k=0))
                                    cache_load(S, e, l, i, 0, "k")
                                    cache_load(S, e, l, i, 0, "v")
                        elif phase == "R":
                            for j, what in enumerate(us):
                                load_unit(j, what)
                                if j == 1:
                                    e.wait_ge(*S.at("pe_step", k=0))
                                    e.wait_ge(*S.at("dve_step", k=0))
                                    e.wait_ge(*S.at("act_step", k=0))
                                    e.wait_ge(*S.at("act_free_t", k=0))
                                    e.wait_ge(*S.at("dve_free_t", k=0))
                                    e.wait_ge(*S.at("dve_free_o", k=0))
                                    e.wait_ge(*S.at("act_free_o", k=0))
                                    e.dma_start(decay[:, :, :].rearrange("p h n -> p (h n)"),
                                                         A["tab_decay"][:, ds(i * 2 * SEQ, 2 * SEQ)]).then_inc(
                                                             *S.up("decay_in", "d", n=16))
                                if j in (1, 4):
                                    hh = j // 3
                                    e.wait_ge(*(S.at("dve_free_s1", ("snew", 0)) if hh else S.at("dve_free_s1", k=0)))
                                    e.dma_start(sin[:, :], A["state_ret"][ds(l, 1), 0, ds(i * 2 + hh, 1)]
                                             .rearrange("a h d e -> d (a h e)")).then_inc(*S.up("sin_in", ("s", hh), n=16))
                        else:
                            for j, what in enumerate(us):
                                load_unit(j, what)
            e.wait_ge(*S.at("w_ready", k=-2))
            for a in (0, KC // 2):
                e.dma_start(raw[:, 0, a * UC:(a + KC // 2) * UC].rearrange("p (c n) -> p c n", c=KC // 2),
                                     A["w_in"][0, a * P:(a + KC // 2) * P, 0:UC].rearrange("(c p) n -> p c n", p=P)).then_inc(
                                         *S.up("raw0", n=16))
            for hf in range(2):
                for m in (NT, 0, 1, 2, 3):
                    dst = A["y_prompt"][0, m * P:(m + 1) * P, :] if m < NT else A["y_sample"][0]
                    e.wait_ge(*S.at("dve_free_" + DOWN_BANKS[m], k=hf - 1))
                    e.dma_start(dst[:, hf * 512:(hf + 1) * 512], x[0:ROWS[m], m, hf * 512:(hf + 1) * 512]).then_inc(
                        *S.up("y_out", n=16))
            e.wait_ge(*S.at("y_out", k=2 * TILES * 16))
            e.wait_ge(*S.at("kv_out", k=0))
            e.wait_ge(*S.at("st_out0", k=0))
            e.wait_ge(*S.at("st_out1", k=0))
            e.wait_ge(*S.at("cs_out", k=0))
            e.wait_ge(*S.at("w_ready", k=0))

        def pool_program(S):
            e = S.e

            def lo(phase, j):
                n = prep_len(phase, j)
                s = j % 2
                e.wait_ge(*S.at("hi_ready", k=j)) if phase != "P" else e.wait_ge(*S.at("hi_ready", ("hi", 0)))
                e.tensor_tensor(wlo[:, s, 0:n], raw[:, s, 0:n], whi[:, s, 0:n].bitcast(F32), ALU.subtract).then_inc(
                    *S.up("w_ready", ("lo", j)))

            def power(n, key, at=0):
                e.wait_ge(*S.at("dve_step", ("ms", key)))
                e.tensor_tensor(rstd[:, at:at + n], ms[:, at:at + n], mhalf[:, at:at + n], ALU.pow).then_inc(
                    *S.up("pool_step", ("rstd", key)))

            S.prime("w_ready", 2)
            S.prime("pool_step", 1)
            e.memset(mhalf[:, :], -0.5).then_inc(*S.up("pool_step"))
            lo("P", 0)
            with S.layers() as l:
                with S.body("N"):
                    power(5, "n")
                    for s in ("mm_ready", "act_step", "dve_step"):
                        e.wait_ge(*S.at(s, k=0))
                    S.settle()
                    e.memset(rawq[:, NT, :], 0.0).then_inc(*S.up("pool_step"))
                    e.memset(rawk[:, NT, :], 0.0).then_inc(*S.up("pool_step"))
                    e.memset(odif[:, NT, :], 0.0).then_inc(*S.up("pool_step"))
                    e.memset(nmax[:, :, :], 0.0).then_inc(*S.up("pool_step"))
                    e.wait_ge(*S.at("s_ready", ("norm", KC - 1)))
                    e.wait_ge(*S.own())
                    S.settle()
                    e.memset(qz[DIFF_HD:P, :, 0:TOK], 0.0).then_inc(*S.up("pool_step"))
                    e.wait_ge(*S.own())
                    S.settle()
                    e.memset(qz[0:DIFF_HD, :, TOK:2 * TOK], 0.0).then_inc(*S.up("pool_step"))
                with S.body("D") as p:
                    lo("D", 1)
                    lo("D", 2)
                    power(20, "q")
                    lo("D", 3)
                    power(20, "k")
                    lo("D", 4)
                with S.body("R") as i:
                    for hh in range(2):
                        for j in range(3 * hh + 1, 3 * hh + 4):
                            lo("R", j)
                with S.body("M"):
                    lo("M", 1)
                    power(20, "ret", 40)
                    lo("M", 2)
                    power(20, "dif0", 0)
                    power(20, "dif1", 20)
                    for j in range(3, 17):
                        lo("M", j)
                        if j == 16:
                            power(5, "n")
                with S.body("F") as f:
                    for j in range(FB):
                        lo("F", j + 1)
                    for j in range(FB, UNITS["F"]):
                        lo("F", j + 1)

        def pe_program(S):
            e = S.e
            free = {}

            def acquire(bank, act=0, dve=0):
                if bank not in free:
                    free[bank] = {"act": 0, "dve": 0, "last": ("act", "dve")}
                b = free[bank]
                for who in b["last"]:
                    e.wait_ge(*S.at(f"{who}_free_{bank}", k=b[who]))
                b["last"] = tuple(w for w, n in (("act", act), ("dve", dve)) if n)
                b["act"] += act
                b["dve"] += dve

            def start():
                free.clear()

            tile = [0]

            def mm_bank():
                tile[0] += 1
                return f"mm{(tile[0] - 1) % 2}"

            def ready(ins, *keys):
                ins.then_inc(*S.up("mm_ready", keys[0]))
                for k in keys[1:]:
                    S.note("mm_ready", k)

            def chunk_ready(c):
                e.wait_ge(*S.at(f"dve_free_{NORM_BANKS[c % 4]}", k=0 if c >= 4 else -1))

            def t_tile(j, col, half, X, act=0, dve=0, bank=None, chunk=None):
                bank = bank or mm_bank()
                acquire(bank, act, dve)
                out = pv(bank, P, HALF)
                for c in range(KC):
                    w0 = c * UC + col * P
                    hi, lo = (X[:, c, v, half * HALF:(half + 1) * HALF] for v in (0, 1))
                    wh, wl = whi[:, j % 2, w0:w0 + P], wlo[:, j % 2, w0:w0 + P]
                    if chunk:
                        chunk(c)
                    e.matmul(out, wh, hi, start=(c == 0), stop=False)
                    e.matmul(out, wh, lo, start=False, stop=False)
                    ins = e.matmul(out, wl, hi, start=False, stop=(c == KC - 1))
                keys = [("T", j, col, half)] + ([("end", j)] if col and half else [])
                ready(ins, *keys)

            def n_tile(j, m, X, XS, act=0, dve=0, chunk=None):
                bank = mm_bank()
                acquire(bank, act, dve)
                if m < NT:
                    out = pv(bank, P, UC)
                    for c in range(KC):
                        hi, lo = (X[:, c, v, m * P:(m + 1) * P] for v in (0, 1))
                        wh, wl = (w[:, j % 2, c * UC:(c + 1) * UC] for w in (whi, wlo))
                        if chunk:
                            chunk(c)
                        e.matmul(out, hi, wh, start=(c == 0), stop=False)
                        e.matmul(out, hi, wl, start=False, stop=False)
                        ins = e.matmul(out, lo, wh, start=False, stop=(c == KC - 1))
                    ready(ins, ("N", j, m))
                else:
                    out = pv(bank, 2 * DEC, UC)
                    for c in range(KC):
                        st = XS[:, c, :, :].rearrange("p v s -> p (v s)")
                        e.matmul(out, st, whi[:, j % 2, c * UC:(c + 1) * UC], start=(c == 0), stop=False)
                        ins = e.matmul(out, st, wlo[:, j % 2, c * UC:(c + 1) * UC], start=False, stop=(c == KC - 1))
                    ready(ins, ("N", j, m), ("end", j))

            def n_unit(j, X, XS, dve=False, before=None, after=None, chunk=None):
                e.wait_ge(*S.at("w_ready", k=j))
                for m in range(TILES):
                    if before:
                        before(m)
                    if m == NT:
                        n_tile(j, m, X, XS, act=1, dve=1)
                    else:
                        n_tile(j, m, X, XS, act=int(not dve), dve=int(dve), chunk=chunk if m == 0 else None)
                    if after:
                        after(m)

            def feature_transposes(src, bank, key, act, dve):
                acquire(bank, act, dve)
                for m in range(TILES):
                    ins = e.transpose(pv(bank, P, ROWS[m], m * P), src(m), ident[0:ROWS[m], 0:ROWS[m]])
                ins.then_inc(*S.up("s_ready", key))

            def norm(key):
                acquire("mm1")
                acquire("o")
                acquire("s0b")
                acquire("s1b")
                for c in range(KC):
                    if c in (0, 4):
                        e.wait_ge(*S.at("act_step", ("xn", key, c // 4)))
                        e.wait_ge(*S.at("dve_step", ("xn", key, c // 4)))
                    feature_transposes(lambda m: xn[0:ROWS[m], m, c * P:(c + 1) * P], NORM_BANKS[c % 4], ("norm", c), 1, 1)

            S.prime("mm_ready", 1)
            S.prime("pe_step", 1)
            S.prime("o_ready", 1)
            S.prime("t_ready", 1)
            S.prime("s_ready", 1)
            e.wait_ge(*S.at("tables", "in"))
            with S.layers():
                with S.body("N"):
                    start()
                    norm("n")
                with S.body("D"):
                    start()
                    tile[0] = 0
                    n_unit(0, hl1, xs, before=lambda m: e.wait_ge(*S.at("act_step", k=0)) if m == NT else None, chunk=chunk_ready)

                    def cached_keys(hh):
                        e.wait_ge(*S.at(f"cache_k{hh}", "in"))
                        acquire("t", act=1)
                        for c in range(NT):
                            ins = e.transpose(pv("t", P, P, c * P), kc_n[:, c, :], ident)
                        ins.then_inc(*S.up("t_ready", ("kc", hh)))

                    n_unit(1, hl1, xs)

                    def queries(m):
                        if m == 1:
                            e.wait_ge(*S.at("dve_step", ("rope", "q")))
                            for hh in range(2):
                                feature_transposes(lambda m: rawq[0:ROWS[m], m, hh * P:(hh + 1) * P], f"s{hh}", ("q", hh), 1, 2)

                    n_unit(2, hl1, xs, after=queries)
                    cached_keys(0)
                    e.wait_ge(*S.at("w_ready", k=3))
                    t_tile(3, 0, 0, hl1, act=1)
                    for hh in range(2):
                        if hh == 0:
                            e.wait_ge(*S.at("dve_step", ("rope", "k")))
                        feature_transposes(lambda m: rawk[0:ROWS[m], m, hh * P:(hh + 1) * P], f"s{hh}", ("k", hh), 1, 0)
                    steps = [(hh, ib) for hh in range(2) for ib in range(TILES)]

                    def scores(n):
                        hh, ib = steps[n]
                        bank = f"s{n % 2}"
                        if ib < NT:
                            acquire(bank, act=1)
                            if n == 0:
                                e.wait_ge(*S.at("act_free_s0", ("q", 0)))
                                e.wait_ge(*S.at("dve_free_s0", ("q1", 0)))
                                e.wait_ge(*S.at("act_free_s0", ("k", 0)))
                            if n == 5:
                                e.wait_ge(*S.at("dve_free_s1", ("q1", 1)))
                                e.wait_ge(*S.at("act_free_s1", ("k", 1)))
                            keys = (ib + 1) * P
                            for c in range(2):
                                o = c * (TOK + DEC) + ib * P
                                ins = e.matmul(pv(bank, P, keys, c * 512), qz[:, hh, o:o + P], kdT[:, hh, 0:keys],
                                               start=True, stop=True)
                        else:
                            acquire(bank, act=1)
                            e.wait_ge(*S.at("act_free_t", ("kc", hh)))
                            st = qz[:, hh, SEQ:SEQ + 2 * DEC]
                            e.matmul(pv(bank, 2 * DEC, PAST), st, kcT[:, :], start=True, stop=True)
                            ins = e.matmul(pv(bank, 2 * DEC, DEC, PAST), st, kdT[:, hh, SEQ:TOK], start=True, stop=True)
                        ins.then_inc(*S.up("s_ready", ("s", n)))

                    def weighted(n):
                        hh, ib = steps[n]
                        e.wait_ge(*S.at("dve_step", ("a", n)))
                        if ib < NT:
                            acquire("t", act=1)
                            for jb in range(ib + 1):
                                ins = e.transpose(pv("t", P, P, jb * P), prob[:, n % 2, jb * P:(jb + 1) * P], ident)
                            ins.then_inc(*S.up("t_ready", ("a", n)))
                        else:
                            acquire("t", act=2, dve=2)
                            S.settle()
                            for c in range(TILES):
                                ins = e.transpose(pv("t", ROWS[c], 2 * DEC, c * 2 * DEC),
                                                  prob[0:2 * DEC, n % 2, c * P:c * P + ROWS[c]], ident[0:2 * DEC, 0:2 * DEC])
                            ins.then_inc(*S.up("t_ready", ("a", n)))

                    def values(n):
                        hh, ib = steps[n]
                        acquire("o", act=1)
                        if ib < NT:
                            e.wait_ge(*S.at("act_free_t", ("aT", n)))
                            if n == 0:
                                e.wait_ge(*S.at("act_free_mm1", ("v", 3)))
                                e.wait_ge(*S.at("act_free_mm0", ("v", 2)))
                            for jb in range(ib + 1):
                                ins = e.matmul(pv("o", P, HW), aT[:, n % 2, jb * P:(jb + 1) * P],
                                               vd[:, jb, hh * HW:(hh + 1) * HW], start=(jb == 0), stop=(jb == ib))
                        else:
                            e.wait_ge(*S.at("dve_free_t", ("aT", n)))
                            e.wait_ge(*S.at("dve_free_mm0", ("rest", "v")))
                            e.wait_ge(*S.at(f"cache_v{hh}", "in"))
                            for c in range(TILES):
                                r = ROWS[c]
                                v = vc_n[:, c, :] if c < NT else vd[0:DEC, NT, hh * HW:(hh + 1) * HW]
                                ins = e.matmul(pv("o", DEC, HW), aTs[0:r, c, :], v, start=(c == 0), stop=(c == NT))
                        ins.then_inc(*S.up("o_ready", (hh, ib)))

                    gate_at = [KC]

                    def gate_chunks(n):
                        for g in range(gate_at[0], gate_at[0] + n):
                            t, c = g // KC, g % KC
                            if c == 0:
                                gate_at.append(mm_bank())
                                acquire(gate_at[-1], act=1)
                            out = pv(gate_at[-1], P, HALF)
                            w0 = c * UC + (t // 2) * P
                            hi, lo = (hl1[:, c, v, (t % 2) * HALF:(t % 2 + 1) * HALF] for v in (0, 1))
                            wh, wl = whi[:, 1, w0:w0 + P], wlo[:, 1, w0:w0 + P]
                            e.matmul(out, wh, hi, start=(c == 0), stop=False)
                            e.matmul(out, wh, lo, start=False, stop=False)
                            ins = e.matmul(out, wl, hi, start=False, stop=(c == KC - 1))
                            if c == KC - 1:
                                ready(ins, ("T", 3, t // 2, t % 2), *([("end", 3)] if t == 3 else []))
                        gate_at[0] += n

                    scores(0)
                    scores(1)
                    for n in range(10):
                        if n + 2 < 10:
                            scores(n + 2)
                        gate_chunks(GATE_SHARE[n])
                        weighted(n)
                        if n:
                            values(n - 1)
                        if n == 5:
                            cached_keys(1)
                    values(9)
                with S.body("R"):
                    start()
                    tile[0] = 0
                    for hh in range(2):
                        u = 3 * hh
                        n_unit(u, hl1, xs)
                        n_unit(u + 1, hl1, xs)
                        e.wait_ge(*S.at("dve_step", ("rope", hh)))
                        for v in range(2):
                            feature_transposes(lambda m: rk[0:ROWS[m], m, v * P:(v + 1) * P], f"s{v}", ("qk", hh, v), 1, 0)
                        e.wait_ge(*S.at("w_ready", k=u + 2))

                        def rscores(jb):
                            n = SEQ - jb * P
                            if jb == 0:
                                e.wait_ge(*S.at("act_free_s0", ("qk", hh, 0)))
                                e.wait_ge(*S.at("act_free_s1", ("qk", hh, 1)))
                                acquire("s0", dve=2)
                            if jb == 2:
                                acquire("s1", dve=2)
                            bank = "s0" if jb < 2 else "s1"
                            e.matmul(pv(bank, P, n, (jb % 2) * 512), krT[:, jb * P:(jb + 1) * P], qrT[:, jb * P:SEQ],
                                              start=True, stop=True).then_inc(*S.up("s_ready", ("ret", hh, jb)))

                        def outs(ib):
                            bank = "to"[ib % 2]
                            acquire(bank, act=1, dve=1)
                            e.wait_ge(*S.at(("dve_free_s0", "dve_free_s1")[ib // 2], ("sT", hh, ib)))
                            for jb in range(ib + 1):
                                o = SOFF[jb] + (ib - jb) * P
                                ins = e.matmul(pv(bank, P, RET_DV), sT[:, o:o + P], vr[:, jb, :], start=(jb == 0), stop=(jb == ib))
                            ins.then_inc(*S.up(("t_ready", "o_ready")[ib % 2], ("o", hh, ib)))

                        j = u + 2
                        n_tile(j, 0, hl1, xs, dve=1, act=1)
                        rscores(0)
                        rscores(1)
                        n_tile(j, 1, hl1, xs, dve=1, act=1)
                        rscores(2)
                        rscores(3)
                        n_tile(j, 2, hl1, xs, dve=1, act=1)
                        outs(0)
                        outs(1)
                        acquire("s0", dve=1)
                        S.settle()
                        e.matmul(pv("s0", DEC, DEC), krT[:, SEQ:TOK], qrT[:, SEQ:TOK], start=True, stop=True).then_inc(
                            *S.up("s_ready", ("rets", hh)))
                        n_tile(j, 3, hl1, xs, dve=1, act=1)
                        outs(2)
                        outs(3)
                        n_tile(j, 4, hl1, xs, act=1, dve=2)
                        acquire("t", act=1, dve=1)
                        e.wait_ge(*S.at("dve_free_s0", ("sTs", hh)))
                        e.wait_ge(*S.at("sin_in", ("s", hh)))
                        S.settle()
                        e.matmul(pv("t", DEC, RET_DV), sTs_x[:, :], vr[0:DEC, NT, :], start=True, stop=False)
                        e.matmul(pv("t", DEC, RET_DV), qx[:, :], sin[:, :], start=False, stop=True).then_inc(
                            *S.up("t_ready", ("os", hh)))
                        acquire("o", act=1)
                        e.wait_ge(*S.at("dve_step", ("kz", hh)))
                        for m in range(NT):
                            ins = e.matmul(pv("o", P, RET_DV), kz[:, m, :], vr[:, m, :], start=(m == 0), stop=(m == NT - 1))
                        ins.then_inc(*S.up("o_ready", ("sfin", hh)))
                        acquire("s1", dve=1)
                        e.matmul(pv("s1", P, RET_DV), kz[0:DEC, NT, :], vr[0:DEC, NT, :], start=True, stop=True).then_inc(
                            *S.up("s_ready", ("snew", hh)))
                with S.body("M"):
                    start()
                    tile[0] = 0

                    def t_unit(j, X, act=0, dve=0, before=None):
                        e.wait_ge(*S.at("w_ready", k=j))
                        for t in range(4):
                            if before:
                                before(t)
                            t_tile(j, t // 2, t % 2, X, act, dve)

                    def ret_chunk(c):
                        if c == 0:
                            e.wait_ge(*S.at("dve_step", ("oret", "done")))
                        feature_transposes(lambda m: oret[0:ROWS[m], c, m, :], f"s{c % 2}", ("ret", c), 1, 1)

                    for j in range(4):
                        t_unit(j, hl1, act=1, before=(lambda t, j=j: ret_chunk(4 * (j - 2) + t)) if j >= 2 else None)
                    e.wait_ge(*S.at("dve_free_s0", ("lo", "ret", KC - 2)))
                    e.wait_ge(*S.at("dve_free_s1", ("lo", "ret", KC - 1)))

                    def dif_chunk(c):
                        if c in (0, 4):
                            e.wait_ge(*S.at("dve_step", ("odif", c // 4)))
                        feature_transposes(lambda m: odif[0:ROWS[m], m, c * P:(c + 1) * P], f"s{c % 2}", ("dif", c), 1, 1)

                    for u in range(4):
                        t_unit(4 + u, hl2, dve=1, before=lambda t, u=u: None if t % 2 else dif_chunk(2 * u + t // 2))
                    e.wait_ge(*S.at("dve_free_s1", ("lo", "dif", KC - 1)))
                    e.wait_ge(*S.at("dve_free_s0", ("lo", "dif", KC - 2)))
                    for u in range(4):
                        t_unit(8 + u, hl1, dve=1)

                    def merged(m):
                        if m == 0:
                            e.wait_ge(*S.at("dve_step", ("lo", "mer", 2)))
                        if m == 2:
                            e.wait_ge(*S.at("dve_step", ("lo", "mer", 3)))
                        if m == NT:
                            e.wait_ge(*S.at("act_step", ("xs", "mer")))

                    for u in range(4):
                        n_unit(12 + u, hl2, xs2, dve=True, before=merged if u == 0 else None)
                    norm("n")
                with S.body("F"):
                    start()
                    tile[0] = 0
                    for j in range(FB):
                        e.wait_ge(*S.at("w_ready", k=j))
                        for t in range(4):
                            reads = 2 if t % 2 else 1
                            t_tile(j, t // 2, t % 2, hl1, act=reads * (t < 2), dve=reads * (t >= 2), bank=UP_BANKS[j % 2][t],
                                   chunk=chunk_ready if j == 0 and t == 0 else None)

                    def conv_rows():
                        acquire("t", dve=1)
                        e.wait_ge(*S.at("dve_step", ("cs", FB - 1)))
                        for q in range(4):
                            ins = e.transpose(pv("t", 2 * FB, P, q * P), cs[:, q, :], ident)
                        ins.then_inc(*S.up("t_ready", "cs"))

                    j = FB
                    for hf in range(2):
                        kc = 0
                        for n, nk in enumerate(DOWN[hf]):
                            e.wait_ge(*S.at("w_ready", k=j))
                            if hf == 0:
                                e.wait_ge(*S.at("act_step", ("acts", n)))
                                e.wait_ge(*S.at("dve_step", ("alo", kc + nk - 1)))
                            for q in range(nk):
                                last = kc == FB - 1
                                wh, wl = (w[:, j % 2, q * 512:(q + 1) * 512] for w in (whi, wlo))
                                if kc == 0:
                                    acquire(DOWN_BANKS[NT], act=1, dve=1)
                                st = acts[:, kc, :, :].rearrange("p v s -> p (v s)")
                                out = ps[0:2 * DEC, 2048:2560]
                                e.matmul(out, st, wh, start=(kc == 0), stop=False)
                                ins = e.matmul(out, st, wl, start=False, stop=last)
                                if last:
                                    ready(ins, ("down", hf, NT))
                                for m in range(NT):
                                    if kc == 0:
                                        acquire(DOWN_BANKS[m], dve=1)
                                    out = ps[:, m * 512:(m + 1) * 512]
                                    hi, lo = (act[:, kc, v, m * P:(m + 1) * P] for v in (0, 1))
                                    e.matmul(out, hi, wh, start=(kc == 0), stop=False)
                                    e.matmul(out, hi, wl, start=False, stop=False)
                                    ins = e.matmul(out, lo, wh, start=False, stop=last)
                                    end = [("end", j)] if q == nk - 1 and m == NT - 1 else []
                                    if last:
                                        ready(ins, ("down", hf, m), *end)
                                    elif end:
                                        ready(ins, *end)
                                kc += 1
                            j += 1
                        if hf == 0:
                            conv_rows()

        SOFF = [0, 512, 896, 1152]
        GATE_SHARE = (3, 2, 2, 2, 1, 2, 2, 2, 4, 4)
        GATE_AT = [next(n for n in range(10) if sum(GATE_SHARE[:n + 1]) >= KC * t) for t in (1, 2, 3)]

        def act_program(S):
            e = S.e

            def hi(phase, j, part):
                n = prep_len(phase, j)
                s = j % 2
                if part == 0:
                    if phase != "P":
                        if j >= 2:
                            e.wait_ge(*S.at("mm_ready", ("end", j - 2)))
                        else:
                            e.wait_ge(*S.at("mm_ready", k=0))
                    e.wait_ge(*S.at(f"raw{s}", k=32 * (j // 2 + 1) if phase != "P" else 32))
                a, b = (0, n // 2) if part == 0 else (n // 2, n)
                if part == 0:
                    e.activation(whi[:, s, a:b], raw[:, s, a:b], ACT.Copy)
                else:
                    e.activation(whi[:, s, a:b], raw[:, s, a:b], ACT.Copy).then_inc(*S.up("hi_ready", ("hi", j)))

            def prep(phase, j):
                hi(phase, j, 0)
                hi(phase, j, 1)

            def rest_copy(bank, key, prev, n=UC):
                e.wait_ge(*S.at("mm_ready", key))
                e.wait_ge(*(S.at(*prev) if prev else S.at("dve_step", k=0)))
                e.wait_ge(*S.own())
                e.activation(rest[:, 0:n], ps[DEC:2 * DEC, BANK[bank]:BANK[bank] + n], ACT.Copy).then_inc(
                    *S.up(f"act_free_{bank}", ("rest",) + key))

            def squares_of_x(m, c0, n, junk, at, key):
                r = ROWS[m]
                e.wait_ge(*S.own())
                e.activation(junk[0:r], x[0:r, m, c0:c0 + n], ACT.Square, accum_out=ss[0:r, at:at + 1]).then_inc(
                    *S.up("act_step", key=key))

            def norm(key):
                e.wait_ge(*S.at("pool_step", ("rstd", key)))
                for half in range(2):
                    h = slice(half * 512, (half + 1) * 512)
                    for m in (1, 3):
                        e.activation(xn[:, m, h], x[:, m, h], ACT.Copy, scale=rstd[:, m:m + 1]).then_inc(
                            *S.up("act_step", key=("xn", key, half) if m == 3 else None))
                for c in range(KC):
                    bank = NORM_BANKS[c % 4]
                    g = vecs[:, ds(S.layer, 1), (c if S.phase == "N" else KC + c):(c if S.phase == "N" else KC + c) + 1].rearrange(
                        "p a b -> p (a b)")
                    e.wait_ge(*S.at("s_ready", ("norm", c)))
                    if c == 0:
                        e.wait_ge(*(S.at("mm_ready", k=0) if S.phase == "N" else S.at("mm_ready", ("end", 15))))
                    e.wait_ge(*S.own())
                    S.settle()
                    e.activation(hl1[:, c, 0, :], pv(bank, P, TOK), ACT.Copy, scale=g).then_inc(
                        *S.up(f"act_free_{bank}", ("norm", c)))
                for c in range(4, KC):
                    e.wait_ge(*S.at(f"dve_free_{NORM_BANKS[c % 4]}", ("norm", c)))
                e.wait_ge(*S.own())
                e.activation(xs[:, :, :, :].rearrange("p c v s -> p (c v) s"),
                             hl1[:, :, :, SEQ:TOK].rearrange("p c v s -> p (c v) s"), ACT.Copy).then_inc(
                                 *S.up("act_step", key=("xs", key)))

            for b in BANK:
                S.prime(f"act_free_{b}", 1)
            S.prime("act_step", 1)
            for s in ("kv_out", "st_out0", "st_out1", "cs_out"):
                S.prime(s, 16)
            S.prime("hi_ready", 1)
            for m in range(TILES):
                src = A["x_prompt"][0, m * P:(m + 1) * P, :] if m < NT else A["x_sample"][0]
                e.dma_start(x[0:ROWS[m], m, :], src).then_inc(*S.up(f"x_in{m}", "x", n=16))
            e.dma_start(small[:, :], A["tab_small"]).then_inc(*S.up("tables", "in", n=16))
            e.dma_start(par[:, :, :], A["params"]).then_inc(*S.up("params", "in", n=16))
            e.wait_ge(*S.at("dve_step", "lamp"))
            e.activation(aT[:, 0, 0:2 * DEPTH], aT[:, 0, 8:8 + 2 * DEPTH], ACT.Exp).then_inc(*S.up("act_step", key="lexp"))
            for m in range(TILES):
                e.wait_ge(*S.at(f"x_in{m}", "x"))
                squares_of_x(m, 0, 512, qz[:, 0, 0:512], 40 + 2 * m, None)
                if m in (1, 2):
                    e.wait_ge(*S.at("raw0", k=32))
                    hi("P", 0, m - 1)
            e.wait_ge(*S.at("params", "in"))
            with S.layers() as l:
                with S.body("N"):
                    for m in (NT, 0, 1, 2, 3):
                        e.wait_ge(*S.at("dve_free_" + DOWN_BANKS[m], k=0))
                        squares_of_x(m, 512, 512, junk[:, 0:512], 41 + 2 * m, ("ssq", m))
                    norm("n")
                with S.body("D") as p:
                    prev = None
                    t = 0
                    for u, (name, buf) in enumerate((("q", rawq), ("k", rawk), ("v", vd))):
                        for m in range(TILES):
                            bank = f"mm{t % 2}"
                            t += 1
                            if m == 0:
                                e.wait_ge(*S.at("dve_step", k=0))
                                e.wait_ge(*S.at("dve_free_o", k=0))
                                e.wait_ge(*S.at("kv_out", k=0))
                                e.wait_ge(*S.at("o_ready", k=0))
                                hi("D", u + 1, 0)
                                hi("D", u + 1, 1)
                            if m < NT:
                                e.wait_ge(*S.at("mm_ready", ("N", u, m)))
                                e.activation(buf[:, m, :], pv(bank, P, UC), ACT.Copy).then_inc(
                                    *S.up(f"act_free_{bank}", (name, m)))
                            else:
                                rest_copy(bank, ("N", u, m), prev)
                                prev = (f"dve_free_{bank}", ("rest", name))
                            if u == 1 and m == 0:
                                e.wait_ge(*S.at("dve_free_mm0", ("rest", "q")))
                                e.wait_ge(*S.own())
                                e.activation(prob[:, :, :].rearrange("p a b -> p (a b)")[:, 0:TILES * UC],
                                                rawq[:, :, :].rearrange("p a b -> p (a b)"), ACT.Square).then_inc(
                                                    *S.up("act_step", key=("sq", "q")))
                            if u == 2 and m == 0:
                                e.wait_ge(*S.at("dve_free_mm1", ("rest", "k")))
                                e.wait_ge(*S.at("dve_step", ("ss", "q")))
                                e.wait_ge(*S.own())
                                e.activation(prob[:, :, :].rearrange("p a b -> p (a b)")[:, 0:TILES * UC],
                                                rawk[:, :, :].rearrange("p a b -> p (a b)"), ACT.Square).then_inc(
                                                    *S.up("act_step", key=("sq", "k")))
                            if u == 2 and m == 2:
                                e.wait_ge(*S.at("pool_step", k=0))
                                for hh in range(2):
                                    e.wait_ge(*S.at("s_ready", ("q", hh)))
                                    e.activation(qz[0:DIFF_HD, hh, 0:TOK], pv(f"s{hh}", DIFF_HD, TOK), ACT.Copy,
                                                 scale=DIFF_HD ** -0.5).then_inc(*S.up(f"act_free_s{hh}", ("q", hh)))
                    e.wait_ge(*S.at("t_ready", ("kc", 0)))
                    e.activation(kcT[:, :], pv("t", P, PAST), ACT.Copy).then_inc(*S.up("act_free_t", ("kc", 0)))
                    cache_load(S, e, l, p, 1, "k")
                    def gate(tt):
                        bank = f"mm{(15 + tt) % 2}"
                        e.wait_ge(*S.at("mm_ready", ("T", 3, tt // 2, tt % 2)))
                        e.wait_ge(*S.own())
                        S.settle()
                        e.activation(mer[:, ds(p * 2 + tt // 2, 1), (tt % 2) * HALF:(tt % 2 + 1) * HALF].rearrange("p a b -> p (a b)"),
                                        pv(bank, P, HALF), ACT.Tanh, scale=0.5).then_inc(*S.up(f"act_free_{bank}", ("ga", tt)))

                    steps = [(hh, ib) for hh in range(2) for ib in range(TILES)]

                    def exps(n):
                        hh, ib = steps[n]
                        b = n % 2
                        e.wait_ge(*S.at("dve_step", ("max", n)))
                        if n >= 2:
                            e.wait_ge(*S.at("t_ready", ("a", n - 2)))
                        e.wait_ge(*S.own())
                        if ib < NT:
                            k = (ib + 1) * P
                            for c in range(2):
                                src = pv(f"s{b}", P, k, c * 512)
                                dst = prob[:, b, c * 512:c * 512 + k]
                                i = e.activation(dst, src, ACT.Exp, bias=nmax[:, b, c:c + 1], accum_out=sums[:, b, c:c + 1])
                                if c == 0:
                                    i.then_inc(*S.up("act_step"))
                                else:
                                    i.then_inc(*S.up(f"act_free_s{b}", ("exp", n)))
                        else:
                            e.activation(prob[0:2 * DEC, b, 0:TOK], pv(f"s{b}", 2 * DEC, TOK), ACT.Exp,
                                            bias=nmax[0:2 * DEC, b, 0:1], accum_out=sums[0:2 * DEC, b, 0:1]).then_inc(
                                                *S.up(f"act_free_s{b}", ("exp", n)))

                    def turn(n):
                        hh, ib = steps[n]
                        e.wait_ge(*S.at("t_ready", ("a", n)))
                        if n >= 2:
                            e.wait_ge(*S.at("o_ready", steps[n - 2]))
                        e.wait_ge(*S.own())
                        if ib < NT:
                            e.activation(aT[:, n % 2, 0:(ib + 1) * P], pv("t", P, (ib + 1) * P), ACT.Copy).then_inc(
                                *S.up("act_free_t", ("aT", n)))
                        else:
                            v = pv("t", P, TILES * 2 * DEC).rearrange("p (c n) -> p c n", c=TILES)
                            e.activation(aTt[:, 0:NT, :], v[:, 0:NT, DEC:2 * DEC], ACT.Copy).then_inc(*S.up("act_free_t"))
                            e.activation(aTt[0:DEC, NT, :], v[0:DEC, NT, DEC:2 * DEC], ACT.Copy).then_inc(
                                *S.up("act_free_t", ("aTt", n)))

                    def out(n):
                        hh, ib = steps[n]
                        r = ROWS[ib]
                        e.wait_ge(*S.at("o_ready", (hh, ib)))
                        e.wait_ge(*S.own())
                        S.settle()
                        dst = odif[0:r, ib, ds(p * 2 * HW + hh * HW, HW)]
                        e.activation(dst, pv("o", r, HW), ACT.Copy, scale=rinv[0:r, n % 4, 0:1] if ib < NT else 1.0).then_inc(
                            *S.up("act_free_o", key=("o", n)))

                    hi("D", 4, 0)
                    hi("D", 4, 1)
                    gate(0)
                    for hh in range(2):
                        e.wait_ge(*S.at("s_ready", ("k", hh)))
                        e.activation(kdT[:, hh, :], pv(f"s{hh}", P, TOK), ACT.Copy).then_inc(
                            *S.up(f"act_free_s{hh}", ("k", hh)))
                    exps(0)
                    e.wait_ge(*S.at("dve_step", ("rope", "k")))
                    kv_store(S, e, l, p, "k", rawk)
                    exps(1)
                    e.wait_ge(*S.at("dve_free_mm0", ("rest", "v")))
                    e.wait_ge(*S.own())
                    kv_store(S, e, l, p, "v", vd)
                    for n in range(10):
                        if n == 6:
                            e.wait_ge(*S.at("t_ready", ("kc", 1)))
                            e.wait_ge(*S.own())
                            e.activation(kcT[:, :], pv("t", P, PAST), ACT.Copy).then_inc(*S.up("act_free_t", ("kc", 1)))
                        if n in GATE_AT:
                            gate(GATE_AT.index(n) + 1)
                        turn(n)
                        if n:
                            out(n - 1)
                        if n + 2 < 10:
                            exps(n + 2)
                        if n == 5:
                            e.wait_ge(*S.at("o_ready", (0, NT)))
                            cache_load(S, e, l, p, 1, "v")
                    out(9)
                with S.body("R") as i:
                    prev = None
                    t = 0
                    for hh in range(2):
                        for u, buf in ((0, rk), (1, vr), (2, gs)):
                            for m in range(TILES):
                                bank = f"mm{t % 2}"
                                t += 1
                                j = 3 * hh + u
                                if m == 0 and hh == 0 and u == 0:
                                    for s in ("dve_step", "s_ready", "o_ready", "t_ready", "dve_free_t", "dve_free_o", "dve_free_s0", "dve_free_s1", "dve_free_mm0",
                                              "dve_free_mm1", "kv_out"):
                                        e.wait_ge(*S.at(s, k=0))
                                if m == 0 and hh == 1 and u == 0:
                                    e.wait_ge(*S.at("dve_step", ("kz", 0)))
                                    e.wait_ge(*S.at("s_ready", ("qk", 0, 1)))
                                if m == 0 and hh == 1 and u == 1:
                                    e.wait_ge(*S.at("s_ready", ("snew", 0)))
                                if m == 0 and hh == 1 and u == 2:
                                    e.wait_ge(*S.at("dve_free_t", ("os", 0)))
                                    e.wait_ge(*S.at("dve_free_o", ("o", 0, 3)))
                                key = (("rk", "vr", "gr")[u], hh, m)
                                if m == 0:
                                    hi("R", j + 1, 0)
                                    hi("R", j + 1, 1)
                                if m < NT:
                                    e.wait_ge(*S.at("mm_ready", ("N", j, m)))
                                    if u == 2:
                                        e.wait_ge(*S.own())
                                        e.activation(gs[:, m, :], pv(bank, P, UC), ACT.Tanh, scale=0.5).then_inc(
                                            *S.up(f"act_free_{bank}", key))
                                    else:
                                        e.activation(buf[:, m, :], pv(bank, P, UC), ACT.Copy).then_inc(
                                            *S.up(f"act_free_{bank}", key))
                                else:
                                    rest_copy(bank, ("N", j, m), prev)
                                    prev = (f"dve_free_{bank}", ("rest", hh, u))
                                    if u == 2:
                                        e.wait_ge(*S.at(f"dve_free_{bank}", ("gsum", hh)))
                                        e.wait_ge(*S.own())
                                        e.activation(gs[0:DEC, NT, :], rest[:, 0:UC], ACT.Tanh, scale=0.5).then_inc(
                                            *S.up("act_step", key=("gs", hh)))
                                if u == 2 and m in (2, 3):
                                    for ib in ((0, 1) if m == 2 else (2, 3)):
                                        squares(S, e, hh, ib, i)
                            if u == 1:
                                for v, dst in ((0, qrT), (1, krT)):
                                    e.wait_ge(*S.at("s_ready", ("qk", hh, v)))
                                    e.wait_ge(*S.own())
                                    e.activation(dst[:, :], pv(f"s{v}", P, TOK), ACT.Copy).then_inc(
                                        *S.up(f"act_free_s{v}", ("qk", hh, v)))
                        squares(S, e, hh, NT, i)
                        e.wait_ge(*S.at("o_ready", ("sfin", hh)))
                        if hh:
                            e.wait_ge(*S.at("st_out0", ("st", 0)))
                        else:
                            e.wait_ge(*S.at("st_out0", k=0))
                        e.wait_ge(*S.own())
                        e.activation(sout[:, 0, :], pv("o", P, RET_DV), ACT.Copy).then_inc(*S.up("act_free_o", ("sfin", hh)))
                        for b, (name, w, key) in enumerate((("state_ret_prompt", "act_free_o", ("sfin", hh)),
                                                            ("state_ret_sample", "dve_free_s1", ("snew", hh)))):
                            e.wait_ge(*S.at(w, key))
                            e.dma_start(A[name][ds(l, 1), 0, ds(i * 2 + hh, 1)].rearrange("a h d e -> d (a h e)"),
                                                 sout[:, b, :]).then_inc(*S.up(f"st_out{b}", ("st", hh), n=16))
                with S.body("M"):
                    for j in range(16):
                        kind = j // 4
                        if kind == 0:
                            for tt in range(4):
                                bank = f"mm{(4 * j + tt) % 2}"
                                if tt == 0:
                                    hi("M", j + 1, 0)
                                    hi("M", j + 1, 1)
                                if j >= 2:
                                    c = 4 * (j - 2) + tt
                                    g = vecs[:, ds(l, 1), 2 * KC + c % 2:2 * KC + c % 2 + 1].rearrange("p a b -> p (a b)")
                                    e.wait_ge(*S.at("s_ready", ("ret", c)))
                                    e.wait_ge(*S.at("dve_step", ("ssd", 1)))
                                    e.wait_ge(*S.own())
                                    S.settle()
                                    e.activation(hl2[:, c, 0, :], pv(f"s{c % 2}", P, TOK), ACT.Copy, scale=g).then_inc(
                                        *S.up(f"act_free_s{c % 2}", ("ret", c)))
                                e.wait_ge(*S.at("mm_ready", ("T", j, tt // 2, tt % 2)))
                                if j == 0 and tt == 0:
                                    for s in ("t_ready", "o_ready", "s_ready", "dve_step", "dve_free_t"):
                                        e.wait_ge(*S.at(s, k=0))
                                e.activation(tb[:, 2 * j + tt // 2, (tt % 2) * HALF:(tt % 2 + 1) * HALF], pv(bank, P, HALF),
                                             ACT.Tanh, scale=0.5).then_inc(*S.up(f"act_free_{bank}", ("gb", j, tt)))
                                if j < 2 and tt == 0:
                                    if j:
                                        e.wait_ge(*S.at("dve_step", ("ssd", 0)))
                                    e.wait_ge(*S.own())
                                    e.activation(squares_of_dif[:, :, :], odif[:, :, j * 512:(j + 1) * 512], ACT.Square).then_inc(
                                        *S.up("act_step", key=("sqd", j)))
                        elif kind == 1:
                            u = j - 4
                            hi("M", j + 1, 0)
                            hi("M", j + 1, 1)
                            for c in (2 * u, 2 * u + 1):
                                e.wait_ge(*S.at("s_ready", ("dif", c)))
                                if c == 0:
                                    e.wait_ge(*S.at("mm_ready", ("end", 3)))
                                e.wait_ge(*S.own())
                                S.settle()
                                e.activation(hl1[:, c, 0, :], pv(f"s{c % 2}", P, TOK), ACT.Copy, scale=gd[:, ds(l, 1)]).then_inc(
                                    *S.up(f"act_free_s{c % 2}", ("dif", c)))
                        elif kind == 2:
                            u = j - 8
                            for tt in range(4):
                                if tt == 0:
                                    hi("M", j + 1, 0)
                                    hi("M", j + 1, 1)
                                c, h0 = 2 * u + tt // 2, (tt % 2) * HALF
                                e.wait_ge(*S.at("dve_step", ("mer", j, tt)))
                                if j == 8 and tt == 0:
                                    e.wait_ge(*S.at("mm_ready", ("end", 7)))
                                e.wait_ge(*S.own())
                                e.activation(hl2[:, c, 0, h0:h0 + HALF], mer[:, c, h0:h0 + HALF], ACT.Copy, scale=0.5).then_inc(
                                    *S.up("act_step", key=("mhi", j, tt)))
                            if u == 3:
                                e.wait_ge(*S.at("dve_step", ("lo", "mer", 3)))
                                for st in ("st_out0", "st_out1"):
                                    e.wait_ge(*S.at(st, k=0))
                                e.wait_ge(*S.own())
                                e.activation(xs2[:, :, :, :].rearrange("p c v s -> p (c v) s"),
                                             hl2[:, :, :, SEQ:TOK].rearrange("p c v s -> p (c v) s"), ACT.Copy).then_inc(
                                                 *S.up("act_step", key=("xs", "mer")))
                        else:
                            u = j - 12
                            for m in range(2):
                                hi("M", j + 1, m)
                            for m in range(TILES):
                                bank = f"mm{(48 + u * 5 + m) % 2}"
                                if m == NT:
                                    rest_copy(bank, ("N", j, 4), ("dve_step", ("rest", j - 1)) if u else None)
                                e.wait_ge(*S.at(f"dve_free_{bank}", ("x", u, m)))
                                squares_of_x(m, u * UC, UC, xn[:, m, 0:UC], 40 + 4 * m + u, ("ssq", m) if u == 3 else None)
                    norm("n")
                with S.body("F") as f:
                    for s in ("dve_step", "s_ready", "dve_free_s0", "dve_free_s1", "dve_free_t", "cs_out", "st_out0", "st_out1", "mm_ready"):
                        e.wait_ge(*S.at(s, k=0))
                    def first_tap(j, s):
                        w = lambda v: conv[:, ds(l, 1), v, ds(f * FB + (j + s * FT), 1)]
                        if s == 0:
                            e.wait_ge(*S.at("dve_step", ("pads", j)))
                            if j:
                                e.wait_ge(*S.at("dve_step", ("af", j - 1)))
                        else:
                            e.wait_ge(*S.at("dve_free_" + UP_BANKS[j % 2][3], ("ug", j, 1)))
                        e.wait_ge(*S.own())
                        S.settle()
                        e.activation(ca[:, s, :], up[:, j % 2, s, 0:GP], ACT.Identity, bias=w(5), scale=w(2)).then_inc(
                            *S.up("act_step", key=("tap0", j, s)))

                    def half_tanh(j):
                        e.wait_ge(*S.at("dve_step", ("conv2", j, 1)))
                        e.wait_ge(*S.own())
                        e.activation(th[:, :], ca[:, 1, :], ACT.Tanh, scale=0.5).then_inc(*S.up("act_step", key=("th", j)))

                    def gated_hi(j):
                        e.wait_ge(*S.at("dve_step", ("af", j)))
                        e.wait_ge(*S.own())
                        e.activation(act[:, j, 0, :], af[:, :], ACT.Copy).then_inc(*S.up("act_step", key=("ahi", j)))

                    def sample_rows(n):
                        k0, k1 = sum(DOWN[0][:n]), sum(DOWN[0][:n + 1])
                        e.wait_ge(*S.at("dve_step", ("alo", k1 - 1)))
                        e.wait_ge(*S.own())
                        e.activation(acts[:, k0:k1, :, :].rearrange("p c v s -> p (c v) s"),
                                     act[:, k0:k1, :, GP - DEC:GP].rearrange("p c v s -> p (c v) s"),
                                     ACT.Copy).then_inc(*S.up("act_step", key=("acts", n)))

                    for j in range(FB):
                        b = j % 2
                        b0, b1 = UP_BANKS[b][0:2]
                        if j:
                            first_tap(j - 1, 1)
                        hi("F", j + 1, 0)
                        hi("F", j + 1, 1)
                        if j:
                            half_tanh(j - 1)
                        e.wait_ge(*S.at("mm_ready", ("T", j, 0, 0)))
                        if j >= 2:
                            e.wait_ge(*S.at("dve_step", ("cs", j - 2)))
                            e.wait_ge(*S.at("dve_step", ("conv2", j - 2, 1)))
                        e.activation(up[:, b, 0, 2:2 + HALF], pv(b0, P, HALF), ACT.Copy).then_inc(
                            *S.up(f"act_free_{b0}", ("ua", j, 0)))
                        if j:
                            gated_hi(j - 1)
                        for n in (0, 1):
                            if j == sum(DOWN[0][:n + 1]) + 1:
                                sample_rows(n)
                        e.wait_ge(*S.at("mm_ready", ("T", j, 0, 1)))
                        e.activation(up[:, b, 0, 2 + HALF:2 + SEQ], pv(b1, P, SEQ - HALF), ACT.Copy).then_inc(
                            *S.up(f"act_free_{b1}"))
                        e.activation(up[:, b, 0, 4 + SEQ:4 + TOK], pv(b1, P, DEC, SEQ - HALF), ACT.Copy).then_inc(
                            *S.up(f"act_free_{b1}", ("ua", j, 1)))
                        first_tap(j, 0)
                    first_tap(FB - 1, 1)
                    hi("F", FB + 1, 0)
                    half_tanh(FB - 1)
                    hi("F", FB + 1, 1)
                    gated_hi(FB - 1)
                    sample_rows(2)
                    j = FB
                    for hf in range(2):
                        for n, nk in enumerate(DOWN[hf]):
                            if j > FB:
                                prep("F", j + 1)
                            j += 1
                        rest_copy("s1", ("down", hf, NT), ("dve_step", ("drest", 0)) if hf else None, 512)
                        if hf == 0:
                            for m in (NT, 0, 1, 2, 3):
                                e.wait_ge(*S.at(f"dve_free_{DOWN_BANKS[m]}", ("down", hf, m)))
                                squares_of_x(m, 0, 512, th[:, 0:512], 40 + 2 * m, None)
                    e.wait_ge(*S.at("dve_free_t", "cs"))
                    for q in range(2):
                        name = ("state_conv_prompt", "state_conv_sample")[q]
                        for s in range(2):
                            dst = A[name][ds(l, 1), 0, :, ds(f * FB * P + s * D_FF, FB * P)].rearrange(
                                "a t (c p) -> c (a t) p", p=P)
                            e.dma_start(dst, csT[s * FB:(s + 1) * FB, 2 * q:2 * q + 2, :]).then_inc(
                                *S.up("cs_out", ("cs", q, s), n=16))

        def squares(S, e, hh, ib, i):
            r = ROWS[ib]
            bank = "to"[ib % 2]
            key = ("o", hh, ib) if ib < NT else ("os", hh)
            e.wait_ge(*S.at(f"dve_free_{bank}", key))
            e.wait_ge(*S.own())
            junk = rk[0:r, 0, :]
            S.settle()
            e.activation(junk, pv(bank, r, RET_DV), ACT.Square,
                                  accum_out=ssr[0:r, ib, ds(i * 2 + hh, 1)]).then_inc(*S.up(f"act_free_{bank}", key))

        def dve_program(S):
            e = S.e

            def mean(n, width, key, at=0, sums=None):
                e.wait_ge(*S.own())
                e.tensor_scalar(ms[:, at:at + n], ss[:, at:at + n] if sums is None else sums, 1.0 / width, EPS, ALU.mult, ALU.add).then_inc(
                    *S.up("dve_step", key=("ms", key)))

            def norm(key, parts):
                e.wait_ge(*S.own())
                e.tensor_reduce(ss[:, 0:TILES], ss[:, 40:40 + TILES * parts].rearrange("p (m q) -> p m q", m=TILES), AX, ALU.add).then_inc(
                    *S.up("dve_step"))
                mean(TILES, D_MODEL, key)
                e.wait_ge(*S.at("pool_step", ("rstd", key)))
                for half in range(2):
                    h = slice(half * 512, (half + 1) * 512)
                    for m in (0, 2, 4):
                        r = ROWS[m]
                        e.wait_ge(*S.own())
                        e.tensor_scalar(xn[0:r, m, h], x[0:r, m, h], rstd[0:r, m:m + 1], None, ALU.mult).then_inc(
                            *S.up("dve_step", key=("xn", key, half) if m == NT else None))
                for c in range(KC):
                    o = c if S.phase == "N" else KC + c
                    bank = NORM_BANKS[c % 4]
                    g = vecs[:, ds(S.layer, 1), o:o + 1].rearrange("p a b -> p (a b)")
                    e.wait_ge(*S.at(f"act_free_{bank}", ("norm", c)))
                    e.wait_ge(*S.own())
                    e.scalar_tensor_tensor(out=hl1[:, c, 1, :], in0=pv(bank, P, TOK), scalar=g, in1=hl1[:, c, 0, :].bitcast(F32),
                                           op0=ALU.mult, op1=ALU.subtract).then_inc(*S.up(f"dve_free_{bank}", ("norm", c)))

            for b in BANK:
                S.prime(f"dve_free_{b}", 1)
            S.prime("dve_step", 1)
            e.memset(ss[:, :], 1.0).then_inc(*S.up("dve_step"))
            e.memset(ssr[:, :, :], 1.0).then_inc(*S.up("dve_step", key="ones"))
            e.wait_ge(*S.at("lambdas", "in"))
            for l in range(DEPTH):
                v = prob[:, l, 0:4 * DIFF_HD].rearrange("p (a b) -> p a b", a=4)
                e.wait_ge(*S.own())
                e.tensor_tensor(v[:, 0:2, :], v[:, 0:2, :], v[:, 2:4, :], ALU.mult).then_inc(*S.up("dve_step"))
                e.wait_ge(*S.own())
                e.tensor_reduce(aT[:, 0, 8 + 2 * l:10 + 2 * l], v[:, 0:2, :], AX, ALU.add).then_inc(
                    *S.up("dve_step", key="lamp" if l == DEPTH - 1 else None))
            e.wait_ge(*S.at("act_step", "lexp"))
            e.wait_ge(*S.at("tables", "in"))
            e.wait_ge(*S.at("params", "in"))
            for l in range(DEPTH):
                e.wait_ge(*S.own())
                e.tensor_tensor(lam[:, l:l + 1], aT[:, 0, 2 * l + 1:2 * l + 2], aT[:, 0, 2 * l:2 * l + 1], ALU.subtract).then_inc(
                    *S.up("dve_step"))
                e.wait_ge(*S.own())
                e.tensor_tensor(lam[:, l:l + 1], lam[:, l:l + 1], lamc[:, l:l + 1], ALU.subtract).then_inc(*S.up("dve_step"))
                e.wait_ge(*S.own())
                e.memset(sgn[0:DEC, l:l + 1], 1.0).then_inc(*S.up("dve_step"))
                e.wait_ge(*S.own())
                e.tensor_copy(sgn[DEC:2 * DEC, l:l + 1], lam[0:DEC, l:l + 1]).then_inc(*S.up("dve_step"))
            for l in range(DEPTH):
                e.wait_ge(*S.own())
                e.tensor_tensor(gd[:, l:l + 1], vecs[:, l, 18:19], lamc[:, 2 + l:3 + l], ALU.mult).then_inc(*S.up("dve_step"))
            with S.layers() as l:
                with S.body("N"):
                    e.wait_ge(*S.at("act_step", ("ssq", 3)))
                    e.wait_ge(*S.at("pool_step", k=0))
                    norm("n", 2)
                with S.body("D") as p:
                    lreg = l
                    e.wait_ge(*S.at("pool_step", k=0))

                    def sample_sum(buf, bank, key, name):
                        e.wait_ge(*S.at(f"act_free_{bank}", ("rest",) + key))
                        e.wait_ge(*S.own())
                        e.tensor_tensor(buf, pv(bank, DEC, UC), rest[:, 0:UC], ALU.add).then_inc(
                            *S.up(f"dve_free_{bank}", ("rest", name)))

                    def qk_sums(name):
                        e.wait_ge(*S.at("act_step", ("sq", name)))
                        e.wait_ge(*S.own())
                        e.tensor_reduce(ss[:, 0:20], prob[:, :, :].rearrange("p a b -> p (a b)")[:, 0:TILES * UC].rearrange(
                            "p (g d) -> p g d", d=DIFF_HD), AX, ALU.add).then_inc(*S.up("dve_step", key=("ss", name)))
                        mean(20, DIFF_HD, name)

                    def qk_apply(buf, name, v, between=None):
                        e.wait_ge(*S.at("pool_step", ("rstd", name)))
                        b3 = buf[:, :, :].rearrange("p m (h d) -> p (m h) d", d=DIFF_HD)
                        e.wait_ge(*S.own())
                        e.tensor_tensor(b3, b3, rstd[:, 0:20].unsqueeze(2).broadcast_to([P, 20, DIFF_HD]), ALU.mult).then_inc(
                            *S.up("dve_step"))
                        e.wait_ge(*S.own())
                        e.tensor_tensor(b3, b3, qkg[:, ds(lreg, 1), v, :].broadcast_to([P, 20, DIFF_HD]), ALU.mult).then_inc(
                            *S.up("dve_step"))
                        if between:
                            between()
                        b4 = buf[:, :, :].rearrange("p m (h d) -> p m h d", d=DIFF_HD)
                        x1, x2 = b4[:, :, :, 0:8], b4[:, :, :, 8:16]
                        c, s = (t.unsqueeze(2).broadcast_to([P, TILES, 4, 8]) for t in (dcos, dsin))
                        t1, t2 = (rt[:, k, :].rearrange("p (m h d) -> p m h d", m=TILES, h=4) for k in (0, 1))
                        e.wait_ge(*S.own())
                        e.tensor_tensor(t1, x2, s, ALU.mult).then_inc(*S.up("dve_step"))
                        e.wait_ge(*S.own())
                        e.tensor_tensor(t2, x1, s, ALU.mult).then_inc(*S.up("dve_step"))
                        e.wait_ge(*S.own())
                        e.tensor_tensor(x1, x1, c, ALU.mult).then_inc(*S.up("dve_step"))
                        e.wait_ge(*S.own())
                        e.tensor_tensor(x2, x2, c, ALU.mult).then_inc(*S.up("dve_step"))
                        e.wait_ge(*S.own())
                        e.tensor_tensor(x1, x1, t1, ALU.subtract).then_inc(*S.up("dve_step"))
                        e.wait_ge(*S.own())
                        e.tensor_tensor(x2, x2, t2, ALU.add).then_inc(*S.up("dve_step", key=("rope", name)))

                    sample_sum(rawq[0:DEC, NT, :], "mm0", ("N", 0, 4), "q")
                    qk_sums("q")
                    qk_apply(rawq, "q", 0, lambda: sample_sum(rawk[0:DEC, NT, :], "mm1", ("N", 1, 4), "k"))
                    qk_sums("k")
                    for hh in range(2):
                        e.wait_ge(*S.at("s_ready", ("q", hh)))
                        e.wait_ge(*S.own())
                        e.tensor_scalar(qz[DIFF_HD:P, hh, TOK + DEC:TOK + DEC + SEQ], ps[DIFF_HD:P, BANK[f"s{hh}"]:BANK[f"s{hh}"] + SEQ], DIFF_HD ** -0.5, None, ALU.mult).then_inc(
                            *S.up(f"dve_free_s{hh}", key=("q0", hh)))
                        e.wait_ge(*S.own())
                        e.tensor_scalar(qz[DIFF_HD:P, hh, TOK:TOK + DEC], ps[DIFF_HD:P, BANK[f"s{hh}"] + SEQ:BANK[f"s{hh}"] + TOK], DIFF_HD ** -0.5, None, ALU.mult).then_inc(
                            *S.up(f"dve_free_s{hh}", key=("q1", hh)))
                    qk_apply(rawk, "k", 1)
                    sample_sum(vd[0:DEC, NT, :], "mm0", ("N", 2, 4), "v")

                    steps = [(hh, ib) for hh in range(2) for ib in range(TILES)]

                    def maxes(n):
                        hh, ib = steps[n]
                        b = n % 2
                        e.wait_ge(*S.at("s_ready", ("s", n)))
                        if n >= 2:
                            e.wait_ge(*S.at("act_free_s%d" % b, ("exp", n - 2)))
                        if ib < NT:
                            k = (ib + 1) * P
                            v = pv(f"s{b}", P, 1024).rearrange("p (c n) -> p c n", c=2)
                            e.wait_ge(*S.own())
                            e.memset(v[0:CHUNK, :, k - CHUNK:k], NEG).then_inc(*S.up("dve_step"))
                            e.wait_ge(*S.own())
                            e.tensor_reduce(nmax[:, b, :], v[:, :, 0:k], AX, ALU.max, negate=True).then_inc(
                                *S.up("dve_step", key=("max", n)))
                        else:
                            e.wait_ge(*S.own())
                            e.tensor_reduce(nmax[0:2 * DEC, b, 0:1], pv(f"s{b}", 2 * DEC, TOK), AX, ALU.max, negate=True).then_inc(
                                *S.up("dve_step", key=("max", n)))

                    def combine(n):
                        hh, ib = steps[n]
                        b = n % 2
                        e.wait_ge(*S.at(f"act_free_s{b}", ("exp", n)))
                        if n >= 4:
                            e.wait_ge(*S.at("act_free_o", ("o", n - 4)))
                        e.wait_ge(*S.own())
                        if ib < NT:
                            k = (ib + 1) * P
                            e.reciprocal(rinv[:, n % 4, 0:2], sums[:, b, :]).then_inc(*S.up("dve_step"))
                            e.wait_ge(*S.own())
                            e.scalar_tensor_tensor(out=rinv[:, n % 4, 2:3], in0=sums[:, b, 0:1], scalar=lam[:, ds(lreg, 1)], in1=rinv[:, n % 4, 1:2], op0=ALU.mult, op1=ALU.mult).then_inc(
                                *S.up("dve_step"))
                            e.wait_ge(*S.own())
                            e.scalar_tensor_tensor(out=prob[:, b, 0:k], in0=prob[:, b, 512:512 + k], scalar=rinv[:, n % 4, 2:3], in1=prob[:, b, 0:k], op0=ALU.mult, op1=ALU.add).then_inc(
                                *S.up("dve_step", key=("a", n)))
                        else:
                            r = 2 * DEC
                            e.reciprocal(rinv[0:r, n % 4, 0:1], sums[0:r, b, 0:1]).then_inc(*S.up("dve_step"))
                            e.wait_ge(*S.own())
                            e.tensor_tensor(rinv[0:r, n % 4, 2:3], rinv[0:r, n % 4, 0:1], sgn[:, ds(lreg, 1)],
                                            ALU.mult).then_inc(
                                *S.up("dve_step"))
                            e.wait_ge(*S.own())
                            e.tensor_scalar(prob[0:r, b, 0:TOK], prob[0:r, b, 0:TOK], rinv[0:r, n % 4, 2:3], None,
                                            ALU.mult).then_inc(
                                *S.up("dve_step", key=("a", n)))

                    def weights_of_sample(n):
                        if steps[n][1] < NT:
                            return
                        v = pv("t", P, TILES * 2 * DEC).rearrange("p (c n) -> p c n", c=TILES)
                        e.wait_ge(*S.at("act_free_t", ("aTt", n)))
                        if n > 5:
                            e.wait_ge(*S.at("o_ready", (0, NT)))
                        e.wait_ge(*S.own())
                        e.tensor_tensor(aTs[:, 0:NT, :], v[:, 0:NT, 0:DEC], aTt[:, 0:NT, :], ALU.add).then_inc(
                            *S.up("dve_free_t"))
                        e.wait_ge(*S.own())
                        e.tensor_tensor(aTs[0:DEC, NT, :], v[0:DEC, NT, 0:DEC], aTt[0:DEC, NT, :], ALU.add).then_inc(
                            *S.up("dve_free_t", ("aT", n)))

                    maxes(0)
                    maxes(1)
                    for n in range(10):
                        combine(n)
                        if n + 2 < 10:
                            maxes(n + 2)
                        weights_of_sample(n)
                with S.body("R") as i:
                    for hh in range(2):
                        head = i * 2 + hh
                        t0 = 15 * hh

                        def sample_sum(buf, bank, key, u):
                            e.wait_ge(*S.at(f"act_free_{bank}", ("rest",) + key))
                            e.wait_ge(*S.own())
                            e.tensor_tensor(buf, pv(bank, DEC, UC), rest[:, 0:UC], ALU.add).then_inc(
                                *S.up(f"dve_free_{bank}", ("rest", hh, u)))

                        if hh == 0:
                            for s in ("s_ready", "o_ready", "t_ready", "kv_out", "act_step", "act_free_t"):
                                e.wait_ge(*S.at(s, k=0))
                            e.wait_ge(*S.own())
                            e.memset(rk[:, NT, :], 0.0).then_inc(*S.up("dve_step"))
                        sample_sum(rk[0:DEC, NT, :], f"mm{(t0 + 4) % 2}", ("N", 3 * hh, 4), 0)
                        e.wait_ge(*S.at("act_free_mm0", ("rk", hh, 2 if not hh else 3)))
                        e.wait_ge(*S.at("act_free_mm1", ("rk", hh, 3 if not hh else 2)))
                        if hh:
                            e.wait_ge(*S.at("t_ready", ("os", 0)))
                        rv = rk[:, :, :].rearrange("p m (v d) -> p m v d", v=2)
                        x1, x2 = rv[:, :, :, 0:64], rv[:, :, :, 64:128]
                        c, s = (t.unsqueeze(2).broadcast_to([P, TILES, 2, 64]) for t in (rcos, rsin))
                        t1, t2 = (b[:, 0:TILES * 128].rearrange("p (m v d) -> p m v d", m=TILES, v=2) for b in (sT, kzf))
                        if hh:
                            e.wait_ge(*S.at("s_ready", ("snew", 0)))
                        e.wait_ge(*S.own())
                        e.tensor_tensor(t1, x2, s, ALU.mult).then_inc(*S.up("dve_step"))
                        e.wait_ge(*S.own())
                        e.tensor_tensor(t2, x1, s, ALU.mult).then_inc(*S.up("dve_step"))
                        e.wait_ge(*S.own())
                        e.tensor_tensor(x1, x1, c, ALU.mult).then_inc(*S.up("dve_step"))
                        e.wait_ge(*S.own())
                        e.tensor_tensor(x2, x2, c, ALU.mult).then_inc(*S.up("dve_step"))
                        e.wait_ge(*S.own())
                        e.tensor_tensor(x1, x1, t1, ALU.subtract).then_inc(*S.up("dve_step"))
                        e.wait_ge(*S.own())
                        e.tensor_tensor(x2, x2, t2, ALU.add).then_inc(*S.up("dve_step", key=("rope", hh)))
                        e.wait_ge(*S.own())
                        e.tensor_tensor(kz[:, :, :], rk[:, :, P:2 * P], zeta[:, :, ds(head, 1)].broadcast_to([P, TILES, P]), ALU.mult).then_inc(
                            *S.up("dve_step", key=("kz", hh)))
                        sample_sum(vr[0:DEC, NT, :], f"mm{(t0 + 9) % 2}", ("N", 3 * hh + 1, 4), 1)
                        e.wait_ge(*S.at("act_free_s0", ("qk", hh, 0)))
                        e.wait_ge(*S.own())
                        e.tensor_tensor(qx[:, :], qrT[:, SEQ:TOK], xi[:, ds(head, 1), :].rearrange("p a b -> p (a b)"), ALU.mult).then_inc(
                            *S.up("dve_step", key=("qx0", hh)))

                        def gate(m):
                            bank = f"mm{(t0 + 10 + m) % 2}"
                            e.wait_ge(*S.at(f"act_free_{bank}", ("gr", hh, m)))
                            e.wait_ge(*S.own())
                            e.scalar_tensor_tensor(out=gs[:, m, :], in0=gs[:, m, :], scalar=1.0,
                                                   in1=pv(bank, P, UC), op0=ALU.add, op1=ALU.mult).then_inc(
                                *S.up(f"dve_free_{bank}", ("gr", hh, m)))

                        def decayed(jb):
                            n = SEQ - jb * P
                            bank = ("s0", "s1")[jb // 2]
                            e.wait_ge(*S.at("s_ready", ("ret", hh, jb)))
                            if jb == 0:
                                e.wait_ge(*S.at("decay_in", "d"))
                            e.wait_ge(*S.own())
                            e.tensor_tensor(sT[:, SOFF[jb]:SOFF[jb] + n], pv(bank, P, n, (jb % 2) * 512), decay[:, hh, 0:n], ALU.mult).then_inc(
                                *S.up(f"dve_free_{bank}", ("sT", hh, jb)))

                        def gated(ib):
                            bank = "to"[ib % 2]
                            r = ROWS[ib]
                            key = ("o", hh, ib) if ib < NT else ("os", hh)
                            e.wait_ge(*S.at(f"{'to'[ib % 2]}_ready", key))
                            e.wait_ge(*S.own())
                            e.tensor_tensor(oret[0:r, ds(head * 2, 2), ib, :], pv(bank, r, RET_DV).rearrange("p (t d) -> p t d", t=2),
                                            gs[0:r, ib, :].rearrange("p (t d) -> p t d", t=2), ALU.mult).then_inc(
                                                *S.up(f"dve_free_{bank}", key))

                        gate(0)
                        decayed(0)
                        decayed(1)
                        gate(1)
                        decayed(2)
                        decayed(3)
                        gate(2)
                        gated(0)
                        gated(1)
                        e.wait_ge(*S.at("s_ready", ("rets", hh)))
                        e.wait_ge(*S.own())
                        e.tensor_tensor(sTs_x[:, :], pv("s0", DEC, DEC), decay[0:DEC, hh, 0:DEC], ALU.mult).then_inc(
                            *S.up("dve_free_s0", ("sTs", hh)))
                        gate(3)
                        gated(2)
                        gated(3)
                        bank = f"mm{(t0 + 14) % 2}"
                        e.wait_ge(*S.at(f"act_free_{bank}", ("rest", "N", 3 * hh + 2, 4)))
                        e.wait_ge(*S.own())
                        e.tensor_tensor(rest[:, 0:UC], pv(bank, DEC, UC), rest[:, 0:UC], ALU.add).then_inc(
                            *S.up(f"dve_free_{bank}", ("gsum", hh)))
                        e.wait_ge(*S.at("act_step", ("gs", hh)))
                        e.wait_ge(*S.own())
                        e.scalar_tensor_tensor(out=gs[0:DEC, NT, :], in0=gs[0:DEC, NT, :], scalar=1.0,
                                               in1=rest[:, 0:UC], op0=ALU.add, op1=ALU.mult).then_inc(
                            *S.up(f"dve_free_{bank}", ("rest", hh, 2)))
                        gated(NT)
                        e.wait_ge(*S.at("s_ready", ("snew", hh)))
                        e.wait_ge(*S.at("sin_in", ("s", hh)))
                        e.wait_ge(*S.at("st_out1", ("st", 0))) if hh else e.wait_ge(*S.at("st_out1", k=0))
                        e.wait_ge(*S.own())
                        e.scalar_tensor_tensor(out=sout[:, 1, :], in0=sin[:, :], scalar=g32[:, ds(head, 1)],
                                               in1=pv("s1", P, RET_DV), op0=ALU.mult, op1=ALU.add).then_inc(
                            *S.up("dve_free_s1", ("snew", hh)))
                with S.body("M"):
                    e.wait_ge(*S.at("act_free_o", k=0))
                    e.wait_ge(*S.at("act_free_t", k=0))
                    mean(20, RET_DV, "ret", 40, ssr[:, :, :].rearrange("p m h -> p (m h)"))
                    def sums_of_dif(q):
                        e.wait_ge(*S.at("act_step", ("sqd", q)))
                        e.wait_ge(*S.own())
                        e.tensor_reduce(ss[:, q * 20:q * 20 + 20], squares_of_dif[:, :, :].rearrange("p m (h d) -> p (m h) d", h=4), AX, ALU.add).then_inc(
                            *S.up("dve_step", key=("ssd", q)))
                        mean(20, HW, f"dif{q}", q * 20)

                    def scale_dif(q):
                        e.wait_ge(*S.at("pool_step", ("rstd", f"dif{q}")))
                        for m in range(TILES):
                            r = ROWS[m]
                            v = odif[0:r, m, q * 512:(q + 1) * 512].rearrange("p (h d) -> p h d", h=4)
                            rs = rstd[0:r, q * 20 + m * 4:q * 20 + m * 4 + 4].unsqueeze(2).broadcast_to([r, 4, HW])
                            e.wait_ge(*S.own())
                            e.tensor_tensor(v, v, rs, ALU.mult).then_inc(
                                *S.up("dve_step", key=("odif", q) if m == NT else None))

                    sums_of_dif(0)
                    e.wait_ge(*S.at("pool_step", ("rstd", "ret")))
                    for m in range(TILES):
                        r = ROWS[m]
                        v = oret[0:r, :, m, :].rearrange("p (h t) d -> p h t d", t=2)
                        rs = rstd[0:r, 40 + m * 4:44 + m * 4].unsqueeze(2).unsqueeze(3).broadcast_to([r, RET_HEADS, 2, P])
                        e.wait_ge(*S.own())
                        e.tensor_tensor(v, v, rs, ALU.mult).then_inc(
                            *S.up("dve_step", key=("oret", "done") if m == NT else None))
                    sums_of_dif(1)
                    for c in range(KC):
                        g = vecs[:, ds(l, 1), 2 * KC + c % 2:2 * KC + c % 2 + 1].rearrange("p a b -> p (a b)")
                        e.wait_ge(*S.at(f"act_free_s{c % 2}", ("ret", c)))
                        e.wait_ge(*S.own())
                        e.scalar_tensor_tensor(out=hl2[:, c, 1, :], in0=pv(f"s{c % 2}", P, TOK), scalar=g, in1=hl2[:, c, 0, :].bitcast(F32),
                                               op0=ALU.mult, op1=ALU.subtract).then_inc(
                                                   *S.up(f"dve_free_s{c % 2}", ("lo", "ret", c)))
                        if c == 3:
                            scale_dif(0)
                    for u in range(4):
                        j = 4 + u
                        for t in range(4):
                            bank = f"mm{t % 2}"
                            c, h0 = 2 * u + t // 2, (t % 2) * HALF
                            if t % 2 == 0:
                                e.wait_ge(*S.at(f"act_free_s{c % 2}", ("dif", c)))
                                e.wait_ge(*S.own())
                                e.scalar_tensor_tensor(out=hl1[:, c, 1, :], in0=pv(f"s{c % 2}", P, TOK), scalar=gd[:, ds(l, 1)],
                                                       in1=hl1[:, c, 0, :].bitcast(F32), op0=ALU.mult, op1=ALU.subtract).then_inc(
                                    *S.up(f"dve_free_s{c % 2}", ("lo", "dif", c)))
                            e.wait_ge(*S.at("mm_ready", ("T", j, t // 2, t % 2)))
                            if u == 0 and t == 0:
                                e.wait_ge(*S.at("act_free_mm0", k=0))
                                e.wait_ge(*S.at("act_free_mm1", k=0))
                            e.wait_ge(*S.own())
                            e.scalar_tensor_tensor(out=mer[:, c, h0:h0 + HALF], in0=mer[:, c, h0:h0 + HALF], scalar=1.0,
                                                   in1=pv(bank, P, HALF), op0=ALU.add, op1=ALU.mult).then_inc(
                                *S.up(f"dve_free_{bank}", ("wa", u, t)))
                            if u == 0 and t == 3:
                                scale_dif(1)
                    for u in range(4):
                        j = 8 + u
                        for t in range(4):
                            bank = f"mm{t % 2}"
                            c, h0 = 2 * u + t // 2, (t % 2) * HALF
                            e.wait_ge(*S.at("mm_ready", ("T", j, t // 2, t % 2)))
                            e.wait_ge(*S.at(f"act_free_{bank}", ("gb", u, t)))
                            e.wait_ge(*S.own())
                            e.scalar_tensor_tensor(out=tb[:, c, h0:h0 + HALF], in0=tb[:, c, h0:h0 + HALF], scalar=1.0,
                                                   in1=pv(bank, P, HALF), op0=ALU.add, op1=ALU.mult).then_inc(
                                *S.up(f"dve_free_{bank}"))
                            e.wait_ge(*S.own())
                            e.scalar_tensor_tensor(out=mer[:, c, h0:h0 + HALF], in0=mer[:, c, h0:h0 + HALF], scalar=0.5,
                                                   in1=tb[:, c, h0:h0 + HALF], op0=ALU.mult, op1=ALU.add).then_inc(
                                *S.up("dve_step", key=("mer", j, t)))
                            e.wait_ge(*S.at("act_step", ("mhi", j, t)))
                            e.wait_ge(*S.own())
                            e.scalar_tensor_tensor(out=hl2[:, c, 1, h0:h0 + HALF], in0=mer[:, c, h0:h0 + HALF], scalar=0.5, in1=hl2[:, c, 0, h0:h0 + HALF].bitcast(F32), op0=ALU.mult, op1=ALU.subtract).then_inc(
                                *S.up("dve_step", key=("lo", "mer", t) if u == 3 and t >= 2 else None))
                    for u in range(4):
                        j = 12 + u
                        for m in range(TILES):
                            bank = f"mm{(5 * u + m) % 2}"
                            r = ROWS[m]
                            v = x[0:r, m, u * UC:(u + 1) * UC]
                            e.wait_ge(*S.at("mm_ready", ("N", j, m)))
                            if m == NT:
                                e.wait_ge(*S.at(f"act_free_{bank}", ("rest", "N", j, m)))
                                e.wait_ge(*S.own())
                                e.tensor_tensor(v, v, rest[:, 0:UC], ALU.add).then_inc(*S.up("dve_step", key=("rest", j)))
                            e.wait_ge(*S.own())
                            e.tensor_tensor(v, v, pv(bank, r, UC), ALU.add).then_inc(*S.up(f"dve_free_{bank}", ("x", u, m)))
                    e.wait_ge(*S.at("act_step", ("ssq", NT)))
                    norm("n", 4)
                with S.body("F") as f:
                    for s in ("s_ready", "act_step", "t_ready", "mm_ready", "cs_out", "act_free_s1", "act_free_s0"):
                        e.wait_ge(*S.at(s, k=0))
                    e.wait_ge(*S.own())
                    e.memset(up[:, :, :, 0:2], 0.0).then_inc(*S.up("dve_step"))
                    def pads(j):
                        for s in range(2):
                            e.wait_ge(*S.own())
                            e.tensor_copy(up[:, j % 2, s, SEQ + 2:SEQ + 4],
                                          conv[:, ds(l, 1), 0:2, ds(f * FB + (j + s * FT), 1)].rearrange("p a v c -> p (a v c)")).then_inc(
                                *S.up("dve_step", key=("pads", j) if s else None))

                    pads(0)
                    for j in range(FB):
                        b = j % 2
                        w = lambda v, s: conv[:, ds(l, 1), v, ds(f * FB + (j + s * FT), 1)]
                        for t in range(2):
                            bank = UP_BANKS[j % 2][2 + t]
                            e.wait_ge(*S.at("mm_ready", ("T", j, 1, t)))
                            e.wait_ge(*S.own())
                            if t == 0:
                                e.tensor_copy(up[:, b, 1, 2:2 + HALF], pv(bank, P, HALF)).then_inc(
                                    *S.up(f"dve_free_{bank}", ("ug", j, 0)))
                            else:
                                e.tensor_copy(up[:, b, 1, 2 + HALF:2 + SEQ], pv(bank, P, SEQ - HALF)).then_inc(
                                    *S.up(f"dve_free_{bank}"))
                                e.tensor_copy(up[:, b, 1, 4 + SEQ:4 + TOK], pv(bank, P, DEC, SEQ - HALF)).then_inc(
                                    *S.up(f"dve_free_{bank}", ("ug", j, 1)))
                            if t == 0:
                                e.wait_ge(*S.at("act_step", ("tap0", j, 0)))
                                for v in (1, 2):
                                    e.wait_ge(*S.own())
                                    e.scalar_tensor_tensor(out=ca[:, 0, :], in0=up[:, b, 0, v:v + GP], scalar=w(2 + v, 0), in1=ca[:, 0, :], op0=ALU.mult, op1=ALU.add).then_inc(
                                        *S.up("dve_step"))
                        e.wait_ge(*S.at("act_step", ("tap0", j, 1)))
                        for v in (1, 2):
                            e.wait_ge(*S.own())
                            e.scalar_tensor_tensor(out=ca[:, 1, :], in0=up[:, b, 1, v:v + GP], scalar=w(2 + v, 1),
                                                   in1=ca[:, 1, :], op0=ALU.mult, op1=ALU.add).then_inc(
                                *S.up("dve_step", key=("conv2", j, 1) if v == 2 else None))
                        for q in range(2):
                            c0 = SEQ if q == 0 else TOK + 2
                            e.wait_ge(*S.own())
                            e.tensor_copy(cs[:, 2 * q:2 * q + 2, :].rearrange("p t (s c) -> p s t c", s=2)[:, :, :, j],
                                             up[:, b, :, c0:c0 + 2]).then_inc(*S.up("dve_step", key=("cs", j) if q else None))
                        if j + 1 < FB:
                            pads(j + 1)
                        e.wait_ge(*S.at("act_step", ("th", j)))
                        e.wait_ge(*S.own())
                        e.scalar_tensor_tensor(out=ca[:, 1, :], in0=th[:, :], scalar=1.0,
                                               in1=ca[:, 1, :], op0=ALU.add, op1=ALU.mult).then_inc(
                            *S.up("dve_step"))
                        if j:
                            e.wait_ge(*S.at("act_step", ("ahi", j - 1)))
                        e.wait_ge(*S.own())
                        e.scalar_tensor_tensor(out=af[:, :], in0=ca[:, 1, :], scalar=0.5,
                                               in1=ca[:, 0, :], op0=ALU.mult, op1=ALU.mult).then_inc(
                            *S.up("dve_step", key=("af", j)))
                        e.wait_ge(*S.at("act_step", ("ahi", j)))
                        e.wait_ge(*S.own())
                        e.tensor_tensor(act[:, j, 1, :], af[:, :], act[:, j, 0, :].bitcast(F32), ALU.subtract).then_inc(
                            *S.up("dve_step", key=("alo", j)))
                    for hf in range(2):
                        for m in (NT, 0, 1, 2, 3):
                            bank = DOWN_BANKS[m]
                            r = ROWS[m]
                            v = x[0:r, m, hf * 512:(hf + 1) * 512]
                            e.wait_ge(*S.at("mm_ready", ("down", hf, m)))
                            if m == NT:
                                e.wait_ge(*S.at("act_free_s1", ("rest", "down", hf, NT)))
                                e.wait_ge(*S.own())
                                e.tensor_tensor(v, v, rest[:, 0:512], ALU.add).then_inc(*S.up("dve_step", key=("drest", hf)))
                            e.wait_ge(*S.own())
                            e.tensor_tensor(v, v, ps[0:r, m * 512:(m + 1) * 512], ALU.add).then_inc(
                                *S.up(f"dve_free_{bank}", ("down", hf, m)))
                        if hf == 0:
                            e.wait_ge(*S.at("t_ready", "cs"))
                            e.wait_ge(*S.at("cs_out", k=0))
                            e.wait_ge(*S.own())
                            e.tensor_copy(csT[:, :, :].rearrange("p a b -> p (a b)"), pv("t", 2 * FB, 4 * P)).then_inc(
                                *S.up("dve_free_t", "cs"))

        kzf = kz[:, :, :].rearrange("p m d -> p (m d)")

        with nc.Block() as block:
            @block.sync
            def _(e):
                sync_program(Stream(e, "sync", known, seen, sem))

            @block.gpsimd
            def _(e):
                pool_program(Stream(e, "pool", known, seen, sem))

            @block.tensor
            def _(e):
                pe_program(Stream(e, "pe", known, seen, sem))

            @block.scalar
            def _(e):
                act_program(Stream(e, "act", known, seen, sem))

            @block.vector
            def _(e):
                dve_program(Stream(e, "dve", known, seen, sem))
    return seen


_INS = ["x_prompt", "x_sample", "cache_k", "cache_v", "state_ret", "w_in", "w_branch_a", "w_branch_b", "w_out", "w_up",
        "w_down"]
_OUTS = [("y_prompt", (1, SEQ, D_MODEL)), ("y_sample", (1, DEC, D_MODEL)),
         ("new_k_prompt", (DEPTH, 1, SEQ, DIFF_HEADS, HW)), ("new_v_prompt", (DEPTH, 1, SEQ, DIFF_HEADS, HW)),
         ("state_ret_prompt", (DEPTH, 1, RET_HEADS, RET_DK, RET_DV)), ("state_conv_prompt", (DEPTH, 1, 2, 2 * D_FF)),
         ("new_k_sample", (DEPTH, 1, DEC, DIFF_HEADS, HW)), ("new_v_sample", (DEPTH, 1, DEC, DIFF_HEADS, HW)),
         ("state_ret_sample", (DEPTH, 1, RET_HEADS, RET_DK, RET_DV)), ("state_conv_sample", (DEPTH, 1, 2, 2 * D_FF))]


def lay_out(inputs):
    arrays = {n: np.ascontiguousarray(inputs[n]) for n in _INS}

    def columns(a):
        return a.reshape(DEPTH, -1, P).transpose(2, 0, 1)

    def copies(*names):
        a = np.concatenate([inputs[n] for n in names], axis=1)
        return np.broadcast_to(a[None], (P,) + a.shape)

    conv = [inputs["state_conv"][:, 0, 0], inputs["state_conv"][:, 0, 1], inputs["conv_w"][:, 0], inputs["conv_w"][:, 1],
            inputs["conv_w"][:, 2], inputs["conv_b"]]
    vectors = [inputs[n] for n in ("norm1_g", "norm2_g", "ret_norm_g", "diff_norm_g")]
    arrays["params"] = np.ascontiguousarray(
        np.concatenate([columns(a) for a in vectors + conv] + [copies("q_norm_g", "k_norm_g")], axis=2))
    arrays["lambdas"] = np.ascontiguousarray(copies("lambda_q1", "lambda_q2", "lambda_k1", "lambda_k2"))
    arrays["tab_small"], arrays["tab_decay"] = shape_tables()
    return arrays


def kernel(**inputs):
    import concourse.bacc as _bacc
    from concourse.bass_utils import run_bass_kernel_spmd

    arrays = lay_out(inputs)
    counts = None
    for _ in range(2):
        nc = _bacc.Bacc("TRN2", target_bir_lowering=False, num_devices=1)
        tensors = {n: nc.dram_tensor(f"in_{n}_dram", a.shape, F32, kind="ExternalInput").ap() for n, a in arrays.items()}
        for n, s in _OUTS:
            tensors[n] = nc.dram_tensor(f"out_{n}_dram", s, F32, kind="ExternalOutput").ap()
        counts = program(nc, tensors, counts)
    r = run_bass_kernel_spmd(nc, [{f"in_{n}_dram": a for n, a in arrays.items()}], core_ids=[0])
    return tuple(r.results[0][f"out_{n}_dram"] for n, _ in _OUTS)
```
